# Optimizing a Trainium2 kernel written in Bass

```python
import math
import jax, jax.numpy as jnp
from jax import lax
import numpy as np

D_MODEL = 1024
BATCH = 1
SEQ = 256
DEPTH = 2

N_EVEN = (DEPTH + 1) // 2
N_ODD = DEPTH // 2
EPS = 1e-6

ATTN_WIDTH = D_MODEL // 2
CONV_WIDTH = D_MODEL // 2
DA_HEADS = 4
DA_HEAD_DIM = ATTN_WIDTH // (2 * DA_HEADS)
DA_V_DIM = 2 * DA_HEAD_DIM
Q_BLOCK = 128
CONV_KERNEL = 31
CONV_GROUPS = 8
AB_IN_WIDTH = 3 * ATTN_WIDTH + 2 * CONV_WIDTH

HGRN_HEADS = 8
HGRN_KDIM = D_MODEL // HGRN_HEADS
HGRN_VDIM = D_MODEL // HGRN_HEADS
HGRN_CHUNK = 32
HGRN_IN_WIDTH = 4 * D_MODEL

FFN_DENSE = 2816
N_EXPERTS = 8
TOP_K = 2
FFN_EXPERT = 3584

kernel_name = 'hybrid_diffattn_conformer_hgrn2_moe'

def rms_norm(x, gain):
    xf = x.astype(jnp.float32)
    y = xf * lax.rsqrt(jnp.mean(xf * xf, axis=-1, keepdims=True) + EPS)
    return (y * gain.astype(jnp.float32)).astype(x.dtype)

def swiglu(h, w_in, w_out):
    gate, up = jnp.split(h @ w_in, 2, axis=-1)
    return (jax.nn.silu(gate) * up) @ w_out

def diff_attention(q, k, v, q_gain, k_gain, lam_vecs, subln_gain, lam_init):
    b, s, _ = q.shape
    q = rms_norm(q.reshape(b, s, DA_HEADS, 2, DA_HEAD_DIM), q_gain).transpose(0, 2, 3, 1, 4)
    k = rms_norm(k.reshape(b, s, DA_HEADS, 2, DA_HEAD_DIM), k_gain).transpose(0, 2, 3, 1, 4)
    v = v.reshape(b, s, DA_HEADS, DA_V_DIM).transpose(0, 2, 1, 3)
    lv = lam_vecs.astype(jnp.float32)
    lam = jnp.exp(jnp.sum(lv[0] * lv[1])) - jnp.exp(jnp.sum(lv[2] * lv[3])) + lam_init
    scale = DA_HEAD_DIM ** -0.5
    outs = []
    for blk in range(s // Q_BLOCK):
        q0 = blk * Q_BLOCK
        q1 = q0 + Q_BLOCK
        scores = jnp.einsum('bhcqd,bhckd->bhcqk', q[:, :, :, q0:q1], k[:, :, :, :q1],
                            preferred_element_type=jnp.float32) * scale
        causal = (q0 + jnp.arange(Q_BLOCK))[:, None] >= jnp.arange(q1)[None, :]
        probs = jax.nn.softmax(jnp.where(causal, scores, -jnp.inf), axis=-1)
        weights = probs[:, :, 0] - lam * probs[:, :, 1]
        outs.append(jnp.einsum('bhqk,bhkv->bhqv', weights.astype(v.dtype), v[:, :, :q1]))
    o = rms_norm(jnp.concatenate(outs, axis=2), subln_gain) * (1.0 - lam_init)
    return o.transpose(0, 2, 1, 3).reshape(b, s, ATTN_WIDTH)

def conformer_conv(u, dw, dw_bias, gn_gain, gn_bias):
    b, s, _ = u.shape
    val, gate = jnp.split(u, 2, axis=-1)
    g = val * jax.nn.sigmoid(gate)
    y = lax.conv_general_dilated(g, dw[:, None, :].astype(g.dtype), window_strides=(1,),
                                 padding=[(CONV_KERNEL - 1, 0)],
                                 dimension_numbers=('NWC', 'WIO', 'NWC'),
                                 feature_group_count=CONV_WIDTH) + dw_bias
    yf = y.astype(jnp.float32).reshape(b, s, CONV_GROUPS, CONV_WIDTH // CONV_GROUPS)
    mean = jnp.mean(yf, axis=-1, keepdims=True)
    var = jnp.mean(jnp.square(yf - mean), axis=-1, keepdims=True)
    yn = ((yf - mean) * lax.rsqrt(var + EPS)).reshape(b, s, CONV_WIDTH) * gn_gain + gn_bias
    return jax.nn.silu(yn).astype(u.dtype)

def hgrn2(z, lower_bound, norm_gain):
    b, s, _ = z.shape
    q, f, i, g = jnp.split(z, 4, axis=-1)
    log_f = jnp.logaddexp(jnp.log(lower_bound),
                          jnp.log1p(-lower_bound) + jax.nn.log_sigmoid(f.astype(jnp.float32)))
    k = -jnp.expm1(log_f)
    n = s // HGRN_CHUNK

    def to_chunks(t, d):
        return t.astype(jnp.float32).reshape(b, n, HGRN_CHUNK, HGRN_HEADS, d).transpose(1, 0, 3, 2, 4)

    qc = to_chunks(jax.nn.silu(q), HGRN_KDIM)
    kc = to_chunks(k, HGRN_KDIM)
    vc = to_chunks(i, HGRN_VDIM)
    gc = to_chunks(log_f, HGRN_KDIM)
    causal = jnp.tril(jnp.ones((HGRN_CHUNK, HGRN_CHUNK), dtype=bool))

    def step(state, inp):
        qb, kb, vb, gb = inp
        cum = jnp.cumsum(gb, axis=2)
        last = cum[:, :, -1:, :]
        inter = jnp.einsum('bhtk,bhkv->bhtv', qb * jnp.exp(cum), state)
        rel = cum[:, :, :, None, :] - cum[:, :, None, :, :]
        decay = jnp.exp(jnp.where(causal[:, :, None], rel, -jnp.inf))
        scores = jnp.einsum('bhtk,bhsk,bhtsk->bhts', qb, kb, decay)
        out = inter + jnp.einsum('bhts,bhsv->bhtv', scores, vb)
        state = jnp.exp(last[:, :, 0, :])[..., None] * state + \
            jnp.einsum('bhsk,bhsv->bhkv', kb * jnp.exp(last - cum), vb)
        return state, out

    s0 = jnp.zeros((b, HGRN_HEADS, HGRN_KDIM, HGRN_VDIM), jnp.float32)
    _, o = lax.scan(step, s0, (qc, kc, vc, gc))
    o = o.transpose(1, 0, 3, 2, 4).reshape(b, s, HGRN_HEADS, HGRN_VDIM)
    o = rms_norm(o, norm_gain.reshape(HGRN_HEADS, HGRN_VDIM)).reshape(b, s, D_MODEL)
    return (o * jax.nn.silu(g.astype(jnp.float32))).astype(z.dtype)

def moe_swiglu(h, router, w_in, w_out):
    b, s, d = h.shape
    t = h.reshape(b * s, d)
    logits = (t @ router).astype(jnp.float32)
    top_vals, top_idx = lax.top_k(logits, TOP_K)
    gates = jax.nn.softmax(top_vals, axis=-1)
    combine = jnp.sum(jax.nn.one_hot(top_idx, N_EXPERTS, dtype=jnp.float32) * gates[..., None], axis=1)
    y = jnp.zeros_like(t)
    for e in range(N_EXPERTS):
        y = y + combine[:, e:e + 1].astype(t.dtype) * swiglu(t, w_in[e], w_out[e])
    return y.reshape(b, s, d)

def setup_inputs(seed: int = 0) -> dict:
    key = jax.random.key(seed)
    ks = jax.random.split(key, 22)

    def normal(k, shape, scale):
        return jax.random.normal(k, shape, jnp.float32) * scale

    def gain(k, shape):
        return 1.0 + normal(k, shape, 0.02)

    return {
        'x': normal(ks[0], (BATCH, SEQ, D_MODEL), 1.0),
        'mix_norm': gain(ks[1], (DEPTH, D_MODEL)),
        'ffn_norm': gain(ks[2], (DEPTH, D_MODEL)),
        'ab_w_in': normal(ks[3], (N_EVEN, D_MODEL, AB_IN_WIDTH), D_MODEL ** -0.5),
        'ab_w_out': normal(ks[4], (N_EVEN, ATTN_WIDTH + CONV_WIDTH, D_MODEL), (ATTN_WIDTH + CONV_WIDTH) ** -0.5),
        'da_q_gain': gain(ks[5], (N_EVEN, DA_HEAD_DIM)),
        'da_k_gain': gain(ks[6], (N_EVEN, DA_HEAD_DIM)),
        'da_lambda': normal(ks[7], (N_EVEN, 4, DA_HEAD_DIM), 0.1),
        'da_subln': gain(ks[8], (N_EVEN, DA_V_DIM)),
        'conv_dw': normal(ks[9], (N_EVEN, CONV_KERNEL, CONV_WIDTH), CONV_KERNEL ** -0.5),
        'conv_dw_bias': normal(ks[10], (N_EVEN, CONV_WIDTH), 0.01),
        'conv_gn_gain': gain(ks[11], (N_EVEN, CONV_WIDTH)),
        'conv_gn_bias': normal(ks[12], (N_EVEN, CONV_WIDTH), 0.01),
        'hgrn_w_in': normal(ks[13], (N_ODD, D_MODEL, HGRN_IN_WIDTH), D_MODEL ** -0.5),
        'hgrn_lb_logits': normal(ks[14], (N_ODD, HGRN_HEADS * HGRN_KDIM), 0.5),
        'hgrn_norm': gain(ks[15], (N_ODD, D_MODEL)),
        'hgrn_w_out': normal(ks[16], (N_ODD, D_MODEL, D_MODEL), D_MODEL ** -0.5),
        'ffn_w_in': normal(ks[17], (N_EVEN, D_MODEL, 2 * FFN_DENSE), D_MODEL ** -0.5),
        'ffn_w_out': normal(ks[18], (N_EVEN, FFN_DENSE, D_MODEL), FFN_DENSE ** -0.5),
        'moe_router': normal(ks[19], (N_ODD, D_MODEL, N_EXPERTS), D_MODEL ** -0.5),
        'moe_w_in': normal(ks[20], (N_ODD, N_EXPERTS, D_MODEL, 2 * FFN_EXPERT), D_MODEL ** -0.5),
        'moe_w_out': normal(ks[21], (N_ODD, N_EXPERTS, FFN_EXPERT, D_MODEL), FFN_EXPERT ** -0.5),
    }

def reference(x, mix_norm, ffn_norm, ab_w_in, ab_w_out, da_q_gain, da_k_gain, da_lambda, da_subln,
              conv_dw, conv_dw_bias, conv_gn_gain, conv_gn_bias, hgrn_w_in, hgrn_lb_logits, hgrn_norm,
              hgrn_w_out, ffn_w_in, ffn_w_out, moe_router, moe_w_in, moe_w_out):
    lb_all = jnp.cumsum(jax.nn.softmax(hgrn_lb_logits.astype(jnp.float32), axis=0), axis=0)
    lb_all = lb_all - lb_all[0:1]
    for layer in range(DEPTH):
        j = layer // 2
        h = rms_norm(x, mix_norm[layer])
        if layer % 2 == 0:
            z = h @ ab_w_in[j]
            q, k, v, u = jnp.split(z, [ATTN_WIDTH, 2 * ATTN_WIDTH, 3 * ATTN_WIDTH], axis=-1)
            lam_init = 0.8 - 0.6 * math.exp(-0.3 * layer)
            a = diff_attention(q, k, v, da_q_gain[j], da_k_gain[j], da_lambda[j], da_subln[j], lam_init)
            c = conformer_conv(u, conv_dw[j], conv_dw_bias[j], conv_gn_gain[j], conv_gn_bias[j])
            x = x + jnp.concatenate([a, c], axis=-1) @ ab_w_out[j]
            h = rms_norm(x, ffn_norm[layer])
            x = x + swiglu(h, ffn_w_in[j], ffn_w_out[j])
        else:
            o = hgrn2(h @ hgrn_w_in[j], lb_all[j], hgrn_norm[j])
            x = x + o @ hgrn_w_out[j]
            h = rms_norm(x, ffn_norm[layer])
            x = x + moe_swiglu(h, moe_router[j], moe_w_in[j], moe_w_out[j])
    return x


_drawn_inputs = setup_inputs


def setup_inputs(seed=0):
    import zlib

    import numpy as np

    out = dict(_drawn_inputs(seed))
    spreads = {}
    factors = {'da_k_gain': 9.224,
     'conv_dw_bias': 3.763,
     'conv_gn_gain': 13.393,
     'conv_gn_bias': 26.574,
     'hgrn_norm': 28.762,
     'da_subln': 6.353,
     'ffn_norm': 6.685}
    for name, (base, spread) in spreads.items():
        noise = np.random.default_rng([zlib.crc32(name.encode()), seed]).standard_normal(out[name].shape)
        drawn = base * np.exp(spread * noise) if base else spread * noise
        out[name] = __import__('jax').numpy.asarray(drawn.astype(out[name].dtype))
    for name, factor in factors.items():
        out[name] = (out[name] * factor).astype(out[name].dtype)
    return out
```

```python
import math
from contextlib import ExitStack

import concourse.bass as bass
from concourse import mybir

ALU = mybir.AluOpType
ACT = mybir.ActivationFunctionType
AX = mybir.AxisListType
F32 = mybir.dt.float32
F32R = mybir.dt.float32r
BF16 = mybir.dt.bfloat16
I8 = mybir.dt.int8
I32 = mybir.dt.int32

P = 128
T = 256
TT = T // P
D = 1024
KC = D // P
UC = 256
UNIT = KC * UC
OC = UNIT // D
R = 6
S = 3
POOL_FROM, POOL_TO = 3, 13
EPS = 1e-6
HEADS = 4
HD = 64
TAPS = 31
HH = 8
NE = 8
CAP = 128
LAM_INIT = 0.8 - 0.6 * math.exp(-0.3 * 0)
NEG = -1.0e30

U_AB_IN, N_AB_IN = 0, 10
U_AB_OUT, N_OUT = 10, 4
U_FFN = 14
FFN_STEPS = 11
U_HG_IN, N_HG_IN = U_FFN + 3 * FFN_STEPS, 16
U_HG_OUT = U_HG_IN + N_HG_IN
U_MOE = U_HG_OUT + N_OUT
MOE_STEPS = 14
MOE_UNITS = 3 * MOE_STEPS
AB_ORDER = [1536, 2048, 1792, 2304, 0, 256, 512, 768, 1024, 1280]
HG_ORDER = [1024 + 256 * i for i in range(4)] + [256 * i for i in range(4)] \
    + [3072 + 256 * i for i in range(4)] + [2048 + 256 * i for i in range(4)]

C_MIX, C_FFN, C_HN, C_LB, C_DWB, C_GG, C_GB, C_SUB, C_QG, C_KG = 0, 16, 32, 40, 48, 52, 56, 60, 61, 62
N_PAR = 63
LEVELS = [1, 2, 4, 8, 16, 32, 64]
PAIRS = 4
GROUPS = PAIRS * (HH // 2) * TT


def build(nc, A, out):
    with ExitStack() as ctx:
        def sb(name, shape, dt=F32):
            return ctx.enter_context(nc.sbuf_tensor(name, shape, dt))

        def sem(name):
            return ctx.enter_context(nc.semaphore(name))

        bank = ctx.enter_context(nc.psum_tensor("bank", [P, 8, 512], F32))

        raw = sb("raw", [P, R, UNIT])
        w_h = sb("w_h", [P, S, UNIT], F32R)
        w_l = sb("w_l", [P, S, UNIT], F32R)
        x = sb("x", [P, TT, D])
        xn = sb("xn", [P, TT, D])
        h_h = sb("h_h", [P, KC, T], F32R)
        h_l = sb("h_l", [P, KC, T], F32R)
        ident = sb("ident", [P, P])
        ones = sb("ones", [P, P])
        mean_all = sb("mean_all", [P, P])
        mean_64 = sb("mean_64", [P, P])
        before = sb("before", [P, P])
        slot_no = sb("slot_no", [P, 2, P])
        expert_no = sb("expert_no", [P, NE])
        par = sb("par", [P, P])
        dw = sb("dw", [P, P])
        eps = sb("eps", [P, 1])
        n_stat = sb("n_stat", [P, 4, 3, TT])
        router = sb("router", [P, KC, NE])
        router_h = sb("router_h", [P, KC, NE], F32R)
        router_l = sb("router_l", [P, KC, NE], F32R)
        flag = sb("flag", [P, 1], I32)
        span = sb("span", [P, 5, 2, P], F32R)
        lmask = sb("lmask", [P, 7, P], I8)

        def phase(items):
            made = []
            with ExitStack() as inner:
                for n, shape, dt in items:
                    made.append(inner.enter_context(nc.sbuf_tensor(n, shape, dt)))
            return made

        (par_rows, dw_rows, lam_rows, lam_prod, lam, ident_b, mask_b, conv_in, conv_y, sig, q_raw, sq, rs, q_t, k_t, v_n,
         p_0, p_1, w_t, smx, nmx, ssum, rsum) = phase([
            ("par_rows", [P, P], F32), ("dw_rows", [P, P], F32), ("lam_rows", [P, 4, HD], F32), ("lam_prod", [P, 2, HD], F32),
            ("lam", [P, 8], F32), ("ident_b", [P, P], BF16), ("mask_b", [P, P], BF16),
            ("conv_in", [P, 4, TAPS - 1 + T], F32), ("conv_y", [P, 4, T], F32),
            ("sig", [P, 512], F32), ("q_raw", [P, 2, 512], F32), ("sq", [P, 2, 512], F32), ("rs", [P, 2, 512], F32),
            ("q_t", [P, HEADS, T], F32), ("k_t", [P, HEADS, T], F32), ("v_n", [P, TT, 512], F32),
            ("p_0", [P, 2, HEADS, P], F32), ("p_1", [P, 2, HEADS, T], F32), ("w_t", [P, HEADS, 384], F32),
            ("smx", [P, 16], F32), ("nmx", [P, 16], F32), ("ssum", [P, 16], F32), ("rsum", [P, 16], F32)])
        silu_g, act_f, act_h, act_l = phase([
            ("silu_g", [P, 512], F32), ("act_f", [P, 512], F32),
            ("act_h", [P, 2, 512], F32R), ("act_l", [P, 2, 512], F32R)])
        key_t, qry_t, val_n, lf_h, lf_l, att, dq, dk, decay, lb = phase([
            ("key_t", [P, HH, T], F32), ("qry_t", [P, HH, T], F32), ("val_n", [P, TT, D], F32),
            ("lf_h", [P, TT, D], F32R), ("lf_l", [P, TT, D], F32R), ("att", [P, HH, 3, P], F32),
            ("dq", [P, 2, 512], F32), ("dk", [P, 2, 512], F32), ("decay", [P, 2, 512], F32), ("lb", [P, 5, HH], F32)])
        (gain_row, logit, pick, rank, comb, rank_e, comb_e, sel, scat, comb_s, hs_h, hs_l, m_silu, m_act, ma_h, ma_l,
         y_f, y_h, y_l) = phase([
            ("gain_row", [P, D], F32), ("logit", [P, 12, 2, NE], F32), ("pick", [P, 12, 2], F32),
            ("rank", [P, NE + 1, 2], F32), ("comb", [P, NE + 1, 2], F32),
            ("rank_e", [P, 2], F32), ("comb_e", [P, 2], F32), ("sel", [P, 2, P], F32), ("scat", [P, T], F32R), ("comb_s", [P, 1], F32),
            ("hs_h", [P, KC, P], F32R), ("hs_l", [P, KC, P], F32R), ("m_silu", [P, UC], F32), ("m_act", [P, UC], F32),
            ("ma_h", [P, UC], F32R), ("ma_l", [P, UC], F32R), ("y_f", [P, D], F32), ("y_h", [P, D], F32R), ("y_l", [P, D], F32R)])
        gate_t = xn[:].rearrange("p a (b t) -> p (a b) t", t=T)
        log_f = att[:, :, 0:2, :].rearrange("p h a t -> p h (a t)")

        w_in = [sem(f"w_in{i}") for i in range(R)]
        w_high, w_used = sem("w_high"), sem("w_used")
        w_low, w_low_pool = sem("w_low"), sem("w_low_pool")
        x_in, par_in, lam_in, rout_in, gain_in = sem("x_in"), sem("par_in"), sem("lam_in"), sem("rout_in"), sem("gain_in")
        par_z, par_t, par_cp = sem("par_z"), sem("par_t"), sem("par_cp")
        const, dve_const = sem("const"), sem("dve_const")
        n_sq, n_ln, n_rs, n_xn, n_t, n_high, n_low = (sem(f"n_{k}") for k in "sq ln rs xn t high low".split())
        x_add = sem("x_add")
        lam_d, lam_e, sub_g, lb_d = sem("lam_d"), sem("lam_e"), sem("sub_g"), sem("lb_d")
        c_s, c_g, c_y = sem("c_s"), sem("c_g"), sem("c_y")
        qk_raw, qk_sq, qk_ms, qk_ln, qk_rs, q_n, v_cp = (sem(k) for k in "qk_raw qk_sq qk_ms qk_ln qk_rs q_n v_cp".split())
        s_sc, s_mx, s_nm, s_ex, s_rc, s_w = (sem(k) for k in "s_sc s_mx s_nm s_ex s_rc s_w".split())
        a_t, a_wt, a_o, a_sq, a_ms, a_ln, a_rs, a_of, a_h, a_l = (sem(f"a_{k}") for k in "t wt o sq ms ln rs of h l".split())
        g_m, g_c, g_sq, g_v, g_ln, g_rs, g_n, g_s, g_h, g_l = (sem(f"g_{k}") for k in "m c sq v ln rs n s h l".split())
        f_silu, f_mul, f_high, f_low = (sem(f"f_{k}") for k in "silu mul high low".split())
        hg_ev, hg_d, hg_ln, hg_t, hg_h, hg_l, hg_gg, hg_z = (sem(f"hg_{k}") for k in "ev d ln t h l gg z".split())
        hd, hd_cp, sp_d, sp_e, sp_m, sp_s, sp_c0, sp_c1 = (sem(k) for k in "hd hd_cp sp_d sp_e sp_m sp_s sp_c0 sp_c1".split())
        o_o, o_sq, o_ms, o_ln, o_rs, o_n, o_g, o_h, o_l = (sem(f"o_{k}") for k in "o sq ms ln rs n g h l".split())
        r_high, r_low, r_lg, r_d, r_e, r_rank, r_flag, h3 = (sem(k) for k in "r_high r_low r_lg r_d r_e r_rank r_flag h3".split())
        m_re, m_sel, m_gat, m_pt, m_scat, m_comb, m_hh, m_hl = (sem(f"m_{k}") for k in "re sel gat pt scat comb hh hl".split())
        m_si, m_mul, m_t, m_ah, m_al, m_y, m_yh, m_yl, m_sc, m_add = (sem(f"m_{k}") for k in "si mul t ah al y yh yl sc add".split())
        stored = sem("stored")
        n_const = {}

        def in_cols(w):
            return w.rearrange("(c p) f -> p c f", p=P)

        def out_rows(w):
            return w.rearrange("(s c p) d -> s p c d", p=P, c=OC)

        ab_in, ab_out = in_cols(A["ab_w_in"][0]), out_rows(A["ab_w_out"][0])
        ffn_in, ffn_out = in_cols(A["ffn_w_in"][0]), out_rows(A["ffn_w_out"][0])
        hg_in, hg_out = in_cols(A["hgrn_w_in"][0]), out_rows(A["hgrn_w_out"][0])
        FFN_UP = FFN_STEPS * UC
        MOE_UP = MOE_STEPS * UC

        def as_in(t, slot):
            return t[:, slot, :].rearrange("p (c f) -> p c f", c=KC)

        def as_out(t, slot):
            return t[:, slot, :].rearrange("p (c d) -> p c d", c=OC)

        def second(g):
            return g + 1 - len([n for n in range(g + 1) if n >= GROUPS - 8 and n % 2 == 0])

        def wait_split(eng, u0, rounds=0):
            if POOL_FROM <= u0 < POOL_TO:
                eng.wait_ge(w_low_pool, u0 - POOL_FROM + 1)
            elif u0 < POOL_FROM:
                eng.wait_ge(w_low, u0 + 1)
            else:
                eng.wait_ge(w_low, u0 + 1 - (POOL_TO - POOL_FROM) + R * rounds)

        def load(sp, u0, view, src, rounds=0):
            if u0 >= R:
                wait_split(sp, u0 - R, rounds)
            sp.dma_start(view(raw, u0 % R), src).then_inc(w_in[u0 % R], 16)

        def split_high(act, u0, rounds=0):
            act.wait_ge(w_in[u0 % R], 16 * (u0 // R + 1) + 16 * rounds)
            if u0 >= S:
                act.wait_ge(w_used, u0 - S + 1 + R * rounds)
            act.activation(w_h[:, u0 % S, :], raw[:, u0 % R, :], ACT.Copy).then_inc(w_high, 1)

        def split_low(eng, u0, rounds=0):
            eng.wait_ge(w_high, u0 + 1 + R * rounds)
            eng.tensor_tensor(w_l[:, u0 % S, :], raw[:, u0 % R, :], w_h[:, u0 % S, :],
                              ALU.subtract).then_inc(w_low_pool if POOL_FROM <= u0 < POOL_TO else w_low, 1)

        block = ctx.enter_context(nc.Block())

        @block.gpsimd
        def _(pool):
            made = [0]

            def step(ins):
                made[0] += 1
                ins.then_inc(const, 1)
                pool.wait_ge(const, made[0])

            def select(view, pattern, base, cm, op=ALU.is_ge, fill=0.0):
                step(pool.affine_select(out=view, in_=view, compare_op=op, fill=fill, base=base, pattern=pattern,
                                        channel_multiplier=cm))

            step(pool.memset(ident[:], 0.0))
            select(ident[:], [[-1, P]], 0, 1, ALU.not_equal, 1.0)
            step(pool.memset(par_rows[:], 0.0))
            step(pool.memset(dw_rows[:], 0.0))
            n_const["rows"] = made[0]
            step(pool.memset(ones[:], 1.0))
            step(pool.memset(mean_all[:], 1.0 / P))
            step(pool.memset(mean_64[:], 1.0 / HD))
            select(mean_64[:, 0:HD], [[0, HD]], HD - 1, -1)
            select(mean_64[:, HD:P], [[0, HD]], -HD, 1)
            step(pool.memset(ident_b[:], 0.0))
            select(ident_b[:], [[-1, P]], 0, 1, ALU.not_equal, 1.0)
            step(pool.memset(mask_b[:], 0.0))
            select(mask_b[:], [[-1, P]], 0, 1, ALU.is_ge, NEG)
            step(pool.memset(conv_in[:, :, 0:TAPS - 1], 0.0))
            step(pool.memset(before[:], 1.0))
            select(before[:], [[1, P]], -1, -1)
            for r in range(2):
                step(pool.iota(slot_no[:, r, :], pattern=[[1, P]], base=CAP * r, channel_multiplier=0,
                               allow_small_or_imprecise_dtypes=True))
                if CAP < P:
                    step(pool.memset(slot_no[:, r, CAP:P], -5.0))
            step(pool.iota(expert_no[:], pattern=[[-1, NE]], base=NE, channel_multiplier=0,
                           allow_small_or_imprecise_dtypes=True))
            n_const["early"] = made[0]
            for u in range(POOL_FROM, POOL_TO):
                split_low(pool, u)
            step(pool.memset(span[:].bitcast(F32), 1.0))
            step(pool.memset(lmask[:], 0))
            for n, h in enumerate(LEVELS):
                nb = P // (2 * h)
                for view in ([span[:, n // 2, n % 2, :]] if n < 6 else [span[:, 3, 0, :], span[:, 4, 0, :]]):
                    v = view.rearrange("p (b s r) -> p b s r", s=2, r=h)
                    select(v[:, :, 1, :], [[-2 * h, nb], [0, h]], -h, 1)
                    select(v[:, :, 1, :], [[2 * h, nb], [1, h]], h, -1)
                    select(v[:, :, 0, :], [[-2 * h, nb], [-1, h]], -1, 1)
                    select(v[:, :, 0, :], [[2 * h, nb], [0, h]], h - 1, -1)
                v = lmask[:, n, :].rearrange("p (b s r) -> p b s r", s=2, r=h)
                step(pool.memset(v[:, :, 1, :], 1))
                select(v[:, :, 1, :], [[-2 * h, nb], [0, h]], 0, 1)
                select(v[:, :, 1, :], [[2 * h, nb], [0, h]], h - 1, -1)
            select(span[:, 3, 1, :], [[-1, P]], -1, 1)
            select(span[:, 4, 1, :], [[1, P]], 0, -1)
            n_const["all"] = made[0]

            pool.wait_ge(hg_ev, 16)
            for h in range(HH):
                pool.tensor_scalar(gate_t[:, h, :], gate_t[:, h, :], par[:, C_HN + h:C_HN + h + 1], None,
                                   ALU.mult).then_inc(hg_gg, 1)
            pool.wait_ge(gain_in, 16)
            pool.wait_ge(n_t, 16)
            for tt in range(TT):
                pool.tensor_tensor(xn[:, tt, :], xn[:, tt, :], gain_row[:], ALU.mult).then_inc(h3, 1)

        @block.sync
        def _(sp):
            for tt in range(TT):
                sp.dma_start(x[:, tt, :], A["x"][0, tt * P:(tt + 1) * P, :]).then_inc(x_in, 16)
            for i in range(N_AB_IN):
                load(sp, U_AB_IN + i, as_in, ab_in[:, :, AB_ORDER[i]:AB_ORDER[i] + UC])
            for i in range(N_OUT):
                load(sp, U_AB_OUT + i, as_out, ab_out[i])

            def ffn_ab(u0, step, rounds=0):
                load(sp, u0, as_in, ffn_in[:, :, bass.ds(step * UC, UC)], rounds)
                load(sp, u0 + 1, as_in, ffn_in[:, :, bass.ds(step * UC + FFN_UP, UC)], rounds)

            ffn_ab(U_FFN, 0)
            ffn_ab(U_FFN + 2, 1)
            load(sp, U_FFN + 4, as_out, ffn_out[0])
            with sp.Fori(0, 4) as j:
                for k in (0, 1):
                    u0 = U_FFN + 5 + 3 * k
                    ffn_ab(u0, j * 2 + (2 + k), j)
                    load(sp, u0 + 2, as_out, ffn_out[j * 2 + (1 + k)], j)
            ffn_ab(U_FFN + 29, 10)
            load(sp, U_FFN + 31, as_out, ffn_out[9])
            load(sp, U_FFN + 32, as_out, ffn_out[10])
            for i in range(N_HG_IN):
                load(sp, U_HG_IN + i, as_in, hg_in[:, :, HG_ORDER[i]:HG_ORDER[i] + UC])
            for i in range(N_OUT):
                load(sp, U_HG_OUT + i, as_out, hg_out[i])

            w1, w2 = A["moe_w_in"][0], A["moe_w_out"][0]

            def moe_a(u0, e, step, rounds):
                load(sp, u0, as_in, in_cols(w1[e])[:, :, bass.ds(step * UC, UC)], rounds)

            def moe_b(u0, e, step, rounds):
                load(sp, u0, as_in, in_cols(w1[e])[:, :, bass.ds(step * UC + MOE_UP, UC)], rounds)

            def moe_c(u0, e, step, rounds):
                load(sp, u0, as_out, out_rows(w2[e])[step], rounds)

            def expert(u, e, nxt, rounds):
                moe_b(u + 3, e, 1, rounds)
                moe_c(u + 4, e, 0, rounds)
                with sp.Fori(0, 6) as j:
                    for k in (0, 1):
                        moe_a(u + 5 + 3 * k, e, j * 2 + (2 + k), rounds + j)
                        moe_b(u + 6 + 3 * k, e, j * 2 + (2 + k), rounds + j)
                        moe_c(u + 7 + 3 * k, e, j * 2 + (1 + k), rounds + j)
                moe_c(u + 41, e, 13, rounds)
                moe_a(u + 42, nxt, 0, rounds)
                moe_b(u + 43, nxt, 0, rounds)
                moe_a(u + 44, nxt, 1, rounds)

            def moe_round(r):
                u = U_MOE + r * NE * MOE_UNITS
                with sp.Fori(0, NE - 1) as e:
                    expert(u, e, e + 1, e * 7)
                expert(u, NE - 1, 0, 7 * (NE - 1))

            moe_a(U_MOE, 0, 0, 0)
            moe_b(U_MOE + 1, 0, 0, 0)
            moe_a(U_MOE + 2, 0, 1, 0)
            moe_round(0)
            sp.wait_ge(r_flag, 1)
            over = sp.value_load(flag[0:1, 0:1], min_val=0, max_val=1)
            with sp.If(over > 0):
                moe_round(1)
                sp.wait_ge(m_add, 8 * NE + 1)
            sp.wait_ge(m_add, 4 * NE + 1)
            for tt in range(TT):
                sp.dma_start(out[0, tt * P:(tt + 1) * P, :], x[:, tt, :]).then_inc(stored, 16)
            sp.wait_ge(stored, 16 * TT)

        @block.vector
        def _(dve):
            dve.memset(eps[:], EPS).then_inc(dve_const, 1)
            dve.wait_ge(par_t, 1)
            dve.tensor_copy(par[:], bank[:, 0, 0:P]).then_inc(par_cp, 1)
            dve.wait_ge(par_t, 2)
            dve.tensor_copy(dw[:], bank[:, 1, 0:P]).then_inc(par_cp, 1)
            dve.wait_ge(par_cp, 2)
            dve.tensor_scalar(par[:, C_SUB:C_SUB + 1], par[:, C_SUB:C_SUB + 1], 1.0 - LAM_INIT, None, ALU.mult).then_inc(sub_g, 1)
            dve.wait_ge(lam_in, 16)
            for i in range(2):
                dve.tensor_tensor(lam_prod[:, i, :], lam_rows[:, 2 * i, :], lam_rows[:, 2 * i + 1, :], ALU.mult).then_inc(lam_d, 1)
            dve.wait_ge(lam_d, 2)
            dve.tensor_reduce(lam[:, 0:2], lam_prod[:], AX.X, ALU.add).then_inc(lam_d, 1)

            def norm_scale(n):
                dve.wait_ge(n_rs, n + 1)
                for tt in range(TT):
                    dve.tensor_scalar(xn[:, tt, :], x[:, tt, :], n_stat[:, n, 2, tt:tt + 1], None, ALU.mult).then_inc(n_xn, 1)

            def norm_low(n, col):
                for j in range(4):
                    dve.wait_ge(n_high, 8 * n + 2 * j + 2)
                    b = (2 + j) if n == 0 else j
                    for c in range(2):
                        dve.scalar_tensor_tensor(out=h_l[:, 2 * j + c, :], in0=bank[:, b, c * T:(c + 1) * T],
                                                 scalar=par[:, col + 2 * j + c:col + 2 * j + c + 1], in1=h_h[:, 2 * j + c, :],
                                                 op0=ALU.mult, op1=ALU.subtract).then_inc(n_low, 1)

            def residual(units):
                dve.wait_ge(w_used, units)
                for tt in range(TT):
                    for half in range(2):
                        v = x[:, tt, half * 512:(half + 1) * 512]
                        dve.tensor_tensor(v, bank[:, 4 + 2 * tt + half, :], v, ALU.add).then_inc(x_add, 1)

            norm_scale(0)
            split_low(dve, 0)
            norm_low(0, C_MIX)
            split_low(dve, 1)
            split_low(dve, 2)
            def conv_value(i):
                dve.wait_ge(c_s, i + 1)
                dve.tensor_tensor(conv_in[:, 2 * i:2 * i + 2, TAPS - 1:], bank[:, 0, :].rearrange("p (a t) -> p a t", a=2),
                                  sig[:].rearrange("p (a t) -> p a t", a=2), ALU.mult).then_inc(c_g, 1)

            def conv_taps(i, first, end):
                if first == 0:
                    dve.wait_ge(c_g, i + 1)
                    for c in (2 * i, 2 * i + 1):
                        dve.tensor_scalar(conv_y[:, c, :], conv_in[:, c, 0:T], dw[:, c:c + 1], par[:, C_DWB + c:C_DWB + c + 1],
                                          ALU.mult, ALU.add).then_inc(c_y, 1)
                    first = 1
                with dve.Fori(first, end) as k:
                    for c in (0, 1):
                        ch = 2 * i + c
                        dve.wait_ge(c_y, k * 2 + (2 * TAPS * i + c - 1))
                        dve.scalar_tensor_tensor(out=conv_y[:, ch, :], in0=conv_in[:, ch, bass.ds(k, T)],
                                                 scalar=dw[:, bass.ds(k * 4 + ch, 1)], in1=conv_y[:, ch, :],
                                                 op0=ALU.mult, op1=ALU.add).then_inc(c_y, 1)

            def qk_norm(i):
                dst, col = (q_t, C_QG) if i < 2 else (k_t, C_KG)
                dve.wait_ge(qk_rs, i + 1)
                dve.scalar_tensor_tensor(out=dst[:, 2 * (i % 2):2 * (i % 2) + 2, :],
                                         in0=q_raw[:, i % 2, :].rearrange("p (a t) -> p a t", a=2), scalar=par[:, col:col + 1],
                                         in1=rs[:, i % 2, :].rearrange("p (a t) -> p a t", a=2),
                                         op0=ALU.mult, op1=ALU.mult).then_inc(q_n, 1)

            dve.wait_ge(const, n_const["early"])
            conv_value(0)
            conv_taps(0, 0, 18)
            conv_value(1)
            conv_taps(0, 18, TAPS)
            conv_taps(1, 0, 16)
            qk_norm(0)
            qk_norm(1)
            conv_taps(1, 16, TAPS)
            qk_norm(2)
            qk_norm(3)
            dve.wait_ge(lam_e, 1)
            dve.tensor_tensor(lam[:, 4:5], lam[:, 3:4], lam[:, 2:3], ALU.subtract).then_inc(lam_d, 1)
            dve.wait_ge(lam_d, 4)
            dve.tensor_scalar(lam[:, 5:6], lam[:, 4:5], -LAM_INIT, None, ALU.add).then_inc(lam_d, 1)
            for b in range(6):
                n, w, idx = (4, P, 4 * b) if b < 2 else (2, T, 8 + 2 * (b - 2))
                dve.wait_ge(s_sc, b + 1)
                dve.tensor_reduce(smx[:, idx:idx + n], bank[:, 2 + b, 0:n * w].rearrange("p (n w) -> p n w", n=n),
                                  AX.X, ALU.max).then_inc(s_mx, 1)
                dve.wait_ge(s_mx, b + 1)
                dve.tensor_scalar(nmx[:, idx:idx + n], smx[:, idx:idx + n], -HD ** -0.5, None, ALU.mult).then_inc(s_nm, 1)
            for qt, pr in enumerate((p_0, p_1)):
                dve.wait_ge(s_ex, 8 * qt + 8)
                dve.reciprocal(rsum[:, 8 * qt:8 * qt + 8], ssum[:, 8 * qt:8 * qt + 8]).then_inc(s_rc, 1)
                dve.wait_ge(s_rc, 2 * qt + 1)
                dve.wait_ge(lam_d, 5)
                dve.tensor_scalar(rsum[:, 8 * qt + 4:8 * qt + 8], rsum[:, 8 * qt + 4:8 * qt + 8], lam[:, 5:6], None, ALU.mult).then_inc(s_rc, 1)
                for h in range(HEADS):
                    dve.tensor_scalar(pr[:, 0, h, :], pr[:, 0, h, :], rsum[:, 8 * qt + h:8 * qt + h + 1], None, ALU.mult).then_inc(s_w, 1)
                dve.wait_ge(s_rc, 2 * qt + 2)
                for h in range(HEADS):
                    dve.wait_ge(s_w, 8 * qt + h + 1)
                    dve.scalar_tensor_tensor(out=pr[:, 0, h, :], in0=pr[:, 1, h, :], scalar=rsum[:, 8 * qt + 4 + h:8 * qt + 5 + h],
                                             in1=pr[:, 0, h, :], op0=ALU.mult, op1=ALU.add).then_inc(s_w, 1)
            dve.wait_ge(sub_g, 1)
            for b in range(2):
                dve.wait_ge(a_rs, b + 1)
                dve.scalar_tensor_tensor(out=q_raw[:, b, :], in0=bank[:, 6 + b, :], scalar=par[:, C_SUB:C_SUB + 1], in1=rs[:, b, :],
                                         op0=ALU.mult, op1=ALU.mult).then_inc(a_of, 1)
            for b in range(2):
                dve.wait_ge(a_h, b + 1)
                dve.tensor_tensor(h_l[:, 2 * b:2 * b + 2, :], q_raw[:, b, :].rearrange("p (a t) -> p a t", a=2),
                                  h_h[:, 2 * b:2 * b + 2, :], ALU.subtract).then_inc(a_l, 1)
            for b in range(2):
                dve.wait_ge(g_m, b + 1)
                v = conv_y[:, 2 * b:2 * b + 2, :]
                dve.tensor_tensor(v, v, bank[:, 2 + b, :].rearrange("p (a t) -> p a t", a=2), ALU.subtract).then_inc(g_c, 1)
            for b in range(2):
                dve.wait_ge(g_rs, b + 1)
                v = conv_y[:, 2 * b:2 * b + 2, :]
                dve.tensor_tensor(v, v, rs[:, b, :].rearrange("p (a t) -> p a t", a=2), ALU.mult).then_inc(g_n, 1)
            for b in range(2):
                dve.wait_ge(g_h, b + 1)
                dve.tensor_tensor(h_l[:, 4 + 2 * b:6 + 2 * b, :], conv_y[:, 2 * b:2 * b + 2, :], h_h[:, 4 + 2 * b:6 + 2 * b, :],
                                  ALU.subtract).then_inc(g_l, 1)
            dve.wait_ge(r_high, 1)
            dve.tensor_tensor(router_l[:], router[:], router_h[:], ALU.subtract).then_inc(r_low, 1)
            for u in range(U_AB_OUT, U_FFN):
                split_low(dve, u + 3)
            residual(U_FFN)

            norm_scale(1)
            norm_low(1, C_FFN)

            def ffn_mul(s0, j2, par_s, used):
                dve.wait_ge(w_used, used)
                dve.wait_ge(f_silu, j2 + (s0 + 1))
                if s0:
                    dve.wait_ge(f_low, j2 + s0)
                dve.tensor_tensor(act_f[:], silu_g[:], bank[:, 2 + par_s, :], ALU.mult).then_inc(f_mul, 1)

            def ffn_low(s0, j2, par_s):
                dve.wait_ge(f_high, j2 + (s0 + 1))
                dve.tensor_tensor(act_l[:, par_s, :], act_f[:], act_h[:, par_s, :], ALU.subtract).then_inc(f_low, 1)

            def ffn_step(s0, j, par_s):
                ffn_mul(s0, j * 2, par_s, j * 6 + (U_FFN + (3 * s0 + 1 if s0 else 2)))
                split_low(dve, U_FFN + 3 * s0 + 3, j)
                ffn_low(s0, j * 2, par_s)
                split_low(dve, U_FFN + 3 * s0 + 4, j)
                split_low(dve, U_FFN + 3 * s0 + 5, j)

            ffn_step(0, 0, 0)
            ffn_step(1, 0, 1)
            with dve.Fori(0, 4) as j:
                ffn_step(2, j, 0)
                ffn_step(3, j, 1)
            ffn_step(10, 0, 0)
            residual(U_HG_IN)

            norm_scale(2)
            norm_low(2, C_MIX + 8)
            dve.tensor_tensor(lb[:, 0, :], par[:, C_LB:C_LB + HH], par[:, C_LB:C_LB + HH], ALU.subtract).then_inc(lb_d, 1)
            dve.wait_ge(lb_d, 2)
            dve.reciprocal(lb[:, 2, :], lb[:, 1, :]).then_inc(lb_d, 1)
            dve.wait_ge(lb_d, 3)
            dve.tensor_tensor(lb[:, 3, :], lb[:, 1, :], lb[:, 2, :], ALU.mult).then_inc(lb_d, 1)
            dve.wait_ge(lb_d, 4)
            dve.tensor_tensor(lb[:, 0, :], lb[:, 3, :], lb[:, 3, :], ALU.subtract).then_inc(lb_d, 1)
            dve.wait_ge(lb_d, 5)
            dve.tensor_scalar(lb[:, 4, :], lb[:, 0, :], -1.0, 1.0, ALU.mult, ALU.add).then_inc(lb_d, 1)
            dve.memset(dq[:], 0.0).then_inc(hg_z, 1)
            dve.memset(dk[:], 0.0).then_inc(hg_z, 1)
            dve.wait_ge(lb_d, 6)
            for i in range(N_HG_IN):
                if i < 4:
                    dve.wait_ge(hg_ev, 2 * i + 2)
                    for h in (2 * i, 2 * i + 1):
                        dve.tensor_scalar(log_f[:, h, :], log_f[:, h, :], lb[:, 4, h:h + 1], lb[:, 0, h:h + 1],
                                          ALU.mult, ALU.add).then_inc(hg_z, 1)
                        dve.tensor_scalar(key_t[:, h, :], key_t[:, h, :], lb[:, 4, h:h + 1], None, ALU.mult).then_inc(hg_d, 1)
                    dve.wait_ge(hg_z, 2 * i + 4)
                    dve.tensor_scalar(log_f[:, 2 * i:2 * i + 2, :], log_f[:, 2 * i:2 * i + 2, :], 1.2e-38, None, ALU.max).then_inc(hg_d, 1)
                split_low(dve, U_HG_IN + i + 3)
                if i == 13:
                    for q in range(4):
                        tt, hq = q // 2, q % 2
                        dve.wait_ge(hg_h, q + 1)
                        v = slice(hq * 512, (hq + 1) * 512)
                        dve.tensor_tensor(lf_l[:, tt, v], bank[:, 2 + q, :], lf_h[:, tt, v], ALU.subtract).then_inc(hg_l, 1)
            for q in range(4):
                tt, hq = q // 2, q % 2
                dve.wait_ge(hd, q + 1)
                dve.tensor_tensor(att[:, 4 * hq:4 * hq + 4, 2 * tt, :], bank[:, 2 + q, :].rearrange("p (h t) -> p h t", h=4),
                                  ident[:].unsqueeze(1).to_broadcast([P, 4, P]), ALU.mult).then_inc(hd_cp, 1)

            def decayed(g):
                p, hp, tt = g // 8, (g // 2) % 4, g % 2
                dve.wait_ge(sp_e, g + 1)
                if g >= 2:
                    dve.wait_ge(sp_s, g if (p == 3 and g % 2 == 0 and g >= 26) else g - 1)
                hs = slice(2 * hp, 2 * hp + 2)
                e = decay[:, g % 2, :].rearrange("p (a l t) -> p a l t", a=2, l=2)
                tq = dq[:, g % 2, :].rearrange("p (a l t) -> p a l t", a=2, l=2)
                tk = dk[:, g % 2, :].rearrange("p (a l t) -> p a l t", a=2, l=2)
                q = qry_t[:, hs, tt * P:(tt + 1) * P]
                k = key_t[:, hs, tt * P:(tt + 1) * P]
                for li in range(2):
                    if 2 * p + li < 7:
                        h = LEVELS[2 * p + li]
                        how = "p a (b s r) -> p a b s r"
                        for half, dst, src in ((1, tq, q), (0, tk, k)):
                            ins = dve.tensor_tensor(dst[:, :, li, :].rearrange(how, s=2, r=h)[:, :, :, half, :],
                                                    src.rearrange(how, s=2, r=h)[:, :, :, half, :],
                                                    e[:, :, li, :].rearrange(how, s=2, r=h)[:, :, :, half, :], ALU.mult)
                    elif tt == 0:
                        ins = dve.tensor_tensor(tk[:, :, li, :], k, e[:, :, li, :], ALU.mult)
                    else:
                        ins = dve.tensor_tensor(tq[:, :, li, :], q, e[:, :, li, :], ALU.mult)
                ins.then_inc(sp_m, 1)

            def keep(g, li):
                p, hp, tt = g // 8, (g // 2) % 4, g % 2
                b = bank[:, 2 + g % 4, :].rearrange("p (a l t) -> p a l t", a=2, l=2)[:, :, li, :]
                if li == 0:
                    dve.wait_ge(sp_s, g + 1)
                    if g >= 8:
                        dve.wait_ge(sp_c1, second(g - 8))
                else:
                    dve.wait_ge(sp_c0, g + 1)
                if 2 * p + li < 7:
                    dve.copy_predicated(att[:, 2 * hp:2 * hp + 2, 2 * tt, :],
                                        lmask[:, 2 * p + li, :].unsqueeze(1).to_broadcast([P, 2, P]), b).then_inc((sp_c0, sp_c1)[li], 1)
                elif tt == 1:
                    dve.tensor_copy(att[:, 2 * hp:2 * hp + 2, 1, :], b).then_inc(sp_c1, 1)

            dve.wait_ge(const, n_const["all"])
            dve.wait_ge(hd_cp, 4)
            decayed(0)
            for g in range(GROUPS):
                if g + 1 < GROUPS:
                    decayed(g + 1)
                keep(g, 0)
                if g:
                    keep(g - 1, 1)
            keep(GROUPS - 1, 1)
            dve.wait_ge(hg_gg, HH)

            def hg_low(j):
                dve.wait_ge(o_h, j + 1)
                dve.tensor_tensor(h_l[:, 2 * j:2 * j + 2, :], dk[:, j % 2, :].rearrange("p (a t) -> p a t", a=2),
                                  h_h[:, 2 * j:2 * j + 2, :], ALU.subtract).then_inc(o_l, 1)

            for j in range(4):
                dve.wait_ge(o_rs, j + 1)
                if j >= 2:
                    dve.wait_ge(o_l, j - 1)
                dve.tensor_tensor(dk[:, j % 2, :], bank[:, 2 + j, :], dq[:, j % 2, :], ALU.mult).then_inc(o_n, 1)
                dve.wait_ge(o_n, j + 1)
                v = dk[:, j % 2, :].rearrange("p (a t) -> p a t", a=2)
                dve.tensor_tensor(v, v, gate_t[:, 2 * j:2 * j + 2, :], ALU.mult).then_inc(o_g, 1)
                if j >= 1:
                    hg_low(j - 1)
            hg_low(3)
            for u in range(U_HG_OUT, U_MOE):
                split_low(dve, u + 3)
            residual(U_MOE)

            norm_scale(3)
            norm_low(3, C_FFN + 8)
            done = [0]

            def step(ins):
                done[0] += 1
                ins.then_inc(r_d, 1)
                dve.wait_ge(r_d, done[0])

            def wide(v):
                return v.unsqueeze(2).to_broadcast([P, TT, NE])

            ordr = expert_no[:].unsqueeze(1).to_broadcast([P, TT, NE])
            dve.wait_ge(r_lg, 1)
            step(dve.tensor_copy(logit[:, 0, :, :], bank[:, 4, 0:TT * NE].rearrange("p (a e) -> p a e", a=TT)))
            for k in range(2):
                src, sl = logit[:, 2 * k + 0, :, :] if k == 0 else logit[:, 3, :, :], logit[:, 4 + k, :, :]
                step(dve.tensor_reduce(pick[:, k, :], src, AX.X, ALU.max))
                step(dve.tensor_tensor(logit[:, 1, :, :], src, wide(pick[:, k, :]), ALU.is_ge))
                step(dve.tensor_tensor(logit[:, 2, :, :], logit[:, 1, :, :], ordr, ALU.mult))
                step(dve.tensor_reduce(pick[:, 2 + k, :], logit[:, 2, :, :], AX.X, ALU.max))
                step(dve.tensor_tensor(sl, ordr, wide(pick[:, 2 + k, :]), ALU.is_equal))
                if k == 0:
                    step(dve.scalar_tensor_tensor(out=logit[:, 3, :, :], in0=sl, scalar=-3.0e38, in1=src, op0=ALU.mult, op1=ALU.add))
            step(dve.tensor_tensor(pick[:, 4, :], pick[:, 1, :], pick[:, 0, :], ALU.subtract))
            n_const["exp"] = done[0]
            step(dve.tensor_tensor(logit[:, 6, :, :], logit[:, 4, :, :], logit[:, 5, :, :], ALU.add))
            n_const["sel"] = done[0]
            dve.wait_ge(r_e, 1)
            step(dve.tensor_scalar(pick[:, 6, :], pick[:, 5, :], 1.0, None, ALU.add))
            step(dve.reciprocal(pick[:, 7, :], pick[:, 6, :]))
            step(dve.tensor_tensor(pick[:, 8, :], pick[:, 5, :], pick[:, 7, :], ALU.mult))
            step(dve.tensor_tensor(logit[:, 7, :, :], logit[:, 4, :, :], wide(pick[:, 7, :]), ALU.mult))
            step(dve.tensor_tensor(logit[:, 8, :, :], logit[:, 5, :, :], wide(pick[:, 8, :]), ALU.mult))
            step(dve.memset(comb[:], 0.0))
            step(dve.memset(rank[:], -1.0))
            step(dve.tensor_tensor(comb[:, 0:NE, :].rearrange("p e a -> p a e"), logit[:, 7, :, :], logit[:, 8, :, :], ALU.add))
            dve.wait_ge(r_rank, 1)
            step(dve.scalar_tensor_tensor(out=logit[:, 9, :, :], in0=bank[:, 5, 0:TT * NE].rearrange("p (a e) -> p a e", a=TT), scalar=1.0,
                                          in1=logit[:, 6, :, :], op0=ALU.add, op1=ALU.mult))
            step(dve.tensor_scalar(rank[:, 0:NE, :].rearrange("p e a -> p a e"), logit[:, 9, :, :], -1.0, None, ALU.add))
            step(dve.tensor_reduce(pick[:, 9, 0:1], bank[:, 5, TT * NE:(TT + 1) * NE], AX.X, ALU.max))
            step(dve.tensor_scalar(pick[:, 10, 0:1], pick[:, 9, 0:1], CAP + 0.5, None, ALU.is_gt))
            dve.tensor_copy(flag[:], pick[:, 10, 0:1]).then_inc(r_flag, 1)
            dve.memset(comb_s[:], 0.0).then_inc(m_add, 1)

            def choose(e, r, pts, n):
                if pts is not None:
                    dve.wait_ge(m_pt, pts)
                dve.tensor_copy(rank_e[:], rank[:, bass.ds(e, 1), :].squeeze(1)).then_inc(m_re, 1)
                dve.tensor_copy(comb_e[:], comb[:, bass.ds(e, 1), :].squeeze(1)).then_inc(m_re, 1)
                dve.wait_ge(m_re, n * 2 + 2)
                for tt in range(TT):
                    dve.tensor_scalar(sel[:, tt, :], slot_no[:, r, :], rank_e[:, tt:tt + 1], None, ALU.is_equal).then_inc(m_sel, 1)

            def gather_low(n):
                for j in range(2):
                    dve.wait_ge(m_hh, n * 2 + (j + 1))
                    dve.tensor_tensor(hs_l[:, 4 * j:4 * j + 4, :], bank[:, 5 + j, :].rearrange("p (c t) -> p c t", c=4),
                                      hs_h[:, 4 * j:4 * j + 4, :], ALU.subtract).then_inc(m_hl, 1)

            def moe_mul(g, b):
                dve.wait_ge(m_si, g + 1)
                dve.tensor_tensor(m_act[:], m_silu[:], bank[:, b, UC:2 * UC], ALU.mult).then_inc(m_mul, 1)

            def moe_low(g):
                dve.wait_ge(m_ah, g + 1)
                dve.tensor_tensor(ma_l[:], bank[:, 2, 0:UC], ma_h[:], ALU.subtract).then_inc(m_al, 1)

            def moe_round(r):
                u = U_MOE + r * NE * MOE_UNITS
                g0 = r * NE * MOE_STEPS
                n0 = r * (NE + 1)
                if r:
                    dve.wait_ge(m_gat, 2 * n0)
                choose(0, r, None, n0)
                gather_low(n0)
                with dve.Fori(0, NE) as e:
                    q = e * 7
                    g = e * MOE_STEPS + g0
                    split_low(dve, u + 3, q)
                    dve.wait_ge(m_scat, e + (r * NE + 1))
                    dve.tensor_copy(comb_s[:], bank[:, 7, T:T + 1]).then_inc(m_comb, 1)
                    moe_mul(g, 0)
                    split_low(dve, u + 4, q)
                    moe_low(g)
                    split_low(dve, u + 5, q)
                    with dve.Fori(0, 6) as j:
                        for k in (0, 1):
                            gs = g + j * 2 + (1 + k)
                            moe_mul(gs, (1 + k) % 2)
                            split_low(dve, u + 6 + 3 * k, q + j)
                            split_low(dve, u + 7 + 3 * k, q + j)
                            moe_low(gs)
                            split_low(dve, u + 8 + 3 * k, q + j)
                    choose(e + 1, r, e + (r * NE + 1), e + (n0 + 1))
                    moe_mul(g + 13, 1)
                    moe_low(g + 13)
                    split_low(dve, u + 42, q)
                    dve.wait_ge(w_used, e * MOE_UNITS + (u + 42))
                    dve.wait_ge(m_comb, e + (r * NE + 1))
                    dve.wait_ge(m_add, e * 4 + (r * NE * 4 + 1))
                    for j in range(2):
                        dve.tensor_scalar(y_f[:, j * 512:(j + 1) * 512], bank[:, 3 + j, :], comb_s[:, 0:1], None, ALU.mult).then_inc(m_y, 1)
                    for j in range(2):
                        dve.wait_ge(m_yh, e * 2 + (r * NE * 2 + j + 1))
                        dve.tensor_tensor(y_l[:, j * 512:(j + 1) * 512], y_f[:, j * 512:(j + 1) * 512],
                                          y_h[:, j * 512:(j + 1) * 512], ALU.subtract).then_inc(m_yl, 1)
                    gather_low(e + (n0 + 1))
                    split_low(dve, u + 43, q)
                    for i in range(4):
                        dve.wait_ge(m_sc, e * 4 + (r * NE * 4 + i + 1))
                        v = x[:, i // 2, (i % 2) * 512:(i % 2 + 1) * 512]
                        dve.tensor_tensor(v, bank[:, (0, 1, 2, 7)[i], :], v, ALU.add).then_inc(m_add, 1)
                    split_low(dve, u + 44, q)

            moe_round(0)
            over = dve.value_load(flag[0:1, 0:1], min_val=0, max_val=1)
            with dve.If(over > 0):
                moe_round(1)

        @block.scalar
        def _(act):
            act.wait_ge(const, n_const["rows"])
            with nc.allow_non_contiguous_dma(reason="small parameters, loaded once"):
                rows = [(A["mix_norm"], C_MIX, "l (c p) -> (l c) p"), (A["ffn_norm"], C_FFN, "l (c p) -> (l c) p"),
                        (A["hgrn_norm"], C_HN, "l (c p) -> (l c) p"), (A["hgrn_lb_logits"], C_LB, "l (c p) -> (l c) p"),
                        (A["conv_dw_bias"], C_DWB, "l (c p) -> (l c) p"), (A["conv_gn_gain"], C_GG, "l (c p) -> (l c) p"),
                        (A["conv_gn_bias"], C_GB, "l (c p) -> (l c) p"), (A["da_subln"], C_SUB, "l (c p) -> (l c) p")]
                for src, at, how in rows:
                    v = src.rearrange(how, p=P)
                    act.dma_start(par_rows[at:at + v.shape[0], :], v).then_inc(par_in, 16)
                for c in (0, 1):
                    act.dma_start(par_rows[C_QG:C_QG + 1, c * HD:(c + 1) * HD], A["da_q_gain"]).then_inc(par_in, 16)
                    act.dma_start(par_rows[C_KG:C_KG + 1, c * HD:(c + 1) * HD], A["da_k_gain"]).then_inc(par_in, 16)
                act.dma_start(dw_rows[0:TAPS * 4, :], A["conv_dw"].rearrange("o k (c p) -> (o k c) p", p=P)).then_inc(par_in, 16)
                act.dma_start(lam_rows[:], A["da_lambda"].rearrange("o a b -> o (a b)").to_broadcast([P, 4 * HD])).then_inc(lam_in, 16)
                act.dma_start(router[:], A["moe_router"][0].rearrange("(c p) e -> p c e", p=P)).then_inc(rout_in, 16)

            def norm_sums(n):
                for tt in range(TT):
                    if n == 0:
                        act.wait_ge(x_in, 16 * TT)
                    else:
                        act.wait_ge(x_add, 4 * n)
                        act.wait_ge(n_t, 4 * n)
                    act.activation(xn[:, tt, :], x[:, tt, :], ACT.Square, accum_out=n_stat[:, n, 0, tt:tt + 1]).then_inc(n_sq, 1)
                act.wait_ge(n_sq, TT * (n + 1))
                act.wait_ge(dve_const, 1)
                act.activation(n_stat[:, n, 1, :], n_stat[:, n, 0, :], ACT.Ln, scale=1.0 / D, bias=eps[:]).then_inc(n_ln, 1)
                act.wait_ge(n_ln, n + 1)
                act.activation(n_stat[:, n, 2, :], n_stat[:, n, 1, :], ACT.Exp, scale=-0.5).then_inc(n_rs, 1)

            def norm_high(n, col):
                if n == 0:
                    act.wait_ge(par_cp, 1)
                for j in range(4):
                    act.wait_ge(n_t, 4 * n + j + 1)
                    b = (2 + j) if n == 0 else j
                    for c in range(2):
                        act.activation(h_h[:, 2 * j + c, :], bank[:, b, c * T:(c + 1) * T], ACT.Copy,
                                       scale=par[:, col + 2 * j + c:col + 2 * j + c + 1]).then_inc(n_high, 1)

            def inv_rms(src, dst, ln, rs_sem, n):
                act.activation(dst, src, ACT.Ln, bias=eps[:]).then_inc(ln, 1)
                act.wait_ge(ln, n + 1)
                act.activation(dst, dst, ACT.Exp, scale=-0.5).then_inc(rs_sem, 1)

            norm_sums(0)
            split_high(act, 0)
            norm_high(0, C_MIX)
            split_high(act, 1)
            split_high(act, 2)

            def qk_inv(i):
                act.wait_ge(qk_ms, i + 1)
                if i >= 2:
                    act.wait_ge(q_n, i - 1)
                inv_rms(bank[:, 6 + i % 2, :], rs[:, i % 2, :], qk_ln, qk_rs, i)

            for u in range(N_AB_IN):
                act.wait_ge(w_used, u + 1)
                if u in (1, 3):
                    if u == 3:
                        act.wait_ge(c_g, 1)
                    act.activation(sig[:], bank[:, 1, :], ACT.Sigmoid).then_inc(c_s, 1)
                if 4 <= u < 8:
                    i = u - 4
                    if i >= 2:
                        act.wait_ge(q_n, i - 1)
                        act.wait_ge(qk_ms, i - 1)
                    act.activation(q_raw[:, i % 2, :], bank[:, u % 2, :], ACT.Copy).then_inc(qk_raw, 1)
                    act.activation(sq[:, i % 2, :], bank[:, u % 2, :], ACT.Square).then_inc(qk_sq, 1)
                if u >= 8:
                    act.activation(v_n[:, :, (u - 8) * UC:(u - 7) * UC], bank[:, u % 2, :].rearrange("p (a f) -> p a f", a=TT),
                                   ACT.Copy).then_inc(v_cp, 1)
                split_high(act, u + 3)
                if 5 <= u <= 8:
                    qk_inv(u - 5)
            act.wait_ge(lam_d, 3)
            act.activation(lam[:, 2:4], lam[:, 0:2], ACT.Exp).then_inc(lam_e, 1)
            for b in range(6):
                act.wait_ge(s_nm, b + 1)
                n = 4 if b < 2 else 2
                for g in range(n):
                    idx = 4 * b + g if b < 2 else 8 + 2 * (b - 2) + g
                    c, h = (b, g) if b < 2 else ((b - 2) // 2, 2 * ((b - 2) % 2) + g)
                    w = P if b < 2 else T
                    dst = p_0[:, c, h, :] if b < 2 else p_1[:, c, h, :]
                    act.activation(dst, bank[:, 2 + b, g * w:(g + 1) * w], ACT.Exp, scale=HD ** -0.5,
                                   bias=nmx[:, idx:idx + 1], accum_out=ssum[:, idx:idx + 1]).then_inc(s_ex, 1)
            for h in range(HEADS):
                act.wait_ge(a_t, h + 1)
                act.activation(w_t[:, h, :], bank[:, 2 + h, 0:384], ACT.Copy).then_inc(a_wt, 1)
            act.wait_ge(qk_ms, 4)
            for b in range(2):
                act.wait_ge(a_o, b + 1)
                act.activation(sq[:, b, :], bank[:, 6 + b, :], ACT.Square).then_inc(a_sq, 1)
            for b in range(2):
                act.wait_ge(a_ms, b + 1)
                act.wait_ge(q_n, 4)
                inv_rms(bank[:, b, :], rs[:, b, :], a_ln, a_rs, b)
            for b in range(2):
                act.wait_ge(a_of, b + 1)
                act.activation(h_h[:, 2 * b:2 * b + 2, :], q_raw[:, b, :].rearrange("p (a t) -> p a t", a=2), ACT.Copy).then_inc(a_h, 1)
            for b in range(2):
                act.wait_ge(g_c, b + 1)
                act.activation(sq[:, b, :].rearrange("p (a t) -> p a t", a=2), conv_y[:, 2 * b:2 * b + 2, :], ACT.Square).then_inc(g_sq, 1)
            for b in range(2):
                act.wait_ge(g_v, b + 1)
                act.wait_ge(a_of, b + 1)
                inv_rms(bank[:, 2 + b, :], rs[:, b, :], g_ln, g_rs, b)
            for b in range(2):
                act.wait_ge(g_n, b + 1)
                for c in (2 * b, 2 * b + 1):
                    act.activation(conv_y[:, c, :], conv_y[:, c, :], ACT.Silu, scale=par[:, C_GG + c:C_GG + c + 1],
                                   bias=par[:, C_GB + c:C_GB + c + 1]).then_inc(g_s, 1)
                act.wait_ge(g_s, 2 * b + 2)
                act.activation(h_h[:, 4 + 2 * b:6 + 2 * b, :], conv_y[:, 2 * b:2 * b + 2, :], ACT.Copy).then_inc(g_h, 1)
            act.wait_ge(rout_in, 16)
            act.activation(router_h[:], router[:], ACT.Copy).then_inc(r_high, 1)
            for u in range(U_AB_OUT, U_FFN):
                split_high(act, u + 3)

            norm_sums(1)
            norm_high(1, C_FFN)

            def ffn_gate(s0, j2, s_par, a_used):
                act.wait_ge(w_used, a_used)
                if not (isinstance(j2, int) and s0 + j2 == 0):
                    act.wait_ge(f_mul, s0 + j2)
                act.activation(silu_g[:], bank[:, s_par, :], ACT.Silu).then_inc(f_silu, 1)

            def ffn_high(s0, j2, s_par):
                act.wait_ge(f_mul, s0 + j2 + 1)
                if s0 >= 2:
                    act.wait_ge(w_used, U_FFN + 3 * s0 - 1 + (j2 * 3))
                act.activation(act_h[:, s_par, :], act_f[:], ACT.Copy).then_inc(f_high, 1)

            ffn_gate(0, 0, 0, U_FFN + 1)
            split_high(act, U_FFN + 3)
            ffn_high(0, 0, 0)
            split_high(act, U_FFN + 4)
            split_high(act, U_FFN + 5)
            ffn_gate(1, 0, 1, U_FFN + 3)
            split_high(act, U_FFN + 6)
            ffn_high(1, 0, 1)
            split_high(act, U_FFN + 7)
            split_high(act, U_FFN + 8)
            with act.Fori(0, 4) as j:
                for k in (0, 1):
                    ffn_gate(2 + k, j * 2, k, U_FFN + 6 + 3 * k + j * 6)
                    split_high(act, U_FFN + 9 + 3 * k, j)
                    ffn_high(2 + k, j * 2, k)
                    split_high(act, U_FFN + 10 + 3 * k, j)
                    split_high(act, U_FFN + 11 + 3 * k, j)
            ffn_gate(10, 0, 0, U_FFN + 30)
            split_high(act, U_FFN + 33)
            ffn_high(10, 0, 0)
            split_high(act, U_FFN + 34)
            split_high(act, U_FFN + 35)

            norm_sums(2)
            norm_high(2, C_MIX + 8)
            act.wait_ge(lb_d, 1)
            act.activation(lb[:, 1, :], lb[:, 0, :], ACT.Exp).then_inc(lb_d, 1)
            for i in range(N_HG_IN):
                act.wait_ge(w_used, U_HG_IN + i + 1)
                src = bank[:, (U_HG_IN + i) % 2, :].rearrange("p (a t) -> p a t", a=2)
                c = 2 * (i % 4)
                if i < 4:
                    act.activation(log_f[:, c:c + 2, :], src, ACT.Sigmoid).then_inc(hg_ev, 1)
                    act.activation(key_t[:, c:c + 2, :], src, ACT.Sigmoid, scale=-1.0).then_inc(hg_ev, 1)
                elif i < 8:
                    act.activation(qry_t[:, c:c + 2, :], src, ACT.Silu).then_inc(hg_ev, 1)
                elif i < 12:
                    if i == 8:
                        act.wait_ge(n_t, 12)
                    act.activation(gate_t[:, c:c + 2, :], src, ACT.Silu).then_inc(hg_ev, 1)
                else:
                    act.activation(val_n[:, :, (i - 12) * UC:(i - 11) * UC], src, ACT.Copy).then_inc(hg_ev, 1)
                split_high(act, U_HG_IN + i + 3)
                if i == 11:
                    for q in range(4):
                        act.wait_ge(hg_d, 3 * 4)
                        act.activation(log_f[:, 2 * q:2 * q + 2, :], log_f[:, 2 * q:2 * q + 2, :], ACT.Ln).then_inc(hg_ln, 1)
                if i == 13:
                    for q in range(4):
                        act.wait_ge(hg_t, q + 1)
                        tt, hq = q // 2, q % 2
                        act.activation(lf_h[:, tt, hq * 512:(hq + 1) * 512], bank[:, 2 + q, :], ACT.Copy).then_inc(hg_h, 1)
            for g in range(GROUPS):
                act.wait_ge(sp_d, g + 1)
                if g >= 2:
                    act.wait_ge(sp_m, g - 1)
                act.activation(decay[:, g % 2, :], bank[:, (0, 1, 6)[g % 3], :], ACT.Exp).then_inc(sp_e, 1)

            def hg_inv(j):
                act.wait_ge(o_ms, j + 1)
                if j >= 2:
                    act.wait_ge(o_n, j - 1)
                inv_rms(bank[:, (0, 1, 6, 7)[j], :], dq[:, j % 2, :], o_ln, o_rs, j)

            for j in range(4):
                act.wait_ge(o_o, j + 1)
                if j >= 2:
                    act.wait_ge(o_ms, j - 1)
                act.activation(decay[:, j % 2, :], bank[:, 2 + j, :], ACT.Square).then_inc(o_sq, 1)
                if j >= 1:
                    hg_inv(j - 1)
            hg_inv(3)
            for j in range(4):
                act.wait_ge(o_g, j + 1)
                act.activation(h_h[:, 2 * j:2 * j + 2, :], dk[:, j % 2, :].rearrange("p (a t) -> p a t", a=2), ACT.Copy).then_inc(o_h, 1)
            for u in range(U_HG_OUT, U_MOE):
                split_high(act, u + 3)

            act.wait_ge(x_add, 12)
            act.dma_start(gain_row[:], A["ffn_norm"][1:2, :].to_broadcast([P, D])).then_inc(gain_in, 16)
            norm_sums(3)
            norm_high(3, C_FFN + 8)
            act.wait_ge(r_d, n_const["exp"])
            act.activation(pick[:, 5, :], pick[:, 4, :], ACT.Exp).then_inc(r_e, 1)

            def gather_high(n):
                for j in range(2):
                    act.wait_ge(m_gat, n * 2 + (j + 1))
                    act.activation(hs_h[:, 4 * j:4 * j + 4, :], bank[:, 5 + j, :].rearrange("p (c t) -> p c t", c=4), ACT.Copy).then_inc(m_hh, 1)

            def moe_gate(g, first, b_par, b_used):
                act.wait_ge(w_used, b_used)
                if not first:
                    act.wait_ge(m_mul, g)
                act.activation(m_silu[:], bank[:, b_par, 0:UC], ACT.Silu).then_inc(m_si, 1)

            def moe_high(g):
                act.wait_ge(m_t, g + 1)
                act.activation(ma_h[:], bank[:, 2, 0:UC], ACT.Copy).then_inc(m_ah, 1)

            def moe_round(r):
                u = U_MOE + r * NE * MOE_UNITS
                g0 = r * NE * MOE_STEPS
                gather_high(r * (NE + 1))
                with act.Fori(0, NE) as e:
                    q = e * 7
                    g = e * MOE_STEPS + g0
                    gat = e + r * (NE + 1)
                    split_high(act, u + 3, q)
                    act.wait_ge(m_pt, e + (r * NE + 1))
                    act.activation(scat[:], bank[:, 7, 0:T], ACT.Copy).then_inc(m_scat, 1)
                    act.wait_ge(w_used, e * MOE_UNITS + (u + 2))
                    act.activation(m_silu[:], bank[:, 0, 0:UC], ACT.Silu).then_inc(m_si, 1)
                    split_high(act, u + 4, q)
                    moe_high(g)
                    split_high(act, u + 5, q)
                    with act.Fori(0, 6) as j:
                        for k in (0, 1):
                            gs = g + j * 2 + (1 + k)
                            moe_gate(gs, False, (1 + k) % 2, e * MOE_UNITS + j * 6 + (u + 4 + 3 * k))
                            split_high(act, u + 6 + 3 * k, q + j)
                            split_high(act, u + 7 + 3 * k, q + j)
                            moe_high(gs)
                            split_high(act, u + 8 + 3 * k, q + j)
                    moe_gate(g + 13, False, 1, e * MOE_UNITS + (u + 40))
                    moe_high(g + 13)
                    split_high(act, u + 42, q)
                    for j in range(2):
                        act.wait_ge(m_y, e * 2 + (r * NE * 2 + j + 1))
                        act.activation(y_h[:, j * 512:(j + 1) * 512], y_f[:, j * 512:(j + 1) * 512], ACT.Copy).then_inc(m_yh, 1)
                    gather_high(gat + 1)
                    split_high(act, u + 43, q)
                    split_high(act, u + 44, q)

            moe_round(0)
            act.wait_ge(r_flag, 1)
            over = act.value_load(flag[0:1, 0:1], min_val=0, max_val=1)
            with act.If(over > 0):
                moe_round(1)

        @block.tensor
        def _(pe):
            def three(o, a_high, a_low, b_high, b_low, start, stop):
                pe.matmul(o, a_high, b_high, start=start, stop=False, skip_group_check=True)
                pe.matmul(o, a_high, b_low, start=False, stop=False, skip_group_check=True)
                return pe.matmul(o, a_low, b_high, start=False, stop=stop, skip_group_check=True)

            def unit_to_features(u0, b, rounds=0):
                wait_split(pe, u0, rounds)
                wh, wl = as_in(w_h, u0 % S), as_in(w_l, u0 % S)
                for mch in range(2):
                    f = slice(mch * P, (mch + 1) * P)
                    for c in range(KC):
                        last = three(bank[:, b, mch * T:(mch + 1) * T], wh[:, c, f], wl[:, c, f], h_h[:, c, :], h_l[:, c, :],
                                     c == 0, c == KC - 1)
                last.then_inc(w_used, 1)

            def unit_to_tokens(u0, b):
                wait_split(pe, u0)
                wh, wl = as_in(w_h, u0 % S), as_in(w_l, u0 % S)
                for tt in range(TT):
                    t = slice(tt * P, (tt + 1) * P)
                    for c in range(KC):
                        last = three(bank[:, b, tt * UC:(tt + 1) * UC], h_h[:, c, t], h_l[:, c, t], wh[:, c, :], wl[:, c, :],
                                     c == 0, c == KC - 1)
                last.then_inc(w_used, 1)

            def unit_out(u0, ah, al, first, last_unit, rounds=0):
                wait_split(pe, u0, rounds)
                wh, wl = as_out(w_h, u0 % S), as_out(w_l, u0 % S)
                for c in range(OC):
                    for tt in range(TT):
                        for half in range(2):
                            v = slice(half * 512, (half + 1) * 512)
                            last = three(bank[:, 4 + 2 * tt + half, :], ah(c, tt), al(c, tt), wh[:, c, v], wl[:, c, v],
                                         first and c == 0, last_unit and c == OC - 1)
                last.then_inc(w_used, 1)

            def norm_turn(n):
                pe.wait_ge(n_xn, 2 * n + 2)
                for j in range(4):
                    b = (2 + j) if n == 0 else j
                    for c in range(2):
                        for tt in range(TT):
                            last = pe.transpose(bank[:, b, c * T + tt * P:c * T + (tt + 1) * P],
                                                xn[:, tt, (2 * j + c) * P:(2 * j + c + 1) * P], ident[:])
                    last.then_inc(n_t, 1)
                pe.wait_ge(n_low, 8 * n + 8)

            pe.wait_ge(const, n_const["early"])
            pe.wait_ge(par_in, 16 * 13)
            pe.transpose(bank[:, 0, 0:P], par_rows[:], ident[:]).then_inc(par_t, 1)
            pe.transpose(bank[:, 1, 0:P], dw_rows[:], ident[:]).then_inc(par_t, 1)
            pe.wait_ge(par_cp, 2)
            norm_turn(0)
            free = {2: (c_g, 1), 3: (c_s, 1), 4: (c_g, 2), 5: (c_s, 2), 6: (qk_sq, 1), 7: (qk_sq, 2), 8: (qk_sq, 3), 9: (qk_sq, 4)}

            def qk_mean(i):
                pe.wait_ge(qk_sq, i + 1)
                if i >= 2:
                    pe.wait_ge(qk_ln, i - 1)
                pe.matmul(bank[:, 6 + i % 2, :], mean_64[:], sq[:, i % 2, :], start=True, stop=True).then_inc(qk_ms, 1)

            for u in range(N_AB_IN):
                if u in free:
                    pe.wait_ge(*free[u])
                (unit_to_features if u < 8 else unit_to_tokens)(u, u % 2)
                if 5 <= u <= 8:
                    qk_mean(u - 5)
            pe.wait_ge(q_n, 4)
            pe.wait_ge(qk_ln, 4)
            for b in range(6):
                qt = 0 if b < 2 else 1
                c = b if b < 2 else (b - 2) // 2
                n, w = (4, P) if qt == 0 else (2, T)
                rows = slice(HD * c, HD * (c + 1))
                for g in range(n):
                    h = g if qt == 0 else 2 * ((b - 2) % 2) + g
                    pe.matmul(bank[:, 2 + b, g * w:(g + 1) * w], q_t[rows, h, qt * P:(qt + 1) * P], k_t[rows, h, 0:w],
                              start=True, stop=False, skip_group_check=True)
                    last = pe.matmul(bank[:, 2 + b, g * w + qt * P:g * w + (qt + 1) * P], ident_b[:], mask_b[:], start=False, stop=True,
                                     skip_group_check=True)
                last.then_inc(s_sc, 1)
            for h in range(HEADS):
                pe.wait_ge(s_w, 8 + 4 + h + 1)
                pe.transpose(bank[:, 2 + h, 0:P], p_0[:, 0, h, :], ident[:])
                pe.transpose(bank[:, 2 + h, P:2 * P], p_1[:, 0, h, 0:P], ident[:])
                pe.transpose(bank[:, 2 + h, 2 * P:3 * P], p_1[:, 0, h, P:2 * P], ident[:]).then_inc(a_t, 1)
            pe.wait_ge(v_cp, 2)
            for b in range(2):
                for h in (2 * b, 2 * b + 1):
                    pe.wait_ge(a_wt, h + 1)
                    o = (h % 2) * T
                    pe.matmul(bank[:, 6 + b, o:o + T], v_n[:, 0, h * P:(h + 1) * P], w_t[:, h, 0:T], start=True, stop=False,
                              skip_group_check=True)
                    last = pe.matmul(bank[:, 6 + b, o + P:o + T], v_n[:, 1, h * P:(h + 1) * P], w_t[:, h, T:T + P], start=False,
                                     stop=True, skip_group_check=True)
                last.then_inc(a_o, 1)
            for b in range(2):
                pe.wait_ge(a_sq, b + 1)
                pe.matmul(bank[:, b, :], mean_all[:], sq[:, b, :], start=True, stop=True).then_inc(a_ms, 1)
            pe.wait_ge(c_y, 4 * TAPS)
            for b in range(2):
                pe.matmul(bank[:, 2 + b, :], mean_64[:], conv_y[:, 2 * b:2 * b + 2, :], start=True, stop=True).then_inc(g_m, 1)
            for b in range(2):
                pe.wait_ge(g_sq, b + 1)
                pe.matmul(bank[:, 2 + b, :], mean_64[:], sq[:, b, :], start=True, stop=True).then_inc(g_v, 1)

            def from_h(i):
                return (lambda c, tt: h_h[:, 2 * i + c, tt * P:(tt + 1) * P]), (lambda c, tt: h_l[:, 2 * i + c, tt * P:(tt + 1) * P])

            for i in range(N_OUT):
                pe.wait_ge(*((a_l, i + 1) if i < 2 else (g_l, i - 1)))
                unit_out(U_AB_OUT + i, *from_h(i), i == 0, i == N_OUT - 1)
            norm_turn(1)

            def ffn_out_unit(s0, j, b, first, last_unit, u0=None):
                pe.wait_ge(f_low, j * 2 + (s0 + 1))
                unit_out(U_FFN + 3 * s0 + 4 if u0 is None else u0, lambda c, tt: act_h[:, b, c * T + tt * P:c * T + (tt + 1) * P],
                         lambda c, tt: act_l[:, b, c * T + tt * P:c * T + (tt + 1) * P], first, last_unit, j)

            def ffn_body(s0, j, b):
                nb = 1 - b
                if s0:
                    pe.wait_ge(f_silu, j * 2 + s0)
                unit_to_features(U_FFN + 3 * s0 + 2, nb, j)
                if s0:
                    pe.wait_ge(f_mul, j * 2 + s0)
                unit_to_features(U_FFN + 3 * s0 + 3, 2 + nb, j)
                ffn_out_unit(s0, j, b, s0 == 0, False)

            unit_to_features(U_FFN, 0)
            unit_to_features(U_FFN + 1, 2)
            ffn_body(0, 0, 0)
            with pe.Fori(0, 4) as j:
                ffn_body(1, j, 1)
                ffn_body(2, j, 0)
            ffn_body(9, 0, 1)
            ffn_out_unit(10, 0, 0, False, True, U_FFN + 32)
            norm_turn(2)

            for i in range(N_HG_IN):
                if i >= 2:
                    pe.wait_ge(hg_ev, 2 * (i - 1) if i < 6 else i + 3)
                (unit_to_features if i < 12 else unit_to_tokens)(U_HG_IN + i, (U_HG_IN + i) % 2)
                if i == 13:
                    for q in range(4):
                        tt, hq = q // 2, q % 2
                        pe.wait_ge(hg_ln, 2 * hq + 2)
                        for h in range(4):
                            last = pe.transpose(bank[:, 2 + q, h * P:(h + 1) * P], log_f[:, 4 * hq + h, tt * P:(tt + 1) * P], ident[:])
                        last.then_inc(hg_t, 1)
            pe.wait_ge(hg_l, 4)
            for q in range(4):
                tt, hq = q // 2, q % 2
                for h in range(4):
                    t = slice(tt * P, (tt + 1) * P)
                    last = pe.matmul(bank[:, 2 + q, h * P:(h + 1) * P], key_t[:, 4 * hq + h, t], qry_t[:, 4 * hq + h, t], start=True, stop=True)
                last.then_inc(hd, 1)

            def spans(g):
                p, hp, tt = g // 8, (g // 2) % 4, g % 2
                if g >= 3:
                    pe.wait_ge(sp_e, g - 2)
                b = (0, 1, 6)[g % 3]
                mm = span[:, p if p < 3 else 3 + tt, :, :]
                for a in range(2):
                    f = slice((2 * hp + a) * P, (2 * hp + a + 1) * P)
                    pe.matmul(bank[:, b, a * T:(a + 1) * T], lf_h[:, tt, f], mm, start=True, stop=False)
                    last = pe.matmul(bank[:, b, a * T:(a + 1) * T], lf_l[:, tt, f], mm, start=False, stop=True)
                last.then_inc(sp_d, 1)

            def scores(g):
                p, hp, tt = g // 8, (g // 2) % 4, g % 2
                pe.wait_ge(sp_m, g + 1)
                if g >= 4:
                    pe.wait_ge(sp_c0, g - 3)
                    pe.wait_ge(sp_c1, second(g - 4))
                else:
                    pe.wait_ge(hd_cp, g % 4 + 1)
                b = 2 + g % 4
                for a in range(2):
                    for li in range(2):
                        o = bank[:, b, (2 * a + li) * P:(2 * a + li + 1) * P]
                        v = slice((2 * a + li) * P, (2 * a + li + 1) * P)
                        if 2 * p + li < 7:
                            last = pe.matmul(o, dk[:, g % 2, v], dq[:, g % 2, v], start=True, stop=True)
                        elif tt == 1:
                            last = pe.matmul(o, dk[:, 1 - g % 2, v], dq[:, g % 2, v], start=True, stop=True)
                last.then_inc(sp_s, 1)

            pe.wait_ge(const, n_const["all"])
            pe.wait_ge(hg_ev, 20)
            spans(0)
            spans(1)
            for g in range(GROUPS):
                if g + 2 < GROUPS:
                    spans(g + 2)
                scores(g)
            pe.wait_ge(sp_c0, GROUPS)
            pe.wait_ge(sp_c1, second(GROUPS - 1))
            for j in range(4):
                for h in (2 * j, 2 * j + 1):
                    o = (h % 2) * T
                    pe.matmul(bank[:, 2 + j, o:o + T], val_n[:, 0, h * P:(h + 1) * P], att[:, h, 0:2, :], start=True, stop=False,
                              skip_group_check=True)
                    last = pe.matmul(bank[:, 2 + j, o + P:o + T], val_n[:, 1, h * P:(h + 1) * P], att[:, h, 2, :], start=False, stop=True,
                                     skip_group_check=True)
                last.then_inc(o_o, 1)
            for j in range(4):
                pe.wait_ge(o_sq, j + 1)
                pe.matmul(bank[:, (0, 1, 6, 7)[j], :], mean_all[:], decay[:, j % 2, :], start=True, stop=True).then_inc(o_ms, 1)
            for i in range(N_OUT):
                pe.wait_ge(o_l, i + 1)
                if i == 0:
                    pe.wait_ge(o_n, 4)
                unit_out(U_HG_OUT + i, *from_h(i), i == 0, i == N_OUT - 1)
            norm_turn(3)

            pe.wait_ge(r_low, 1)
            for tt in range(TT):
                t = slice(tt * P, (tt + 1) * P)
                for c in range(KC):
                    three(bank[:, 4, tt * NE:(tt + 1) * NE], h_h[:, c, t], h_l[:, c, t], router_h[:, c, :], router_l[:, c, :], c == 0, False)
                    last = pe.matmul(bank[:, 4, tt * NE:(tt + 1) * NE], h_l[:, c, t], router_l[:, c, :], start=False, stop=c == KC - 1,
                                     skip_group_check=True)
            last.then_inc(r_lg, 1)
            pe.wait_ge(r_d, n_const["sel"])
            s0, s1 = logit[:, 6, 0, :], logit[:, 6, 1, :]
            pe.matmul(bank[:, 5, 0:NE], before[:], s0, start=True, stop=True)
            pe.matmul(bank[:, 5, NE:2 * NE], ones[:], s0, start=True, stop=False)
            pe.matmul(bank[:, 5, NE:2 * NE], before[:], s1, start=False, stop=True)
            pe.matmul(bank[:, 5, 2 * NE:3 * NE], ones[:], s0, start=True, stop=False)
            pe.matmul(bank[:, 5, 2 * NE:3 * NE], ones[:], s1, start=False, stop=True).then_inc(r_rank, 1)

            def gather(n):
                pe.wait_ge(m_sel, n * 2 + 2)
                for j in range(2):
                    for c in range(4):
                        f = slice((4 * j + c) * P, (4 * j + c + 1) * P)
                        for tt in range(TT):
                            last = pe.matmul(bank[:, 5 + j, c * P:(c + 1) * P], xn[:, tt, f], sel[:, tt, :], start=tt == 0, stop=tt == 1,
                                             skip_group_check=True)
                    last.then_inc(m_gat, 1)

            def moe_in(u0, b, half, rounds):
                wait_split(pe, u0, rounds)
                wh, wl = as_in(w_h, u0 % S), as_in(w_l, u0 % S)
                for c in range(KC):
                    last = three(bank[:, b, half * UC:(half + 1) * UC], hs_h[:, c, :], hs_l[:, c, :], wh[:, c, :], wl[:, c, :],
                                 c == 0, c == KC - 1)
                last.then_inc(w_used, 1)

            def moe_turn(g):
                pe.wait_ge(m_mul, g + 1)
                for c in range(2):
                    last = pe.transpose(bank[:, 2, c * P:(c + 1) * P], m_act[:, c * P:(c + 1) * P], ident[:])
                last.then_inc(m_t, 1)

            def moe_out(u0, g, first, last_unit, rounds):
                pe.wait_ge(m_al, g + 1)
                wait_split(pe, u0, rounds)
                wh, wl = as_out(w_h, u0 % S), as_out(w_l, u0 % S)
                for c in range(OC):
                    for half in range(2):
                        v = slice(half * 512, (half + 1) * 512)
                        last = three(bank[:, 3 + half, :], ma_h[:, c * P:(c + 1) * P], ma_l[:, c * P:(c + 1) * P], wh[:, c, v], wl[:, c, v],
                                     first and c == 0, last_unit and c == OC - 1)
                last.then_inc(w_used, 1)

            def moe_round(r):
                u = U_MOE + r * NE * MOE_UNITS
                g0 = r * NE * MOE_STEPS
                n0 = r * (NE + 1)
                gather(n0)
                with pe.Fori(0, NE) as e:
                    q = e * 7
                    g = e * MOE_STEPS + g0
                    pe.wait_ge(m_hl, e * 2 + (2 * n0 + 2))
                    pe.wait_ge(m_add, e * 4 + (r * NE * 4 + 1))
                    moe_in(u, 0, 0, q)
                    moe_in(u + 1, 0, 1, q)
                    for tt in range(TT):
                        pe.transpose(bank[:, 7, tt * P:(tt + 1) * P], sel[:, tt, :], ident[:])
                    pe.matmul(bank[:, 7, T:T + 1], sel[:, 0, :], comb_e[:, 0:1], start=True, stop=False, skip_group_check=True)
                    pe.matmul(bank[:, 7, T:T + 1], sel[:, 1, :], comb_e[:, 1:2], start=False, stop=True,
                              skip_group_check=True).then_inc(m_pt, 1)
                    moe_in(u + 2, 1, 0, q)
                    moe_turn(g)
                    moe_in(u + 3, 1, 1, q)
                    moe_out(u + 4, g, True, False, q)
                    with pe.Fori(0, 6) as j:
                        for k in (0, 1):
                            gs = g + j * 2 + (1 + k)
                            pe.wait_ge(m_mul, gs)
                            moe_in(u + 5 + 3 * k, k, 0, q + j)
                            moe_turn(gs)
                            moe_in(u + 6 + 3 * k, k, 1, q + j)
                            moe_out(u + 7 + 3 * k, gs, False, False, q + j)
                    moe_turn(g + 13)
                    moe_out(u + 41, g + 13, False, True, q)
                    gather(e + (n0 + 1))
                    pe.wait_ge(m_comb, e + (r * NE + 1))
                    pe.wait_ge(m_yl, e * 2 + (r * NE * 2 + 2))
                    for i in range(4):
                        tt, v = i // 2, slice((i % 2) * 512, (i % 2 + 1) * 512)
                        b = (0, 1, 2, 7)[i]
                        pe.matmul(bank[:, b, :], scat[:, tt * P:(tt + 1) * P], y_h[:, v], start=True, stop=False, skip_group_check=True)
                        pe.matmul(bank[:, b, :], scat[:, tt * P:(tt + 1) * P], y_l[:, v], start=False, stop=True,
                                  skip_group_check=True).then_inc(m_sc, 1)

            pe.wait_ge(h3, 2)
            moe_round(0)
            pe.wait_ge(r_flag, 1)
            over = pe.value_load(flag[0:1, 0:1], min_val=0, max_val=1)
            with pe.If(over > 0):
                moe_round(1)


_INS = ['x', 'mix_norm', 'ffn_norm', 'ab_w_in', 'ab_w_out', 'da_q_gain', 'da_k_gain', 'da_lambda', 'da_subln',
        'conv_dw', 'conv_dw_bias', 'conv_gn_gain', 'conv_gn_bias', 'hgrn_w_in', 'hgrn_lb_logits', 'hgrn_norm',
        'hgrn_w_out', 'ffn_w_in', 'ffn_w_out', 'moe_router', 'moe_w_in', 'moe_w_out']


def kernel(**inputs):
    import numpy as np
    import concourse.bacc as bacc
    from concourse.bass_utils import run_bass_kernel_spmd

    nc = bacc.Bacc("TRN2", target_bir_lowering=False, num_devices=1)
    arrays, args = {}, {}
    for name in _INS:
        a = np.ascontiguousarray(inputs[name])
        arrays[f"in_{name}"] = a
        args[name] = nc.dram_tensor(f"in_{name}", a.shape, mybir.dt.from_np(a.dtype), kind="ExternalInput").ap()
    out = nc.dram_tensor("out", (1, T, D), F32, kind="ExternalOutput").ap()
    build(nc, args, out)
    return run_bass_kernel_spmd(nc, [arrays], core_ids=[0]).results[0]["out"]
```

```python
import math
from contextlib import ExitStack

import concourse.bass as bass
from concourse import mybir

ALU = mybir.AluOpType
ACT = mybir.ActivationFunctionType
AX = mybir.AxisListType
F32 = mybir.dt.float32
F32R = mybir.dt.float32r
BF16 = mybir.dt.bfloat16
I8 = mybir.dt.int8
I32 = mybir.dt.int32

P = 128
T = 256
TT = T // P
D = 1024
KC = D // P
UC = 256
UNIT = KC * UC
OC = UNIT // D
R = 6
S = 3
POOL_FROM, POOL_TO = 3, 13
EPS = 1e-6
HEADS = 4
HD = 64
TAPS = 31
HH = 8
NE = 8
CAP = 128
LAM_INIT = 0.8 - 0.6 * math.exp(-0.3 * 0)
NEG = -1.0e30

U_AB_IN, N_AB_IN = 0, 10
U_AB_OUT, N_OUT = 10, 4
U_FFN = 14
FFN_STEPS = 11
U_HG_IN, N_HG_IN = U_FFN + 3 * FFN_STEPS, 16
U_HG_OUT = U_HG_IN + N_HG_IN
U_MOE = U_HG_OUT + N_OUT
MOE_STEPS = 14
MOE_UNITS = 3 * MOE_STEPS
AB_ORDER = [1536, 2048, 1792, 2304, 0, 256, 512, 768, 1024, 1280]
HG_ORDER = [1024 + 256 * i for i in range(4)] + [256 * i for i in range(4)] \
    + [3072 + 256 * i for i in range(4)] + [2048 + 256 * i for i in range(4)]

C_MIX, C_FFN, C_HN, C_LB, C_DWB, C_GG, C_GB, C_SUB, C_QG, C_KG = 0, 16, 32, 40, 48, 52, 56, 60, 61, 62
N_PAR = 63
LEVELS = [1, 2, 4, 8, 16, 32, 64]
PAIRS = 4
GROUPS = PAIRS * (HH // 2) * TT


def build(nc, A, out):
    with ExitStack() as ctx:
        def sb(name, shape, dt=F32):
            return ctx.enter_context(nc.sbuf_tensor(name, shape, dt))

        def sem(name):
            return ctx.enter_context(nc.semaphore(name))

        bank = ctx.enter_context(nc.psum_tensor("bank", [P, 8, 512], F32))

        raw = sb("raw", [P, R, UNIT])
        w_h = sb("w_h", [P, S, UNIT], F32R)
        w_l = sb("w_l", [P, S, UNIT], F32R)
        x = sb("x", [P, TT, D])
        xn = sb("xn", [P, TT, D])
        h_h = sb("h_h", [P, KC, T], F32R)
        h_l = sb("h_l", [P, KC, T], F32R)
        ident = sb("ident", [P, P])
        ones = sb("ones", [P, P])
        mean_all = sb("mean_all", [P, P])
        mean_64 = sb("mean_64", [P, P])
        before = sb("before", [P, P])
        slot_no = sb("slot_no", [P, 2, P])
        expert_no = sb("expert_no", [P, NE])
        par = sb("par", [P, P])
        dw = sb("dw", [P, P])
        eps = sb("eps", [P, 1])
        n_stat = sb("n_stat", [P, 4, 3, TT])
        router = sb("router", [P, KC, NE])
        router_h = sb("router_h", [P, KC, NE], F32R)
        router_l = sb("router_l", [P, KC, NE], F32R)
        flag = sb("flag", [P, 1], I32)
        warm = sb("warm", [P, 16])
        ident_h = sb("ident_h", [P, P], BF16)
        span = sb("span", [P, 5, 2, P], F32R)
        lmask = sb("lmask", [P, 7, P], I8)

        def phase(items):
            made = []
            with ExitStack() as inner:
                for n, shape, dt in items:
                    made.append(inner.enter_context(nc.sbuf_tensor(n, shape, dt)))
            return made

        (par_rows, dw_rows, lam_rows, lam_prod, lam, ident_b, mask_b, conv_in, conv_y, sig, q_raw, sq, rs, q_t, k_t, v_n,
         p_0, p_1, w_t, smx, nmx, ssum, rsum) = phase([
            ("par_rows", [P, P], F32), ("dw_rows", [P, P], F32), ("lam_rows", [P, 4, HD], F32), ("lam_prod", [P, 2, HD], F32),
            ("lam", [P, 8], F32), ("ident_b", [P, P], BF16), ("mask_b", [P, P], BF16),
            ("conv_in", [P, 4, TAPS - 1 + T], F32), ("conv_y", [P, 4, T], F32),
            ("sig", [P, 512], F32), ("q_raw", [P, 4, 512], F32), ("sq", [P, 2, 512], F32), ("rs", [P, 2, 512], F32),
            ("q_t", [P, HEADS, T], F32), ("k_t", [P, HEADS, T], F32), ("v_n", [P, TT, 512], F32),
            ("p_0", [P, 2, HEADS, P], F32), ("p_1", [P, 2, HEADS, T], F32), ("w_t", [P, HEADS, 384], F32),
            ("smx", [P, 16], F32), ("nmx", [P, 16], F32), ("ssum", [P, 16], F32), ("rsum", [P, 16], F32)])
        silu_g, act_f, act_h, act_l = phase([
            ("silu_g", [P, 512], F32), ("act_f", [P, 512], F32),
            ("act_h", [P, 2, 512], F32R), ("act_l", [P, 2, 512], F32R)])
        key_t, qry_t, val_n, lf_h, lf_l, att, dq, dk, decay, lb = phase([
            ("key_t", [P, HH, T], F32), ("qry_t", [P, HH, T], F32), ("val_n", [P, TT, D], F32),
            ("lf_h", [P, TT, D], F32R), ("lf_l", [P, TT, D], F32R), ("att", [P, HH, 3, P], F32),
            ("dq", [P, 2, 512], F32), ("dk", [P, 2, 512], F32), ("decay", [P, 2, 512], F32), ("lb", [P, 5, HH], F32)])
        (gain_row, x_g, x_b, logit_t, logit, pick, rank, comb, sel, scat, hs_h, hs_l, m_silu, m_act, ma_h, ma_l,
         y_h, y_l) = phase([
            ("gain_row", [P, D], F32), ("x_g", [P, TT, D], F32), ("x_b", [P, 3, TT, D], BF16), ("logit_t", [NE, T], F32),
            ("logit", [P, 12, 2, NE], F32), ("pick", [P, 12, 2], F32),
            ("rank", [P, TT * (NE + 1)], F32),
            ("comb", [P, TT * (NE + 1)], F32),
            ("sel", [P, 2, P], BF16), ("scat", [P, T], F32R),
            ("hs_h", [P, KC, P], F32R), ("hs_l", [P, KC, P], F32R), ("m_silu", [P, UC], F32), ("m_act", [P, UC], F32),
            ("ma_h", [P, 2, UC], F32R), ("ma_l", [P, 2, UC], F32R), ("y_h", [P, D], F32R), ("y_l", [P, D], F32R)])
        gate_t = xn[:].rearrange("p a (b t) -> p (a b) t", t=T)
        def o_sqs(j):
            return key_t[:, 2 * j:2 * j + 2, :].rearrange("p a t -> p (a t)")

        def o_inv(j):
            return qry_t[:, 2 * j:2 * j + 2, :].rearrange("p a t -> p (a t)")

        def o_nrm(j):
            return (dq, dk)[j // 2][:, j % 2, :]

        log_f = att[:, :, 0:2, :].rearrange("p h a t -> p h (a t)")

        w_in = [sem(f"w_in{i}") for i in range(R)]
        w_high, w_used = sem("w_high"), sem("w_used")
        w_low, w_low_pool = sem("w_low"), sem("w_low_pool")
        x_in, par_in, lam_in, rout_in, gain_in = sem("x_in"), sem("par_in"), sem("lam_in"), sem("rout_in"), sem("gain_in")
        par_in_pool = sem("par_in_pool")
        par_z, par_t, par_cp = sem("par_z"), sem("par_t"), sem("par_cp")
        const, dve_const = sem("const"), sem("dve_const")
        n_sq, n_ln, n_rs, n_xn, n_t, n_high, n_low = (sem(f"n_{k}") for k in "sq ln rs xn t high low".split())
        o_part, x_add = sem("o_part"), sem("x_add")
        lam_d, lam_e, sub_g, lb_d = sem("lam_d"), sem("lam_e"), sem("sub_g"), sem("lb_d")
        c_s, c_g, c_y = sem("c_s"), sem("c_g"), sem("c_y")
        qk_raw, qk_sq, qk_ms, qk_ln, qk_rs, q_n, v_cp = (sem(k) for k in "qk_raw qk_sq qk_ms qk_ln qk_rs q_n v_cp".split())
        s_sc, s_mx, s_nm, s_ex, s_rc, s_w = (sem(k) for k in "s_sc s_mx s_nm s_ex s_rc s_w".split())
        a_t, a_wt, a_o, a_sq, a_ms, a_ln, a_rs, a_of, a_h, a_l = (sem(f"a_{k}") for k in "t wt o sq ms ln rs of h l".split())
        g_m, g_c, g_sq, g_v, g_ln, g_rs, g_n, g_s, g_h, g_l = (sem(f"g_{k}") for k in "m c sq v ln rs n s h l".split())
        f_silu, f_mul, f_high, f_low = (sem(f"f_{k}") for k in "silu mul high low".split())
        hg_ev, hg_d, hg_ln, hg_t, hg_h, hg_l, hg_gg, hg_z = (sem(f"hg_{k}") for k in "ev d ln t h l gg z".split())
        hd, hd_cp, sp_d, sp_e, sp_m, sp_s, sp_c0, sp_c1 = (sem(k) for k in "hd hd_cp sp_d sp_e sp_m sp_s sp_c0 sp_c1".split())
        o_o, o_sq, o_ms, o_ln, o_rs, o_n, o_g, o_h, o_l = (sem(f"o_{k}") for k in "o sq ms ln rs n g h l".split())
        r_high, r_low, r_lt, r_lc, r_lg, r_d, r_e, r_rank, r_flag = (sem(f"r_{k}") for k in "high low lt lc lg d e rank flag".split())
        x_gain, x_part = sem("x_gain"), sem("x_part")
        m_sel, m_gat, m_pt, m_scat, m_hh, m_hl = (sem(f"m_{k}") for k in "sel gat pt scat hh hl".split())
        m_si, m_mul, m_t, m_ah, m_al, m_yh, m_yl, m_sc, m_add = (sem(f"m_{k}") for k in "si mul t ah al yh yl sc add".split())
        stored = sem("stored")
        n_const = {}

        def in_cols(w):
            return w.rearrange("(c p) f -> p c f", p=P)

        def out_rows(w):
            return w.rearrange("(s c p) d -> s p c d", p=P, c=OC)

        ab_in, ab_out = in_cols(A["ab_w_in"][0]), out_rows(A["ab_w_out"][0])
        ffn_in, ffn_out = in_cols(A["ffn_w_in"][0]), out_rows(A["ffn_w_out"][0])
        hg_in, hg_out = in_cols(A["hgrn_w_in"][0]), out_rows(A["hgrn_w_out"][0])
        FFN_UP = FFN_STEPS * UC
        MOE_UP = MOE_STEPS * UC

        def as_in(t, slot):
            return t[:, slot, :].rearrange("p (c f) -> p c f", c=KC)

        def as_out(t, slot):
            return t[:, slot, :].rearrange("p (c d) -> p c d", c=OC)

        def second(g):
            return g + 1 - len([n for n in range(g + 1) if n >= GROUPS - 8 and n % 2 == 0])

        def wait_split(eng, u0, rounds=0):
            if POOL_FROM <= u0 < POOL_TO:
                eng.wait_ge(w_low_pool, u0 - POOL_FROM + 1)
            elif u0 < POOL_FROM:
                eng.wait_ge(w_low, u0 + 1)
            else:
                eng.wait_ge(w_low, u0 + 1 - (POOL_TO - POOL_FROM) + R * rounds)

        def load(sp, u0, view, src, rounds=0):
            if u0 >= R:
                wait_split(sp, u0 - R, rounds)
            sp.dma_start(view(raw, u0 % R), src).then_inc(w_in[u0 % R], 16)

        def split_high(act, u0, rounds=0):
            act.wait_ge(w_in[u0 % R], 16 * (u0 // R + 1) + 16 * rounds)
            if u0 >= S:
                act.wait_ge(w_used, u0 - S + 1 + R * rounds)
            act.activation(w_h[:, u0 % S, :], raw[:, u0 % R, :], ACT.Copy).then_inc(w_high, 1)

        def split_low(eng, u0, rounds=0):
            eng.wait_ge(w_high, u0 + 1 + R * rounds)
            eng.tensor_tensor(w_l[:, u0 % S, :], raw[:, u0 % R, :], w_h[:, u0 % S, :],
                              ALU.subtract).then_inc(w_low_pool if POOL_FROM <= u0 < POOL_TO else w_low, 1)

        block = ctx.enter_context(nc.Block())

        def param_rows(eng, done, *rows):
            for src, at in rows:
                v = src.rearrange("l (c p) -> (l c) p", p=P)
                eng.dma_start(par_rows[at:at + v.shape[0], :], v).then_inc(done, 16)

        @block.gpsimd
        def _(pool):
            made = [0]

            def step(ins):
                made[0] += 1
                ins.then_inc(const, 1)
                pool.wait_ge(const, made[0])

            def select(view, pattern, base, cm, op=ALU.is_ge, fill=0.0):
                step(pool.affine_select(out=view, in_=view, compare_op=op, fill=fill, base=base, pattern=pattern,
                                        channel_multiplier=cm))

            step(pool.memset(ident[:], 0.0))
            select(ident[:], [[-1, P]], 0, 1, ALU.not_equal, 1.0)
            step(pool.memset(par_rows[:], 0.0))
            step(pool.memset(dw_rows[:], 0.0))
            n_const["rows"] = made[0]
            with nc.allow_non_contiguous_dma(reason="small parameters, loaded once"):
                param_rows(pool, par_in_pool, (A["conv_dw_bias"], C_DWB), (A["conv_gn_gain"], C_GG), (A["conv_gn_bias"], C_GB))
                pool.dma_start(lam_rows[:], A["da_lambda"].rearrange("o a b -> o (a b)").to_broadcast([P, 4 * HD])).then_inc(lam_in, 16)
                pool.dma_start(router[:], A["moe_router"][0].rearrange("(c p) e -> p c e", p=P)).then_inc(rout_in, 16)
            step(pool.memset(ones[:], 1.0))
            step(pool.memset(mean_all[:], 1.0 / P))
            step(pool.memset(mean_64[:], 1.0 / HD))
            select(mean_64[:, 0:HD], [[0, HD]], HD - 1, -1)
            select(mean_64[:, HD:P], [[0, HD]], -HD, 1)
            step(pool.memset(ident_b[:], 0.0))
            select(ident_b[:], [[-1, P]], 0, 1, ALU.not_equal, 1.0)
            step(pool.memset(mask_b[:], 0.0))
            select(mask_b[:], [[-1, P]], 0, 1, ALU.is_ge, NEG)
            step(pool.memset(ident_h[:], 0.0))
            select(ident_h[:], [[-1, P]], 0, 1, ALU.not_equal, 1.0)
            step(pool.memset(conv_in[:, :, 0:TAPS - 1], 0.0))
            step(pool.memset(before[:], 1.0))
            select(before[:], [[1, P]], -1, -1)
            for r in range(2):
                step(pool.iota(slot_no[:, r, :], pattern=[[1, P]], base=CAP * r, channel_multiplier=0,
                               allow_small_or_imprecise_dtypes=True))
                if CAP < P:
                    step(pool.memset(slot_no[:, r, CAP:P], -5.0))
            step(pool.iota(expert_no[:], pattern=[[-1, NE]], base=NE, channel_multiplier=0,
                           allow_small_or_imprecise_dtypes=True))
            n_const["early"] = made[0]
            for u in range(POOL_FROM, POOL_TO):
                split_low(pool, u)
            step(pool.memset(span[:].bitcast(F32), 1.0))
            step(pool.memset(lmask[:], 0))
            for n, h in enumerate(LEVELS):
                nb = P // (2 * h)
                for view in ([span[:, n // 2, n % 2, :]] if n < 6 else [span[:, 3, 0, :], span[:, 4, 0, :]]):
                    v = view.rearrange("p (b s r) -> p b s r", s=2, r=h)
                    select(v[:, :, 1, :], [[-2 * h, nb], [0, h]], -h, 1)
                    select(v[:, :, 1, :], [[2 * h, nb], [1, h]], h, -1)
                    select(v[:, :, 0, :], [[-2 * h, nb], [-1, h]], -1, 1)
                    select(v[:, :, 0, :], [[2 * h, nb], [0, h]], h - 1, -1)
                v = lmask[:, n, :].rearrange("p (b s r) -> p b s r", s=2, r=h)
                step(pool.memset(v[:, :, 1, :], 1))
                select(v[:, :, 1, :], [[-2 * h, nb], [0, h]], 0, 1)
                select(v[:, :, 1, :], [[2 * h, nb], [0, h]], h - 1, -1)
            select(span[:, 3, 1, :], [[-1, P]], -1, 1)
            select(span[:, 4, 1, :], [[1, P]], 0, -1)
            n_const["all"] = made[0]

            pool.wait_ge(hg_ev, 16)
            for h in range(HH):
                pool.tensor_scalar(gate_t[:, h, :], gate_t[:, h, :], par[:, C_HN + h:C_HN + h + 1], None,
                                   ALU.mult).then_inc(hg_gg, 1)
            pool.wait_ge(gain_in, 16)
            for tt in range(TT):
                pool.wait_ge(n_xn, 2 * 3 + tt + 1)
                pool.tensor_tensor(x_g[:, tt, :], xn[:, tt, :], gain_row[:], ALU.mult).then_inc(x_gain, 1)
            for part in range(2):
                for tt in range(TT):
                    pool.wait_ge(x_part, 2 * part + tt + 1)
                    dst = x_g[:, tt, :] if part == 0 else x_b[:, 2, tt, :]
                    pool.tensor_tensor(dst, x_g[:, tt, :], x_b[:, part, tt, :], ALU.subtract).then_inc(x_gain, 1)

        @block.sync
        def _(sp):
            for tt in range(TT):
                sp.dma_start(x[:, tt, :], A["x"][0, tt * P:(tt + 1) * P, :]).then_inc(x_in, 16)
            sp.wait_ge(const, n_const["rows"])
            with nc.allow_non_contiguous_dma(reason="small parameters, loaded once"):
                sp.dma_start(dw_rows[0:TAPS * 4, :], A["conv_dw"].rearrange("o k (c p) -> (o k c) p", p=P)).then_inc(par_in, 16)
                param_rows(sp, par_in, (A["ffn_norm"], C_FFN), (A["hgrn_norm"], C_HN), (A["hgrn_lb_logits"], C_LB))
            for i in range(N_AB_IN):
                load(sp, U_AB_IN + i, as_in, ab_in[:, :, AB_ORDER[i]:AB_ORDER[i] + UC])
            for i in range(N_OUT):
                load(sp, U_AB_OUT + i, as_out, ab_out[i])

            def ffn_ab(u0, step, rounds=0):
                load(sp, u0, as_in, ffn_in[:, :, bass.ds(step * UC, UC)], rounds)
                load(sp, u0 + 1, as_in, ffn_in[:, :, bass.ds(step * UC + FFN_UP, UC)], rounds)

            ffn_ab(U_FFN, 0)
            ffn_ab(U_FFN + 2, 1)
            load(sp, U_FFN + 4, as_out, ffn_out[0])
            with sp.Fori(0, 4) as j:
                for k in (0, 1):
                    u0 = U_FFN + 5 + 3 * k
                    ffn_ab(u0, j * 2 + (2 + k), j)
                    load(sp, u0 + 2, as_out, ffn_out[j * 2 + (1 + k)], j)
            ffn_ab(U_FFN + 29, 10)
            load(sp, U_FFN + 31, as_out, ffn_out[9])
            load(sp, U_FFN + 32, as_out, ffn_out[10])
            for i in range(N_HG_IN):
                load(sp, U_HG_IN + i, as_in, hg_in[:, :, HG_ORDER[i]:HG_ORDER[i] + UC])
            for i in range(N_OUT):
                load(sp, U_HG_OUT + i, as_out, hg_out[i])

            w1, w2 = A["moe_w_in"][0], A["moe_w_out"][0]

            def moe_a(u0, e, step, rounds):
                load(sp, u0, as_in, in_cols(w1[e])[:, :, bass.ds(step * UC, UC)], rounds)

            def moe_b(u0, e, step, rounds):
                load(sp, u0, as_in, in_cols(w1[e])[:, :, bass.ds(step * UC + MOE_UP, UC)], rounds)

            def moe_c(u0, e, step, rounds):
                load(sp, u0, as_out, out_rows(w2[e])[step], rounds)

            def expert(u, e, nxt, rounds):
                moe_b(u + 3, e, 1, rounds)
                moe_c(u + 4, e, 0, rounds)
                with sp.Fori(0, 6) as j:
                    for k in (0, 1):
                        moe_a(u + 5 + 3 * k, e, j * 2 + (2 + k), rounds + j)
                        moe_b(u + 6 + 3 * k, e, j * 2 + (2 + k), rounds + j)
                        moe_c(u + 7 + 3 * k, e, j * 2 + (1 + k), rounds + j)
                moe_c(u + 41, e, 13, rounds)
                moe_a(u + 42, nxt, 0, rounds)
                moe_b(u + 43, nxt, 0, rounds)
                moe_a(u + 44, nxt, 1, rounds)

            def moe_round(r):
                u = U_MOE + r * NE * MOE_UNITS
                with sp.Fori(0, NE - 1) as e:
                    expert(u, e, e + 1, e * 7)
                expert(u, NE - 1, 0, 7 * (NE - 1))

            moe_a(U_MOE, 0, 0, 0)
            moe_b(U_MOE + 1, 0, 0, 0)
            moe_a(U_MOE + 2, 0, 1, 0)
            moe_round(0)
            sp.wait_ge(r_flag, 1)
            over = sp.value_load(flag[0:1, 0:1], min_val=0, max_val=1)
            with sp.If(over > 0):
                moe_round(1)
                sp.wait_ge(m_add, 8 * (NE + 1) + 1)
            sp.wait_ge(m_add, 4 * (NE + 1) + 1)
            for tt in range(TT):
                sp.dma_start(out[0, tt * P:(tt + 1) * P, :], x[:, tt, :]).then_inc(stored, 16)
            sp.wait_ge(stored, 16 * TT)

        @block.vector
        def _(dve):
            dve.memset(eps[:], EPS).then_inc(dve_const, 1)
            dve.wait_ge(par_t, 1)
            dve.tensor_copy(par[:], bank[:, 0, 0:P]).then_inc(par_cp, 1)
            dve.wait_ge(par_t, 2)
            dve.tensor_copy(dw[:], bank[:, 1, 0:P]).then_inc(par_cp, 1)
            dve.wait_ge(par_cp, 2)
            dve.tensor_scalar(par[:, C_SUB:C_SUB + 1], par[:, C_SUB:C_SUB + 1], 1.0 - LAM_INIT, None, ALU.mult).then_inc(sub_g, 1)
            dve.wait_ge(lam_in, 16)
            for i in range(2):
                dve.tensor_tensor(lam_prod[:, i, :], lam_rows[:, 2 * i, :], lam_rows[:, 2 * i + 1, :], ALU.mult).then_inc(lam_d, 1)
            dve.wait_ge(lam_d, 2)
            dve.tensor_reduce(lam[:, 0:2], lam_prod[:], AX.X, ALU.add).then_inc(lam_d, 1)

            def norm_scale(n):
                dve.wait_ge(n_rs, n + 1)
                for tt in range(TT):
                    dve.tensor_scalar(xn[:, tt, :], x[:, tt, :], n_stat[:, n, 2, tt:tt + 1], None, ALU.mult).then_inc(n_xn, 1)

            def norm_low(n, col):
                for j in range(4):
                    dve.wait_ge(n_high, 8 * n + 2 * j + 2)
                    b = (2 + j) if n == 0 else j
                    for c in range(2):
                        dve.scalar_tensor_tensor(out=h_l[:, 2 * j + c, :], in0=bank[:, b, c * T:(c + 1) * T],
                                                 scalar=par[:, col + 2 * j + c:col + 2 * j + c + 1], in1=h_h[:, 2 * j + c, :],
                                                 op0=ALU.mult, op1=ALU.subtract).then_inc(n_low, 1)

            def residual(units):
                for tt in range(TT):
                    if tt == 0:
                        dve.wait_ge(o_part, {U_FFN: 1, U_HG_IN: 2, U_MOE: 3}[units])
                    else:
                        dve.wait_ge(w_used, units)
                    for half in range(2):
                        v = x[:, tt, half * 512:(half + 1) * 512]
                        dve.tensor_tensor(v, bank[:, 4 + 2 * tt + half, :], v, ALU.add).then_inc(x_add, 1)

            norm_scale(0)
            split_low(dve, 0)
            norm_low(0, C_MIX)
            split_low(dve, 1)
            split_low(dve, 2)
            def conv_value(i):
                dve.wait_ge(c_s, i + 1)
                dve.tensor_tensor(conv_in[:, 2 * i:2 * i + 2, TAPS - 1:], bank[:, 0, :].rearrange("p (a t) -> p a t", a=2),
                                  sig[:].rearrange("p (a t) -> p a t", a=2), ALU.mult).then_inc(c_g, 1)

            def conv_taps(i, first, end):
                if first == 0:
                    dve.wait_ge(c_g, i + 1)
                    for c in (2 * i, 2 * i + 1):
                        dve.tensor_scalar(conv_y[:, c, :], conv_in[:, c, 0:T], dw[:, c:c + 1], par[:, C_DWB + c:C_DWB + c + 1],
                                          ALU.mult, ALU.add).then_inc(c_y, 1)
                    first = 1
                with dve.Fori(first, end) as k:
                    for c in (0, 1):
                        ch = 2 * i + c
                        dve.wait_ge(c_y, k * 2 + (2 * TAPS * i + c - 1))
                        dve.scalar_tensor_tensor(out=conv_y[:, ch, :], in0=conv_in[:, ch, bass.ds(k, T)],
                                                 scalar=dw[:, bass.ds(k * 4 + ch, 1)], in1=conv_y[:, ch, :],
                                                 op0=ALU.mult, op1=ALU.add).then_inc(c_y, 1)

            def qk_norm(i):
                dst, col = (q_t, C_QG) if i < 2 else (k_t, C_KG)
                dve.wait_ge(qk_rs, i + 1)
                dve.scalar_tensor_tensor(out=dst[:, 2 * (i % 2):2 * (i % 2) + 2, :],
                                         in0=q_raw[:, i, :].rearrange("p (a t) -> p a t", a=2), scalar=par[:, col:col + 1],
                                         in1=rs[:, i % 2, :].rearrange("p (a t) -> p a t", a=2),
                                         op0=ALU.mult, op1=ALU.mult).then_inc(q_n, 1)

            dve.wait_ge(const, n_const["early"])
            conv_value(0)
            conv_taps(0, 0, 10)
            conv_value(1)
            conv_taps(0, 10, 29)
            qk_norm(0)
            qk_norm(1)
            conv_taps(0, 29, TAPS)
            conv_taps(1, 0, 8)
            qk_norm(2)
            qk_norm(3)
            dve.wait_ge(lam_e, 1)
            dve.tensor_tensor(lam[:, 4:5], lam[:, 3:4], lam[:, 2:3], ALU.subtract).then_inc(lam_d, 1)
            dve.wait_ge(lam_d, 4)
            dve.tensor_scalar(lam[:, 5:6], lam[:, 4:5], -LAM_INIT, None, ALU.add).then_inc(lam_d, 1)
            for b in range(6):
                n, w, idx = (4, P, 4 * b) if b < 2 else (2, T, 8 + 2 * (b - 2))
                dve.wait_ge(s_sc, b + 1)
                dve.tensor_reduce(smx[:, idx:idx + n], bank[:, 2 + b, 0:n * w].rearrange("p (n w) -> p n w", n=n),
                                  AX.X, ALU.max).then_inc(s_mx, 1)
                dve.wait_ge(s_mx, b + 1)
                dve.tensor_scalar(nmx[:, idx:idx + n], smx[:, idx:idx + n], -HD ** -0.5, None, ALU.mult).then_inc(s_nm, 1)
                conv_taps(1, 8 + 2 * b, 10 + 2 * b)
            conv_taps(1, 20, TAPS)
            for qt, pr in enumerate((p_0, p_1)):
                dve.wait_ge(s_ex, 8 * qt + 8)
                dve.reciprocal(rsum[:, 8 * qt:8 * qt + 8], ssum[:, 8 * qt:8 * qt + 8]).then_inc(s_rc, 1)
                dve.wait_ge(s_rc, 2 * qt + 1)
                dve.wait_ge(lam_d, 5)
                dve.tensor_scalar(rsum[:, 8 * qt + 4:8 * qt + 8], rsum[:, 8 * qt + 4:8 * qt + 8], lam[:, 5:6], None, ALU.mult).then_inc(s_rc, 1)
                for h in range(HEADS):
                    dve.tensor_scalar(pr[:, 0, h, :], pr[:, 0, h, :], rsum[:, 8 * qt + h:8 * qt + h + 1], None, ALU.mult).then_inc(s_w, 1)
                dve.wait_ge(s_rc, 2 * qt + 2)
                for h in range(HEADS):
                    dve.wait_ge(s_w, 8 * qt + h + 1)
                    dve.scalar_tensor_tensor(out=pr[:, 0, h, :], in0=pr[:, 1, h, :], scalar=rsum[:, 8 * qt + 4 + h:8 * qt + 5 + h],
                                             in1=pr[:, 0, h, :], op0=ALU.mult, op1=ALU.add).then_inc(s_w, 1)
            dve.wait_ge(sub_g, 1)
            for b in range(2):
                dve.wait_ge(g_m, b + 1)
                v = conv_y[:, 2 * b:2 * b + 2, :]
                dve.tensor_tensor(v, v, bank[:, 2 + b, :].rearrange("p (a t) -> p a t", a=2), ALU.subtract).then_inc(g_c, 1)
            for b in range(2):
                dve.wait_ge(a_rs, b + 1)
                dve.scalar_tensor_tensor(out=q_raw[:, b, :], in0=bank[:, 6 + b, :], scalar=par[:, C_SUB:C_SUB + 1], in1=rs[:, b, :],
                                         op0=ALU.mult, op1=ALU.mult).then_inc(a_of, 1)
            for b in range(2):
                dve.wait_ge(a_h, b + 1)
                dve.tensor_tensor(h_l[:, 2 * b:2 * b + 2, :], q_raw[:, b, :].rearrange("p (a t) -> p a t", a=2),
                                  h_h[:, 2 * b:2 * b + 2, :], ALU.subtract).then_inc(a_l, 1)
            for b in range(2):
                dve.wait_ge(g_rs, b + 1)
                v = conv_y[:, 2 * b:2 * b + 2, :]
                dve.tensor_tensor(v, v, rs[:, b, :].rearrange("p (a t) -> p a t", a=2), ALU.mult).then_inc(g_n, 1)
            for b in range(2):
                dve.wait_ge(g_h, b + 1)
                dve.tensor_tensor(h_l[:, 4 + 2 * b:6 + 2 * b, :], conv_y[:, 2 * b:2 * b + 2, :], h_h[:, 4 + 2 * b:6 + 2 * b, :],
                                  ALU.subtract).then_inc(g_l, 1)
            dve.wait_ge(r_high, 1)
            dve.tensor_tensor(router_l[:], router[:], router_h[:], ALU.subtract).then_inc(r_low, 1)
            for u in range(U_AB_OUT, U_FFN):
                split_low(dve, u + 3)
            residual(U_FFN)

            norm_scale(1)
            norm_low(1, C_FFN)

            def ffn_mul(s0, j2, par_s, used):
                dve.wait_ge(w_used, used)
                dve.wait_ge(f_silu, j2 + (s0 + 1))
                if s0:
                    dve.wait_ge(f_low, j2 + s0)
                dve.tensor_tensor(act_f[:], silu_g[:], bank[:, 2 + par_s, :], ALU.mult).then_inc(f_mul, 1)

            def ffn_low(s0, j2, par_s):
                dve.wait_ge(f_high, j2 + (s0 + 1))
                dve.tensor_tensor(act_l[:, par_s, :], act_f[:], act_h[:, par_s, :], ALU.subtract).then_inc(f_low, 1)

            def ffn_step(s0, j, par_s):
                ffn_mul(s0, j * 2, par_s, j * 6 + (U_FFN + (3 * s0 + 1 if s0 else 2)))
                split_low(dve, U_FFN + 3 * s0 + 3, j)
                ffn_low(s0, j * 2, par_s)
                split_low(dve, U_FFN + 3 * s0 + 4, j)
                split_low(dve, U_FFN + 3 * s0 + 5, j)

            ffn_step(0, 0, 0)
            ffn_step(1, 0, 1)
            with dve.Fori(0, 4) as j:
                ffn_step(2, j, 0)
                ffn_step(3, j, 1)
            ffn_step(10, 0, 0)
            residual(U_HG_IN)

            norm_scale(2)
            norm_low(2, C_MIX + 8)
            dve.tensor_tensor(lb[:, 0, :], par[:, C_LB:C_LB + HH], par[:, C_LB:C_LB + HH], ALU.subtract).then_inc(lb_d, 1)
            dve.wait_ge(lb_d, 2)
            dve.reciprocal(lb[:, 2, :], lb[:, 1, :]).then_inc(lb_d, 1)
            dve.wait_ge(lb_d, 3)
            dve.tensor_tensor(lb[:, 3, :], lb[:, 1, :], lb[:, 2, :], ALU.mult).then_inc(lb_d, 1)
            dve.wait_ge(lb_d, 4)
            dve.tensor_tensor(lb[:, 0, :], lb[:, 3, :], lb[:, 3, :], ALU.subtract).then_inc(lb_d, 1)
            dve.wait_ge(lb_d, 5)
            dve.tensor_scalar(lb[:, 4, :], lb[:, 0, :], -1.0, 1.0, ALU.mult, ALU.add).then_inc(lb_d, 1)
            dve.memset(dq[:], 0.0).then_inc(hg_z, 1)
            dve.memset(dk[:], 0.0).then_inc(hg_z, 1)
            dve.wait_ge(lb_d, 6)
            for i in range(N_HG_IN):
                if i < 4:
                    dve.wait_ge(hg_ev, 2 * i + 2)
                    for h in (2 * i, 2 * i + 1):
                        dve.tensor_scalar(log_f[:, h, :], log_f[:, h, :], lb[:, 4, h:h + 1], lb[:, 0, h:h + 1],
                                          ALU.mult, ALU.add).then_inc(hg_z, 1)
                        dve.tensor_scalar(key_t[:, h, :], key_t[:, h, :], lb[:, 4, h:h + 1], None, ALU.mult).then_inc(hg_d, 1)
                    dve.wait_ge(hg_z, 2 * i + 4)
                    dve.tensor_scalar(log_f[:, 2 * i:2 * i + 2, :], log_f[:, 2 * i:2 * i + 2, :], 1.2e-38, None, ALU.max).then_inc(hg_d, 1)
                split_low(dve, U_HG_IN + i + 3)
                if i == 13:
                    for q in range(4):
                        tt, hq = q // 2, q % 2
                        dve.wait_ge(hg_h, q + 1)
                        v = slice(hq * 512, (hq + 1) * 512)
                        dve.tensor_tensor(lf_l[:, tt, v], bank[:, 2 + q, :], lf_h[:, tt, v], ALU.subtract).then_inc(hg_l, 1)
            for q in range(4):
                tt, hq = q // 2, q % 2
                dve.wait_ge(hd, q + 1)
                dve.tensor_tensor(att[:, 4 * hq:4 * hq + 4, 2 * tt, :], bank[:, 2 + q, :].rearrange("p (h t) -> p h t", h=4),
                                  ident[:].unsqueeze(1).to_broadcast([P, 4, P]), ALU.mult).then_inc(hd_cp, 1)

            def decayed(g):
                p, hp, tt = g // 8, (g // 2) % 4, g % 2
                dve.wait_ge(sp_e, g + 1)
                if g >= 2:
                    dve.wait_ge(sp_s, g if (p == 3 and g % 2 == 0 and g >= 26) else g - 1)
                hs = slice(2 * hp, 2 * hp + 2)
                e = decay[:, g % 2, :].rearrange("p (a l t) -> p a l t", a=2, l=2)
                tq = dq[:, g % 2, :].rearrange("p (a l t) -> p a l t", a=2, l=2)
                tk = dk[:, g % 2, :].rearrange("p (a l t) -> p a l t", a=2, l=2)
                q = qry_t[:, hs, tt * P:(tt + 1) * P]
                k = key_t[:, hs, tt * P:(tt + 1) * P]
                for li in range(2):
                    if 2 * p + li < 7:
                        h = LEVELS[2 * p + li]
                        how = "p a (b s r) -> p a b s r"
                        for half, dst, src in ((1, tq, q), (0, tk, k)):
                            ins = dve.tensor_tensor(dst[:, :, li, :].rearrange(how, s=2, r=h)[:, :, :, half, :],
                                                    src.rearrange(how, s=2, r=h)[:, :, :, half, :],
                                                    e[:, :, li, :].rearrange(how, s=2, r=h)[:, :, :, half, :], ALU.mult)
                    elif tt == 0:
                        ins = dve.tensor_tensor(tk[:, :, li, :], k, e[:, :, li, :], ALU.mult)
                    else:
                        ins = dve.tensor_tensor(tq[:, :, li, :], q, e[:, :, li, :], ALU.mult)
                ins.then_inc(sp_m, 1)

            def keep(g, li):
                p, hp, tt = g // 8, (g // 2) % 4, g % 2
                b = bank[:, 2 + g % 4, :].rearrange("p (a l t) -> p a l t", a=2, l=2)[:, :, li, :]
                if li == 0:
                    dve.wait_ge(sp_s, g + 1)
                    if g >= 8:
                        dve.wait_ge(sp_c1, second(g - 8))
                else:
                    dve.wait_ge(sp_c0, g + 1)
                if 2 * p + li < 7:
                    dve.copy_predicated(att[:, 2 * hp:2 * hp + 2, 2 * tt, :],
                                        lmask[:, 2 * p + li, :].unsqueeze(1).to_broadcast([P, 2, P]), b).then_inc((sp_c0, sp_c1)[li], 1)
                elif tt == 1:
                    dve.tensor_copy(att[:, 2 * hp:2 * hp + 2, 1, :], b).then_inc(sp_c1, 1)

            dve.wait_ge(const, n_const["all"])
            dve.wait_ge(hd_cp, 4)
            decayed(0)
            for g in range(GROUPS):
                if g + 1 < GROUPS:
                    decayed(g + 1)
                keep(g, 0)
                if g:
                    keep(g - 1, 1)
            keep(GROUPS - 1, 1)
            dve.wait_ge(hg_gg, HH)

            def hg_low(j):
                dve.wait_ge(o_h, j + 1)
                dve.tensor_tensor(h_l[:, 2 * j:2 * j + 2, :], o_nrm(j).rearrange("p (a t) -> p a t", a=2),
                                  h_h[:, 2 * j:2 * j + 2, :], ALU.subtract).then_inc(o_l, 1)

            for j in range(4):
                dve.wait_ge(o_rs, j + 1)
                dve.tensor_tensor(o_nrm(j), bank[:, 2 + j, :], o_inv(j), ALU.mult).then_inc(o_n, 1)
                dve.wait_ge(o_n, j + 1)
                v = o_nrm(j).rearrange("p (a t) -> p a t", a=2)
                dve.tensor_tensor(v, v, gate_t[:, 2 * j:2 * j + 2, :], ALU.mult).then_inc(o_g, 1)
                if j >= 1:
                    hg_low(j - 1)
            hg_low(3)
            for u in range(U_HG_OUT, U_MOE):
                split_low(dve, u + 3)
            residual(U_MOE)

            norm_scale(3)
            norm_low(3, C_FFN + 8)
            done = [0]

            def step(ins):
                done[0] += 1
                ins.then_inc(r_d, 1)
                dve.wait_ge(r_d, done[0])

            def wide(v):
                return v.unsqueeze(2).to_broadcast([P, TT, NE])

            ordr = expert_no[:].unsqueeze(1).to_broadcast([P, TT, NE])
            dve.wait_ge(r_lt, 1)
            dve.tensor_copy(logit_t[:], bank[0:NE, 4, 0:T]).then_inc(r_lc, 1)
            dve.wait_ge(r_lg, 1)
            step(dve.tensor_copy(logit[:, 0, :, :], bank[:, 5, 0:TT * NE].rearrange("p (a e) -> p a e", a=TT)))
            for k in range(2):
                src, sl = logit[:, 2 * k + 0, :, :] if k == 0 else logit[:, 3, :, :], logit[:, 4 + k, :, :]
                step(dve.tensor_reduce(pick[:, k, :], src, AX.X, ALU.max))
                step(dve.tensor_tensor(logit[:, 1, :, :], src, wide(pick[:, k, :]), ALU.is_ge))
                step(dve.tensor_tensor(logit[:, 2, :, :], logit[:, 1, :, :], ordr, ALU.mult))
                step(dve.tensor_reduce(pick[:, 2 + k, :], logit[:, 2, :, :], AX.X, ALU.max))
                step(dve.tensor_tensor(sl, ordr, wide(pick[:, 2 + k, :]), ALU.is_equal))
                if k == 0:
                    step(dve.scalar_tensor_tensor(out=logit[:, 3, :, :], in0=sl, scalar=-3.0e38, in1=src, op0=ALU.mult, op1=ALU.add))
            step(dve.tensor_tensor(pick[:, 4, :], pick[:, 1, :], pick[:, 0, :], ALU.subtract))
            n_const["exp"] = done[0]
            step(dve.tensor_tensor(logit[:, 6, :, :], logit[:, 4, :, :], logit[:, 5, :, :], ALU.add))
            n_const["sel"] = done[0]
            dve.wait_ge(r_e, 1)
            step(dve.tensor_scalar(pick[:, 6, :], pick[:, 5, :], 1.0, None, ALU.add))
            step(dve.reciprocal(pick[:, 7, :], pick[:, 6, :]))
            step(dve.tensor_tensor(pick[:, 8, :], pick[:, 5, :], pick[:, 7, :], ALU.mult))
            step(dve.tensor_tensor(logit[:, 7, :, :], logit[:, 4, :, :], wide(pick[:, 7, :]), ALU.mult))
            step(dve.tensor_tensor(logit[:, 8, :, :], logit[:, 5, :, :], wide(pick[:, 8, :]), ALU.mult))
            step(dve.memset(comb[:], 0.0))
            step(dve.memset(rank[:], -1.0))
            step(dve.tensor_tensor(comb[:].rearrange("p (a e) -> p a e", a=TT)[:, :, 1:], logit[:, 7, :, :], logit[:, 8, :, :], ALU.add))
            dve.wait_ge(r_rank, 1)
            step(dve.scalar_tensor_tensor(out=logit[:, 9, :, :], in0=bank[:, 6, 0:TT * NE].rearrange("p (a e) -> p a e", a=TT), scalar=1.0,
                                          in1=logit[:, 6, :, :], op0=ALU.add, op1=ALU.mult))
            step(dve.tensor_scalar(rank[:].rearrange("p (a e) -> p a e", a=TT)[:, :, 0:NE], logit[:, 9, :, :], -1.0, None, ALU.add))
            step(dve.tensor_reduce(pick[:, 9, 0:1], bank[:, 6, TT * NE:(TT + 1) * NE], AX.X, ALU.max))
            step(dve.tensor_scalar(pick[:, 10, 0:1], pick[:, 9, 0:1], CAP + 0.5, None, ALU.is_gt))
            dve.tensor_copy(flag[:], pick[:, 10, 0:1]).then_inc(r_flag, 1)
            dve.memset(pick[:, 11, :], 0.0).then_inc(m_add, 1)

            def choose(e, r, n):
                for tt in range(TT):
                    dve.tensor_scalar(sel[:, tt, :], slot_no[:, r, :], rank[:, bass.ds(e + tt * (NE + 1), 1)], None,
                                      ALU.is_equal).then_inc(m_sel, 1)

            def residual_part(e, tt, n):
                for half in range(2):
                    dve.wait_ge(m_sc, n * 4 + (2 * tt + half + 1))
                    v = x[:, tt, half * 512:(half + 1) * 512]
                    dve.scalar_tensor_tensor(out=v, in0=bank[:, 5 + half, :], scalar=comb[:, bass.ds(e + tt * (NE + 1), 1)], in1=v,
                                             op0=ALU.mult, op1=ALU.add).then_inc(m_add, 1)

            def gather_low(n):
                for j in range(2):
                    dve.wait_ge(m_hh, n * 2 + (j + 1))
                    dve.tensor_tensor(hs_l[:, 4 * j:4 * j + 4, :], bank[:, 5 + j, :].rearrange("p (c t) -> p c t", c=4),
                                      hs_h[:, 4 * j:4 * j + 4, :], ALU.subtract).then_inc(m_hl, 1)

            def moe_mul(g, b):
                dve.wait_ge(m_si, g + 1)
                dve.tensor_tensor(m_act[:], m_silu[:], bank[:, b, UC:2 * UC], ALU.mult).then_inc(m_mul, 1)

            def moe_low(g, b):
                dve.wait_ge(m_ah, g + 1)
                dve.tensor_tensor(ma_l[:, b, :], bank[:, 2, 0:UC], ma_h[:, b, :], ALU.subtract).then_inc(m_al, 1)

            def moe_step(u, k, gs, rounds, last=False):
                moe_mul(gs, (1 + k) % 2)
                split_low(dve, u + 6 + 3 * k, rounds)
                split_low(dve, u + 7 + 3 * k, rounds)
                moe_low(gs, (1 + k) % 2)
                if last:
                    moe_mul(gs + 1, k % 2)
                split_low(dve, u + 8 + 3 * k, rounds)

            def moe_round(r):
                u = U_MOE + r * NE * MOE_UNITS
                g0 = r * NE * MOE_STEPS
                n0 = r * (NE + 1)
                if r:
                    dve.wait_ge(m_pt, n0)
                choose(0, r, n0)
                dve.memset(scat[:].bitcast(F32), 0.0).then_inc(m_scat, 1)
                dve.memset(y_h[:].bitcast(F32), 0.0).then_inc(m_yl, 1)
                dve.memset(y_l[:].bitcast(F32), 0.0).then_inc(m_yl, 1)
                gather_low(n0)
                with dve.Fori(0, NE) as e:
                    q = e * 7
                    g = e * MOE_STEPS + g0
                    n = e + n0
                    split_low(dve, u + 3, q)
                    moe_mul(g, 0)
                    residual_part(e, 0, n)
                    split_low(dve, u + 4, q)
                    moe_low(g, 0)
                    split_low(dve, u + 5, q)
                    residual_part(e, 1, n)
                    dve.wait_ge(m_pt, e + (n0 + 1))
                    choose(e + 1, r, n + 1)
                    with dve.Fori(0, 5) as j:
                        for k in (0, 1):
                            moe_step(u, k, g + j * 2 + (1 + k), q + j)
                    for k in (0, 1):
                        moe_step(u + 5 * 6, k, g + (11 + k), q, k == 1)
                    gather_low(n + 1)
                    moe_low(g + 13, 1)
                    split_low(dve, u + 42, q)
                    split_low(dve, u + 43, q)
                    for j in range(2):
                        dve.wait_ge(m_yh, e * 2 + (r * NE * 2 + j + 1))
                        dve.tensor_tensor(y_l[:, j * 512:(j + 1) * 512], bank[:, 3 + j, :],
                                          y_h[:, j * 512:(j + 1) * 512], ALU.subtract).then_inc(m_yl, 1)
                    split_low(dve, u + 44, q)
                for tt in range(TT):
                    residual_part(NE, tt, NE + n0)

            moe_round(0)
            over = dve.value_load(flag[0:1, 0:1], min_val=0, max_val=1)
            with dve.If(over > 0):
                moe_round(1)

        @block.scalar
        def _(act):
            act.wait_ge(const, n_const["rows"])
            with nc.allow_non_contiguous_dma(reason="small parameters, loaded once"):
                param_rows(act, par_in, (A["mix_norm"], C_MIX), (A["da_subln"], C_SUB))
                for c in (0, 1):
                    act.dma_start(par_rows[C_QG:C_QG + 1, c * HD:(c + 1) * HD], A["da_q_gain"]).then_inc(par_in, 16)
                    act.dma_start(par_rows[C_KG:C_KG + 1, c * HD:(c + 1) * HD], A["da_k_gain"]).then_inc(par_in, 16)

            tables = [0]

            def table(func):
                act.activation(warm[:, tables[0]:tables[0] + 1], eps[:], func)
                tables[0] += 1

            def norm_sums(n):
                act.wait_ge(dve_const, 1)
                table(ACT.Ln)
                for tt in range(TT):
                    if n == 0:
                        act.wait_ge(x_in, 16 * TT)
                    else:
                        act.wait_ge(x_add, 4 * (n - 1) + 2 * (tt + 1))
                        act.wait_ge(n_t, 4 * n)
                    act.activation(xn[:, tt, :], x[:, tt, :], ACT.Square, accum_out=n_stat[:, n, 0, tt:tt + 1]).then_inc(n_sq, 1)
                act.wait_ge(n_sq, TT * (n + 1))
                act.activation(n_stat[:, n, 1, :], n_stat[:, n, 0, :], ACT.Ln, scale=1.0 / D, bias=eps[:]).then_inc(n_ln, 1)
                act.wait_ge(n_ln, n + 1)
                act.activation(n_stat[:, n, 2, :], n_stat[:, n, 1, :], ACT.Exp, scale=-0.5).then_inc(n_rs, 1)

            def norm_high(n, col):
                if n == 0:
                    act.wait_ge(par_cp, 1)
                for j in range(4):
                    act.wait_ge(n_t, 4 * n + j + 1)
                    b = (2 + j) if n == 0 else j
                    for c in range(2):
                        act.activation(h_h[:, 2 * j + c, :], bank[:, b, c * T:(c + 1) * T], ACT.Copy,
                                       scale=par[:, col + 2 * j + c:col + 2 * j + c + 1]).then_inc(n_high, 1)

            def inv_rms(n, count, src, dst, ready, ln, rs_sem, before=None):
                for i in range(n, n + count):
                    act.wait_ge(ready, i + 1)
                    if before is not None and before(i):
                        act.wait_ge(*before(i))
                    act.activation(dst(i), src(i), ACT.Ln, bias=eps[:]).then_inc(ln, 1)
                for i in range(n, n + count):
                    act.wait_ge(ln, i + 1)
                    act.activation(dst(i), dst(i), ACT.Exp, scale=-0.5).then_inc(rs_sem, 1)

            norm_sums(0)
            table(ACT.Sigmoid)
            split_high(act, 0)
            norm_high(0, C_MIX)
            split_high(act, 1)
            split_high(act, 2)

            def qk_inv(i):
                inv_rms(i, 2, lambda i: bank[:, 6 + i % 2, :], lambda i: rs[:, i % 2, :], qk_ms, qk_ln, qk_rs,
                        lambda i: (q_n, i - 1) if i >= 2 else None)

            for u in range(N_AB_IN):
                act.wait_ge(w_used, u + 1)
                if u in (1, 3):
                    if u == 3:
                        act.wait_ge(c_g, 1)
                    act.activation(sig[:], bank[:, 1, :], ACT.Sigmoid).then_inc(c_s, 1)
                if 4 <= u < 8:
                    i = u - 4
                    if i >= 2:
                        act.wait_ge(qk_ms, i - 1)
                    act.activation(q_raw[:, i, :], bank[:, u % 2, :], ACT.Copy).then_inc(qk_raw, 1)
                    act.activation(sq[:, i % 2, :], bank[:, u % 2, :], ACT.Square).then_inc(qk_sq, 1)
                if u >= 8:
                    act.activation(v_n[:, :, (u - 8) * UC:(u - 7) * UC], bank[:, u % 2, :].rearrange("p (a f) -> p a f", a=TT),
                                   ACT.Copy).then_inc(v_cp, 1)
                split_high(act, u + 3)
                if u in (6, 8):
                    qk_inv(u - 6)
            act.wait_ge(lam_d, 3)
            act.activation(lam[:, 2:4], lam[:, 0:2], ACT.Exp).then_inc(lam_e, 1)
            for b in range(6):
                act.wait_ge(s_nm, b + 1)
                n = 4 if b < 2 else 2
                for g in range(n):
                    idx = 4 * b + g if b < 2 else 8 + 2 * (b - 2) + g
                    c, h = (b, g) if b < 2 else ((b - 2) // 2, 2 * ((b - 2) % 2) + g)
                    w = P if b < 2 else T
                    dst = p_0[:, c, h, :] if b < 2 else p_1[:, c, h, :]
                    act.activation(dst, bank[:, 2 + b, g * w:(g + 1) * w], ACT.Exp, scale=HD ** -0.5,
                                   bias=nmx[:, idx:idx + 1], accum_out=ssum[:, idx:idx + 1]).then_inc(s_ex, 1)
            for h in range(HEADS):
                act.wait_ge(a_t, h + 1)
                act.activation(w_t[:, h, :], bank[:, 2 + h, 0:384], ACT.Copy).then_inc(a_wt, 1)
            act.wait_ge(qk_ms, 4)
            for b in range(2):
                act.wait_ge(a_o, b + 1)
                act.activation(sq[:, b, :], bank[:, 6 + b, :], ACT.Square).then_inc(a_sq, 1)
            inv_rms(0, 2, lambda b: bank[:, b, :], lambda b: rs[:, b, :], a_ms, a_ln, a_rs, lambda b: (q_n, 4))
            for b in range(2):
                act.wait_ge(g_c, b + 1)
                act.wait_ge(a_ms, b + 1)
                act.activation(sq[:, b, :].rearrange("p (a t) -> p a t", a=2), conv_y[:, 2 * b:2 * b + 2, :], ACT.Square).then_inc(g_sq, 1)
            for b in range(2):
                act.wait_ge(a_of, b + 1)
                act.activation(h_h[:, 2 * b:2 * b + 2, :], q_raw[:, b, :].rearrange("p (a t) -> p a t", a=2), ACT.Copy).then_inc(a_h, 1)
            inv_rms(0, 2, lambda b: bank[:, 2 + b, :], lambda b: rs[:, b, :], g_v, g_ln, g_rs, lambda b: (a_of, b + 1))
            table(ACT.Silu)
            for b in range(2):
                act.wait_ge(g_n, b + 1)
                for c in (2 * b, 2 * b + 1):
                    act.activation(conv_y[:, c, :], conv_y[:, c, :], ACT.Silu, scale=par[:, C_GG + c:C_GG + c + 1],
                                   bias=par[:, C_GB + c:C_GB + c + 1]).then_inc(g_s, 1)
                act.wait_ge(g_s, 2 * b + 2)
                act.activation(h_h[:, 4 + 2 * b:6 + 2 * b, :], conv_y[:, 2 * b:2 * b + 2, :], ACT.Copy).then_inc(g_h, 1)
            act.wait_ge(rout_in, 16)
            act.activation(router_h[:], router[:], ACT.Copy).then_inc(r_high, 1)
            for u in range(U_AB_OUT, U_FFN):
                split_high(act, u + 3)

            norm_sums(1)
            table(ACT.Silu)
            norm_high(1, C_FFN)

            def ffn_gate(s0, j2, s_par, a_used):
                act.wait_ge(w_used, a_used)
                if not (isinstance(j2, int) and s0 + j2 == 0):
                    act.wait_ge(f_mul, s0 + j2)
                act.activation(silu_g[:], bank[:, s_par, :], ACT.Silu).then_inc(f_silu, 1)

            def ffn_high(s0, j2, s_par):
                act.wait_ge(f_mul, s0 + j2 + 1)
                if s0 >= 2:
                    act.wait_ge(w_used, U_FFN + 3 * s0 - 1 + (j2 * 3))
                act.activation(act_h[:, s_par, :], act_f[:], ACT.Copy).then_inc(f_high, 1)

            ffn_gate(0, 0, 0, U_FFN + 1)
            split_high(act, U_FFN + 3)
            ffn_high(0, 0, 0)
            split_high(act, U_FFN + 4)
            split_high(act, U_FFN + 5)
            ffn_gate(1, 0, 1, U_FFN + 3)
            split_high(act, U_FFN + 6)
            ffn_high(1, 0, 1)
            split_high(act, U_FFN + 7)
            split_high(act, U_FFN + 8)
            with act.Fori(0, 4) as j:
                for k in (0, 1):
                    ffn_gate(2 + k, j * 2, k, U_FFN + 6 + 3 * k + j * 6)
                    split_high(act, U_FFN + 9 + 3 * k, j)
                    ffn_high(2 + k, j * 2, k)
                    split_high(act, U_FFN + 10 + 3 * k, j)
                    split_high(act, U_FFN + 11 + 3 * k, j)
            ffn_gate(10, 0, 0, U_FFN + 30)
            split_high(act, U_FFN + 33)
            ffn_high(10, 0, 0)
            split_high(act, U_FFN + 34)
            split_high(act, U_FFN + 35)

            norm_sums(2)
            table(ACT.Sigmoid)
            norm_high(2, C_MIX + 8)
            act.wait_ge(lb_d, 1)
            act.activation(lb[:, 1, :], lb[:, 0, :], ACT.Exp).then_inc(lb_d, 1)
            for i in range(N_HG_IN):
                act.wait_ge(w_used, U_HG_IN + i + 1)
                src = bank[:, (U_HG_IN + i) % 2, :].rearrange("p (a t) -> p a t", a=2)
                c = 2 * (i % 4)
                if i < 4:
                    act.activation(log_f[:, c:c + 2, :], src, ACT.Sigmoid).then_inc(hg_ev, 1)
                    act.activation(key_t[:, c:c + 2, :], src, ACT.Sigmoid, scale=-1.0).then_inc(hg_ev, 1)
                elif i < 8:
                    act.activation(qry_t[:, c:c + 2, :], src, ACT.Silu).then_inc(hg_ev, 1)
                elif i < 12:
                    if i == 8:
                        act.wait_ge(n_t, 12)
                    act.activation(gate_t[:, c:c + 2, :], src, ACT.Silu).then_inc(hg_ev, 1)
                else:
                    act.activation(val_n[:, :, (i - 12) * UC:(i - 11) * UC], src, ACT.Copy).then_inc(hg_ev, 1)
                split_high(act, U_HG_IN + i + 3)
                if i == 11:
                    for q in range(4):
                        act.wait_ge(hg_d, 3 * 4)
                        act.activation(log_f[:, 2 * q:2 * q + 2, :], log_f[:, 2 * q:2 * q + 2, :], ACT.Ln).then_inc(hg_ln, 1)
                if i == 13:
                    for q in range(4):
                        act.wait_ge(hg_t, q + 1)
                        tt, hq = q // 2, q % 2
                        act.activation(lf_h[:, tt, hq * 512:(hq + 1) * 512], bank[:, 2 + q, :], ACT.Copy).then_inc(hg_h, 1)
            for g in range(GROUPS):
                act.wait_ge(sp_d, g + 1)
                if g >= 2:
                    act.wait_ge(sp_m, g - 1)
                act.activation(decay[:, g % 2, :], bank[:, (0, 1, 6)[g % 3], :], ACT.Exp).then_inc(sp_e, 1)

            table(ACT.Ln)
            for j in range(4):
                act.wait_ge(o_o, j + 1)
                act.activation(o_sqs(j), bank[:, 2 + j, :], ACT.Square).then_inc(o_sq, 1)
            inv_rms(0, 4, lambda j: bank[:, (0, 1, 6, 7)[j], :], o_inv, o_ms, o_ln, o_rs)
            for j in range(4):
                act.wait_ge(o_g, j + 1)
                act.activation(h_h[:, 2 * j:2 * j + 2, :], o_nrm(j).rearrange("p (a t) -> p a t", a=2), ACT.Copy).then_inc(o_h, 1)
            for u in range(U_HG_OUT, U_MOE):
                split_high(act, u + 3)

            act.wait_ge(x_add, 12)
            act.dma_start(gain_row[:], A["ffn_norm"][1:2, :].to_broadcast([P, D])).then_inc(gain_in, 16)
            norm_sums(3)
            norm_high(3, C_FFN + 8)
            for part in range(2):
                for tt in range(TT):
                    act.wait_ge(x_gain, 2 * part + tt + 1)
                    act.activation(x_b[:, part, tt, :], x_g[:, tt, :], ACT.Copy).then_inc(x_part, 1)
            act.wait_ge(r_d, n_const["exp"])
            act.activation(pick[:, 5, :], pick[:, 4, :], ACT.Exp).then_inc(r_e, 1)

            def gather_high(n):
                for j in range(2):
                    act.wait_ge(m_gat, n * 2 + (j + 1))
                    act.activation(hs_h[:, 4 * j:4 * j + 4, :], bank[:, 5 + j, :].rearrange("p (c t) -> p c t", c=4), ACT.Copy).then_inc(m_hh, 1)

            def moe_gate(g, first, b_par, b_used):
                act.wait_ge(w_used, b_used)
                if not first:
                    act.wait_ge(m_mul, g)
                act.activation(m_silu[:], bank[:, b_par, 0:UC], ACT.Silu).then_inc(m_si, 1)

            def moe_high(g, b):
                act.wait_ge(m_t, g + 1)
                act.activation(ma_h[:, b, :], bank[:, 2, 0:UC], ACT.Copy).then_inc(m_ah, 1)

            def moe_step(u, k, gs, used, rounds):
                moe_gate(gs, False, (1 + k) % 2, used)
                split_high(act, u + 6 + 3 * k, rounds)
                split_high(act, u + 7 + 3 * k, rounds)
                moe_high(gs, (1 + k) % 2)
                split_high(act, u + 8 + 3 * k, rounds)

            def moe_round(r):
                u = U_MOE + r * NE * MOE_UNITS
                g0 = r * NE * MOE_STEPS
                n0 = r * (NE + 1)
                act.activation(m_silu[:, 0:1], eps[:], ACT.Silu)
                gather_high(n0)
                with act.Fori(0, NE) as e:
                    q = e * 7
                    g = e * MOE_STEPS + g0
                    split_high(act, u + 3, q)
                    act.wait_ge(w_used, e * MOE_UNITS + (u + 2))
                    act.activation(m_silu[:], bank[:, 0, 0:UC], ACT.Silu).then_inc(m_si, 1)
                    split_high(act, u + 4, q)
                    moe_high(g, 0)
                    split_high(act, u + 5, q)
                    with act.Fori(0, 5) as j:
                        for k in (0, 1):
                            moe_step(u, k, g + j * 2 + (1 + k), e * MOE_UNITS + j * 6 + (u + 4 + 3 * k), q + j)
                    act.wait_ge(m_pt, e + (n0 + 1))
                    act.wait_ge(m_sc, e * 4 + (4 * n0 + 4))
                    act.activation(scat[:], bank[:, 7, 0:T], ACT.Copy).then_inc(m_scat, 1)
                    for k in (0, 1):
                        moe_step(u + 5 * 6, k, g + (11 + k), e * MOE_UNITS + (u + 34 + 3 * k), q)
                    moe_gate(g + 13, False, 1, e * MOE_UNITS + (u + 40))
                    gather_high(e + (n0 + 1))
                    moe_high(g + 13, 1)
                    split_high(act, u + 42, q)
                    split_high(act, u + 43, q)
                    act.wait_ge(w_used, e * MOE_UNITS + (u + 42))
                    for j in range(2):
                        act.activation(y_h[:, j * 512:(j + 1) * 512], bank[:, 3 + j, :], ACT.Copy).then_inc(m_yh, 1)
                    split_high(act, u + 44, q)

            moe_round(0)
            act.wait_ge(r_flag, 1)
            over = act.value_load(flag[0:1, 0:1], min_val=0, max_val=1)
            with act.If(over > 0):
                moe_round(1)

        @block.tensor
        def _(pe):
            def three(o, a_high, a_low, b_high, b_low, start, stop):
                pe.matmul(o, a_high, b_high, start=start, stop=False, skip_group_check=True)
                pe.matmul(o, a_high, b_low, start=False, stop=False, skip_group_check=True)
                return pe.matmul(o, a_low, b_high, start=False, stop=stop, skip_group_check=True)

            def unit_to_features(u0, b, rounds=0):
                wait_split(pe, u0, rounds)
                wh, wl = as_in(w_h, u0 % S), as_in(w_l, u0 % S)
                for mch in range(2):
                    f = slice(mch * P, (mch + 1) * P)
                    for c in range(KC):
                        last = three(bank[:, b, mch * T:(mch + 1) * T], wh[:, c, f], wl[:, c, f], h_h[:, c, :], h_l[:, c, :],
                                     c == 0, c == KC - 1)
                last.then_inc(w_used, 1)

            def unit_to_tokens(u0, b):
                wait_split(pe, u0)
                wh, wl = as_in(w_h, u0 % S), as_in(w_l, u0 % S)
                for tt in range(TT):
                    t = slice(tt * P, (tt + 1) * P)
                    for c in range(KC):
                        last = three(bank[:, b, tt * UC:(tt + 1) * UC], h_h[:, c, t], h_l[:, c, t], wh[:, c, :], wl[:, c, :],
                                     c == 0, c == KC - 1)
                last.then_inc(w_used, 1)

            def unit_out(u0, ah, al, first, last_unit, rounds=0):
                wait_split(pe, u0, rounds)
                wh, wl = as_out(w_h, u0 % S), as_out(w_l, u0 % S)
                for c in range(OC):
                    for tt in range(TT):
                        for half in range(2):
                            v = slice(half * 512, (half + 1) * 512)
                            last = three(bank[:, 4 + 2 * tt + half, :], ah(c, tt), al(c, tt), wh[:, c, v], wl[:, c, v],
                                         first and c == 0, last_unit and c == OC - 1)
                        if last_unit and c == OC - 1 and tt == 0:
                            last.then_inc(o_part, 1)
                last.then_inc(w_used, 1)

            def norm_turn(n):
                pe.wait_ge(n_xn, 2 * n + 2)
                for j in range(4):
                    b = (2 + j) if n == 0 else j
                    for c in range(2):
                        for tt in range(TT):
                            last = pe.transpose(bank[:, b, c * T + tt * P:c * T + (tt + 1) * P],
                                                xn[:, tt, (2 * j + c) * P:(2 * j + c + 1) * P], ident[:])
                    last.then_inc(n_t, 1)
                pe.wait_ge(n_low, 8 * n + 8)

            pe.wait_ge(const, n_const["rows"])
            pe.wait_ge(par_in, 16 * 10)
            pe.wait_ge(par_in_pool, 16 * 3)
            pe.transpose(bank[:, 0, 0:P], par_rows[:], ident[:]).then_inc(par_t, 1)
            pe.transpose(bank[:, 1, 0:P], dw_rows[:], ident[:]).then_inc(par_t, 1)
            pe.wait_ge(par_cp, 2)
            norm_turn(0)
            free = {2: (c_g, 1), 3: (c_s, 1), 4: (c_g, 2), 5: (c_s, 2), 6: (qk_sq, 1), 7: (qk_sq, 2), 8: (qk_sq, 3), 9: (qk_sq, 4)}

            def qk_mean(i):
                pe.wait_ge(qk_sq, i + 1)
                if i >= 2:
                    pe.wait_ge(qk_ln, i - 1)
                pe.matmul(bank[:, 6 + i % 2, :], mean_64[:], sq[:, i % 2, :], start=True, stop=True).then_inc(qk_ms, 1)

            for u in range(N_AB_IN):
                if u in free:
                    pe.wait_ge(*free[u])
                (unit_to_features if u < 8 else unit_to_tokens)(u, u % 2)
                if 5 <= u <= 8:
                    qk_mean(u - 5)
            pe.wait_ge(q_n, 4)
            pe.wait_ge(qk_ln, 4)
            for b in range(6):
                qt = 0 if b < 2 else 1
                c = b if b < 2 else (b - 2) // 2
                n, w = (4, P) if qt == 0 else (2, T)
                rows = slice(HD * c, HD * (c + 1))
                for g in range(n):
                    h = g if qt == 0 else 2 * ((b - 2) % 2) + g
                    pe.matmul(bank[:, 2 + b, g * w:(g + 1) * w], q_t[rows, h, qt * P:(qt + 1) * P], k_t[rows, h, 0:w],
                              start=True, stop=False, skip_group_check=True)
                    last = pe.matmul(bank[:, 2 + b, g * w + qt * P:g * w + (qt + 1) * P], ident_b[:], mask_b[:], start=False, stop=True,
                                     skip_group_check=True)
                last.then_inc(s_sc, 1)
            for h in range(HEADS):
                pe.wait_ge(s_w, 8 + 4 + h + 1)
                pe.transpose(bank[:, 2 + h, 0:P], p_0[:, 0, h, :], ident[:])
                pe.transpose(bank[:, 2 + h, P:2 * P], p_1[:, 0, h, 0:P], ident[:])
                pe.transpose(bank[:, 2 + h, 2 * P:3 * P], p_1[:, 0, h, P:2 * P], ident[:]).then_inc(a_t, 1)
            pe.wait_ge(v_cp, 2)
            for b in range(2):
                for h in (2 * b, 2 * b + 1):
                    pe.wait_ge(a_wt, h + 1)
                    o = (h % 2) * T
                    pe.matmul(bank[:, 6 + b, o:o + T], v_n[:, 0, h * P:(h + 1) * P], w_t[:, h, 0:T], start=True, stop=False,
                              skip_group_check=True)
                    last = pe.matmul(bank[:, 6 + b, o + P:o + T], v_n[:, 1, h * P:(h + 1) * P], w_t[:, h, T:T + P], start=False,
                                     stop=True, skip_group_check=True)
                last.then_inc(a_o, 1)
            pe.wait_ge(c_y, 4 * TAPS)
            for b in range(2):
                pe.matmul(bank[:, 2 + b, :], mean_64[:], conv_y[:, 2 * b:2 * b + 2, :], start=True, stop=True).then_inc(g_m, 1)
            for b in range(2):
                pe.wait_ge(a_sq, b + 1)
                pe.matmul(bank[:, b, :], mean_all[:], sq[:, b, :], start=True, stop=True).then_inc(a_ms, 1)
            for b in range(2):
                pe.wait_ge(g_sq, b + 1)
                pe.matmul(bank[:, 2 + b, :], mean_64[:], sq[:, b, :], start=True, stop=True).then_inc(g_v, 1)

            def from_h(i):
                return (lambda c, tt: h_h[:, 2 * i + c, tt * P:(tt + 1) * P]), (lambda c, tt: h_l[:, 2 * i + c, tt * P:(tt + 1) * P])

            for i in range(N_OUT):
                pe.wait_ge(*((a_l, i + 1) if i < 2 else (g_l, i - 1)))
                unit_out(U_AB_OUT + i, *from_h(i), i == 0, i == N_OUT - 1)
            norm_turn(1)

            def ffn_out_unit(s0, j, b, first, last_unit, u0=None):
                pe.wait_ge(f_low, j * 2 + (s0 + 1))
                unit_out(U_FFN + 3 * s0 + 4 if u0 is None else u0, lambda c, tt: act_h[:, b, c * T + tt * P:c * T + (tt + 1) * P],
                         lambda c, tt: act_l[:, b, c * T + tt * P:c * T + (tt + 1) * P], first, last_unit, j)

            def ffn_body(s0, j, b):
                nb = 1 - b
                if s0:
                    pe.wait_ge(f_silu, j * 2 + s0)
                unit_to_features(U_FFN + 3 * s0 + 2, nb, j)
                if s0:
                    pe.wait_ge(f_mul, j * 2 + s0)
                unit_to_features(U_FFN + 3 * s0 + 3, 2 + nb, j)
                ffn_out_unit(s0, j, b, s0 == 0, False)

            unit_to_features(U_FFN, 0)
            unit_to_features(U_FFN + 1, 2)
            ffn_body(0, 0, 0)
            with pe.Fori(0, 4) as j:
                ffn_body(1, j, 1)
                ffn_body(2, j, 0)
            ffn_body(9, 0, 1)
            ffn_out_unit(10, 0, 0, False, True, U_FFN + 32)
            norm_turn(2)

            for i in range(N_HG_IN):
                if i >= 2:
                    pe.wait_ge(hg_ev, 2 * (i - 1) if i < 6 else i + 3)
                (unit_to_features if i < 12 else unit_to_tokens)(U_HG_IN + i, (U_HG_IN + i) % 2)
                if i == 13:
                    for q in range(4):
                        tt, hq = q // 2, q % 2
                        pe.wait_ge(hg_ln, 2 * hq + 2)
                        for h in range(4):
                            last = pe.transpose(bank[:, 2 + q, h * P:(h + 1) * P], log_f[:, 4 * hq + h, tt * P:(tt + 1) * P], ident[:])
                        last.then_inc(hg_t, 1)
            pe.wait_ge(hg_l, 4)
            for q in range(4):
                tt, hq = q // 2, q % 2
                for h in range(4):
                    t = slice(tt * P, (tt + 1) * P)
                    last = pe.matmul(bank[:, 2 + q, h * P:(h + 1) * P], key_t[:, 4 * hq + h, t], qry_t[:, 4 * hq + h, t], start=True, stop=True)
                last.then_inc(hd, 1)

            def spans(g):
                p, hp, tt = g // 8, (g // 2) % 4, g % 2
                if g >= 3:
                    pe.wait_ge(sp_e, g - 2)
                b = (0, 1, 6)[g % 3]
                mm = span[:, p if p < 3 else 3 + tt, :, :]
                for a in range(2):
                    f = slice((2 * hp + a) * P, (2 * hp + a + 1) * P)
                    pe.matmul(bank[:, b, a * T:(a + 1) * T], lf_h[:, tt, f], mm, start=True, stop=False)
                    last = pe.matmul(bank[:, b, a * T:(a + 1) * T], lf_l[:, tt, f], mm, start=False, stop=True)
                last.then_inc(sp_d, 1)

            def scores(g):
                p, hp, tt = g // 8, (g // 2) % 4, g % 2
                pe.wait_ge(sp_m, g + 1)
                if g >= 4:
                    pe.wait_ge(sp_c0, g - 3)
                    pe.wait_ge(sp_c1, second(g - 4))
                else:
                    pe.wait_ge(hd_cp, g % 4 + 1)
                b = 2 + g % 4
                for a in range(2):
                    for li in range(2):
                        o = bank[:, b, (2 * a + li) * P:(2 * a + li + 1) * P]
                        v = slice((2 * a + li) * P, (2 * a + li + 1) * P)
                        if 2 * p + li < 7:
                            last = pe.matmul(o, dk[:, g % 2, v], dq[:, g % 2, v], start=True, stop=True)
                        elif tt == 1:
                            last = pe.matmul(o, dk[:, 1 - g % 2, v], dq[:, g % 2, v], start=True, stop=True)
                last.then_inc(sp_s, 1)

            pe.wait_ge(const, n_const["all"])
            pe.wait_ge(hg_ev, 20)
            spans(0)
            spans(1)
            for g in range(GROUPS):
                if g + 2 < GROUPS:
                    spans(g + 2)
                scores(g)
            pe.wait_ge(sp_c0, GROUPS)
            pe.wait_ge(sp_c1, second(GROUPS - 1))
            for j in range(4):
                for h in (2 * j, 2 * j + 1):
                    o = (h % 2) * T
                    pe.matmul(bank[:, 2 + j, o:o + T], val_n[:, 0, h * P:(h + 1) * P], att[:, h, 0:2, :], start=True, stop=False,
                              skip_group_check=True)
                    last = pe.matmul(bank[:, 2 + j, o + P:o + T], val_n[:, 1, h * P:(h + 1) * P], att[:, h, 2, :], start=False, stop=True,
                                     skip_group_check=True)
                last.then_inc(o_o, 1)
            for j in range(4):
                pe.wait_ge(o_sq, j + 1)
                pe.matmul(bank[:, (0, 1, 6, 7)[j], :], mean_all[:], o_sqs(j), start=True, stop=True).then_inc(o_ms, 1)
            for i in range(N_OUT):
                pe.wait_ge(o_l, i + 1)
                if i == 0:
                    pe.wait_ge(o_n, 4)
                unit_out(U_HG_OUT + i, *from_h(i), i == 0, i == N_OUT - 1)
            norm_turn(3)

            pe.wait_ge(r_low, 1)
            for c in range(KC):
                three(bank[0:NE, 4, 0:T], router_h[:, c, :], router_l[:, c, :], h_h[:, c, :], h_l[:, c, :], c == 0, False)
                last = pe.matmul(bank[0:NE, 4, 0:T], router_l[:, c, :], h_l[:, c, :], start=False, stop=c == KC - 1,
                                 skip_group_check=True)
            last.then_inc(r_lt, 1)
            pe.wait_ge(r_lc, 1)
            for tt in range(TT):
                last = pe.transpose(bank[:, 5, tt * NE:(tt + 1) * NE], logit_t[:, tt * P:(tt + 1) * P], ident[0:NE, 0:NE])
            last.then_inc(r_lg, 1)
            pe.wait_ge(r_d, n_const["sel"])
            s0, s1 = logit[:, 6, 0, :], logit[:, 6, 1, :]
            pe.matmul(bank[:, 6, 0:NE], before[:], s0, start=True, stop=True)
            pe.matmul(bank[:, 6, NE:2 * NE], ones[:], s0, start=True, stop=False)
            pe.matmul(bank[:, 6, NE:2 * NE], before[:], s1, start=False, stop=True)
            pe.matmul(bank[:, 6, 2 * NE:3 * NE], ones[:], s0, start=True, stop=False)
            pe.matmul(bank[:, 6, 2 * NE:3 * NE], ones[:], s1, start=False, stop=True).then_inc(r_rank, 1)

            def gather(n):
                pe.wait_ge(m_sel, n * 2 + 2)
                pe.wait_ge(m_add, n * 4 + 1)
                for j in range(2):
                    for c in range(4):
                        f = slice((4 * j + c) * P, (4 * j + c + 1) * P)
                        for tt in range(TT):
                            for part in range(3):
                                last = pe.matmul(bank[:, 5 + j, c * P:(c + 1) * P], x_b[:, part, tt, f], sel[:, tt, :],
                                                 start=tt == 0 and part == 0, stop=tt == 1 and part == 2, skip_group_check=True)
                    last.then_inc(m_gat, 1)
                pe.wait_ge(m_scat, n + 1)
                for tt in range(TT):
                    last = pe.matmul(bank[:, 7, tt * P:(tt + 1) * P], sel[:, tt, :], ident_h[:], start=True, stop=True)
                last.then_inc(m_pt, 1)

            def scatter(tt, n):
                if tt == 0:
                    pe.wait_ge(m_yl, n * 2 + 2)
                    pe.wait_ge(m_scat, n + 1)
                else:
                    pe.wait_ge(m_add, n * 4 + 3)
                for half in range(2):
                    v = slice(half * 512, (half + 1) * 512)
                    pe.matmul(bank[:, 5 + half, :], scat[:, tt * P:(tt + 1) * P], y_h[:, v], start=True, stop=False, skip_group_check=True)
                    pe.matmul(bank[:, 5 + half, :], scat[:, tt * P:(tt + 1) * P], y_l[:, v], start=False, stop=True,
                              skip_group_check=True).then_inc(m_sc, 1)

            def moe_in(u0, b, half, rounds):
                wait_split(pe, u0, rounds)
                wh, wl = as_in(w_h, u0 % S), as_in(w_l, u0 % S)
                for c in range(KC):
                    last = three(bank[:, b, half * UC:(half + 1) * UC], hs_h[:, c, :], hs_l[:, c, :], wh[:, c, :], wl[:, c, :],
                                 c == 0, c == KC - 1)
                last.then_inc(w_used, 1)

            def moe_turn(g):
                pe.wait_ge(m_mul, g + 1)
                for c in range(2):
                    last = pe.transpose(bank[:, 2, c * P:(c + 1) * P], m_act[:, c * P:(c + 1) * P], ident[:])
                last.then_inc(m_t, 1)

            def moe_out(u0, g, b, first, last_unit, rounds, turn=None):
                pe.wait_ge(m_al, g + 1)
                wait_split(pe, u0, rounds)
                wh, wl = as_out(w_h, u0 % S), as_out(w_l, u0 % S)
                for c in range(OC):
                    if c == 1 and turn is not None:
                        moe_turn(turn)
                    t = slice(c * P, (c + 1) * P)
                    for half in range(2):
                        v = slice(half * 512, (half + 1) * 512)
                        last = three(bank[:, 3 + half, :], ma_h[:, b, t], ma_l[:, b, t], wh[:, c, v], wl[:, c, v],
                                     first and c == 0, last_unit and c == OC - 1)
                last.then_inc(w_used, 1)

            def moe_step(u, k, gs, rounds, last=False):
                pe.wait_ge(m_mul, gs)
                moe_in(u + 5 + 3 * k, k, 0, rounds)
                moe_turn(gs)
                moe_in(u + 6 + 3 * k, k, 1, rounds)
                moe_out(u + 7 + 3 * k, gs, (1 + k) % 2, False, False, rounds, gs + 1 if last else None)

            def moe_round(r):
                u = U_MOE + r * NE * MOE_UNITS
                g0 = r * NE * MOE_STEPS
                n0 = r * (NE + 1)
                gather(n0)
                with pe.Fori(0, NE) as e:
                    q = e * 7
                    g = e * MOE_STEPS + g0
                    n = e + n0
                    pe.wait_ge(m_hl, e * 2 + (2 * n0 + 2))
                    moe_in(u, 0, 0, q)
                    moe_in(u + 1, 0, 1, q)
                    scatter(0, n)
                    moe_in(u + 2, 1, 0, q)
                    moe_turn(g)
                    moe_in(u + 3, 1, 1, q)
                    scatter(1, n)
                    moe_out(u + 4, g, 0, True, False, q)
                    with pe.Fori(0, 5) as j:
                        for k in (0, 1):
                            moe_step(u, k, g + j * 2 + (1 + k), q + j)
                    gather(n + 1)
                    for k in (0, 1):
                        moe_step(u + 5 * 6, k, g + (11 + k), q, k == 1)
                    moe_out(u + 41, g + 13, 1, False, True, q)
                for tt in range(TT):
                    scatter(tt, NE + n0)

            pe.wait_ge(x_gain, 6)
            moe_round(0)
            pe.wait_ge(r_flag, 1)
            over = pe.value_load(flag[0:1, 0:1], min_val=0, max_val=1)
            with pe.If(over > 0):
                moe_round(1)


_INS = ['x', 'mix_norm', 'ffn_norm', 'ab_w_in', 'ab_w_out', 'da_q_gain', 'da_k_gain', 'da_lambda', 'da_subln',
        'conv_dw', 'conv_dw_bias', 'conv_gn_gain', 'conv_gn_bias', 'hgrn_w_in', 'hgrn_lb_logits', 'hgrn_norm',
        'hgrn_w_out', 'ffn_w_in', 'ffn_w_out', 'moe_router', 'moe_w_in', 'moe_w_out']


def kernel(**inputs):
    import numpy as np
    import concourse.bacc as bacc
    from concourse.bass_utils import run_bass_kernel_spmd

    nc = bacc.Bacc("TRN2", target_bir_lowering=False, num_devices=1)
    arrays, args = {}, {}
    for name in _INS:
        a = np.ascontiguousarray(inputs[name])
        arrays[f"in_{name}"] = a
        args[name] = nc.dram_tensor(f"in_{name}", a.shape, mybir.dt.from_np(a.dtype), kind="ExternalInput").ap()
    out = nc.dram_tensor("out", (1, T, D), F32, kind="ExternalOutput").ap()
    build(nc, args, out)
    return run_bass_kernel_spmd(nc, [arrays], core_ids=[0]).results[0]["out"]
```

```python
import math
from contextlib import ExitStack

import concourse.bass as bass
from concourse import mybir

ALU = mybir.AluOpType
ACT = mybir.ActivationFunctionType
AX = mybir.AxisListType
F32 = mybir.dt.float32
F32R = mybir.dt.float32r
BF16 = mybir.dt.bfloat16
I8 = mybir.dt.int8
I32 = mybir.dt.int32

P = 128
T = 256
TT = T // P
D = 1024
KC = D // P
UC = 256
UNIT = KC * UC
OC = UNIT // D
R = 6
S = 3
POOL_FROM, POOL_TO = 3, 13
EPS = 1e-6
HEADS = 4
HD = 64
TAPS = 31
PE_TAPS = 6
HH = 8
NE = 8
CAP = 128
LAM_INIT = 0.8 - 0.6 * math.exp(-0.3 * 0)
NEG = -1.0e30

U_AB_IN, N_AB_IN = 0, 10
U_AB_OUT, N_OUT = 10, 4
U_FFN = 14
FFN_STEPS = 11
U_HG_IN, N_HG_IN = U_FFN + 3 * FFN_STEPS, 16
U_HG_OUT = U_HG_IN + N_HG_IN
U_MOE = U_HG_OUT + N_OUT
MOE_STEPS = 14
MOE_UNITS = 3 * MOE_STEPS
AB_ORDER = [1536, 2048, 1792, 2304, 0, 256, 512, 768, 1024, 1280]
HG_ORDER = [1024 + 256 * i for i in range(4)] + [256 * i for i in range(4)] \
    + [3072 + 256 * i for i in range(3)] + [2048 + 256 * i for i in range(4)] + [3072 + 256 * 3]

C_MIX, C_FFN, C_HN, C_LB, C_DWB, C_GG, C_GB, C_SUB, C_QG, C_KG = 0, 16, 32, 40, 48, 52, 56, 60, 61, 62
N_PAR = 63
LEVELS = [1, 2, 4, 8, 16, 32, 64]
PAIRS = 4
O_BANK = (7, 6, 0, 1)
GROUPS = PAIRS * (HH // 2) * TT


def build(nc, A, out):
    with ExitStack() as ctx:
        def sb(name, shape, dt=F32):
            return ctx.enter_context(nc.sbuf_tensor(name, shape, dt))

        def sem(name):
            return ctx.enter_context(nc.semaphore(name))

        bank = ctx.enter_context(nc.psum_tensor("bank", [P, 8, 512], F32))

        raw = sb("raw", [P, R, UNIT])
        w_h = sb("w_h", [P, S, UNIT], F32R)
        w_l = sb("w_l", [P, S, UNIT], F32R)
        x = sb("x", [P, TT, D])
        xn = sb("xn", [P, TT, D])
        h_h = sb("h_h", [P, KC, T], F32R)
        h_l = sb("h_l", [P, KC, T], F32R)
        ident = sb("ident", [P, P])
        ones = sb("ones", [P, P])
        mean_all = sb("mean_all", [P, P])
        mean_64 = sb("mean_64", [P, P])
        before = sb("before", [P, P])
        slot_no = sb("slot_no", [P, 2, P])
        expert_no = sb("expert_no", [P, NE])
        par = sb("par", [P, P])
        dw = sb("dw", [P, P])
        eps = sb("eps", [P, 1])
        n_stat = sb("n_stat", [P, 4, 3, TT])
        router = sb("router", [P, KC, NE])
        router_h = sb("router_h", [P, KC, NE], F32R)
        router_l = sb("router_l", [P, KC, NE], F32R)
        flag = sb("flag", [P, 1], I32)
        warm = sb("warm", [P, 16])
        ident_h = sb("ident_h", [P, P], BF16)
        span = sb("span", [P, 5, 2, P], F32R)
        lmask = sb("lmask", [P, 7, P], I8)

        def phase(items):
            made = []
            with ExitStack() as inner:
                for n, shape, dt in items:
                    made.append(inner.enter_context(nc.sbuf_tensor(n, shape, dt)))
            return made

        (par_rows, dw_rows, lam_rows, lam_prod, lam, ident_b, mask_b, conv_in, conv_y, sig, q_raw, sq, rs, q_t, k_t, v_n,
         p_0, p_1, w_t, smx, nmx, ssum, rsum) = phase([
            ("par_rows", [P, P], F32), ("dw_rows", [P, P], F32), ("lam_rows", [P, 4, HD], F32), ("lam_prod", [P, 2, HD], F32),
            ("lam", [P, 8], F32), ("ident_b", [P, P], BF16), ("mask_b", [P, P], BF16),
            ("conv_in", [P, 4, TAPS - 1 + T], F32), ("conv_y", [P, 4, T], F32),
            ("sig", [P, 512], F32), ("q_raw", [P, 4, 512], F32), ("sq", [P, 2, 512], F32), ("rs", [P, 2, 512], F32),
            ("q_t", [P, HEADS, T], F32), ("k_t", [P, HEADS, T], F32), ("v_n", [P, TT, 512], F32),
            ("p_0", [P, 2, HEADS, P], F32), ("p_1", [P, 2, HEADS, T], F32), ("w_t", [P, HEADS, 384], F32),
            ("smx", [P, 16], F32), ("nmx", [P, 16], F32), ("ssum", [P, 16], F32), ("rsum", [P, 16], F32)])
        silu_g, act_f, act_h, act_l = phase([
            ("silu_g", [P, 512], F32), ("act_f", [P, 512], F32),
            ("act_h", [P, 2, 512], F32R), ("act_l", [P, 2, 512], F32R)])
        key_t, qry_t, val_n, lf_h, lf_l, att, dq, dk, decay, lb = phase([
            ("key_t", [P, HH, T], F32), ("qry_t", [P, HH, T], F32), ("val_n", [P, TT, D], F32),
            ("lf_h", [P, TT, D], F32R), ("lf_l", [P, TT, D], F32R), ("att", [P, HH, 3, P], F32),
            ("dq", [P, 2, 512], F32), ("dk", [P, 2, 512], F32), ("decay", [P, 2, 512], F32), ("lb", [P, 5, HH], F32)])
        (gain_row, x_g, x_b, logit_t, logit, pick, rank, comb, sel, scat, hs_h, hs_l, m_silu, m_act, ma_h, ma_l,
         y_h, y_l) = phase([
            ("gain_row", [P, D], F32), ("x_g", [P, TT, D], F32), ("x_b", [P, 3, TT, D], BF16), ("logit_t", [NE, T], F32),
            ("logit", [P, 12, 2, NE], F32), ("pick", [P, 12, 2], F32),
            ("rank", [P, TT * (NE + 1)], F32),
            ("comb", [P, TT * (NE + 1)], F32),
            ("sel", [P, 2, P], BF16), ("scat", [P, T], F32R),
            ("hs_h", [P, KC, P], F32R), ("hs_l", [P, KC, P], F32R), ("m_silu", [P, UC], F32), ("m_act", [P, UC], F32),
            ("ma_h", [P, 2, UC], F32R), ("ma_l", [P, 2, UC], F32R), ("y_h", [P, D], F32R), ("y_l", [P, D], F32R)])
        diag = w_t[:].rearrange("p h (a t) -> p (h a) t", t=P)
        gate_t = xn[:].rearrange("p a (b t) -> p (a b) t", t=T)
        def o_sqs(j):
            return key_t[:, 2 * j:2 * j + 2, :].rearrange("p a t -> p (a t)")

        def o_inv(j):
            return qry_t[:, 2 * j:2 * j + 2, :].rearrange("p a t -> p (a t)")

        def o_nrm(j):
            return (dq, dk)[j // 2][:, j % 2, :]

        log_f = att[:, :, 0:2, :].rearrange("p h a t -> p h (a t)")

        w_in = [sem(f"w_in{i}") for i in range(R)]
        w_high, w_used = sem("w_high"), sem("w_used")
        w_low, w_low_pool = sem("w_low"), sem("w_low_pool")
        x_in, par_in, lam_in, rout_in, gain_in = sem("x_in"), sem("par_in"), sem("lam_in"), sem("rout_in"), sem("gain_in")
        par_in_pool = sem("par_in_pool")
        par_t, par_cp = sem("par_t"), sem("par_cp")
        const, dve_const = sem("const"), sem("dve_const")
        n_sq, n_ln, n_rs, n_xn, n_t, n_high, n_low = (sem(f"n_{k}") for k in "sq ln rs xn t high low".split())
        o_part, x_add = sem("o_part"), sem("x_add")
        lam_d, lam_e, sub_g, lb_d = sem("lam_d"), sem("lam_e"), sem("sub_g"), sem("lb_d")
        c_s, c_g, c_y, c_diag, c_pe, c_sum = (sem(k) for k in "c_s c_g c_y c_diag c_pe c_sum".split())
        qk_raw, qk_sq, qk_ms, qk_ln, qk_rs, q_n, v_cp = (sem(k) for k in "qk_raw qk_sq qk_ms qk_ln qk_rs q_n v_cp".split())
        s_sc, s_mx, s_nm, s_ex, s_rc, s_p0, s_w = (sem(k) for k in "s_sc s_mx s_nm s_ex s_rc s_p0 s_w".split())
        a_t, a_wt, a_o, a_sq, a_ms, a_ln, a_rs, a_of, a_h, a_l = (sem(f"a_{k}") for k in "t wt o sq ms ln rs of h l".split())
        g_m, g_c, g_sq, g_v, g_ln, g_rs, g_n, g_s, g_h, g_l = (sem(f"g_{k}") for k in "m c sq v ln rs n s h l".split())
        f_silu, f_mul, f_high, f_low = (sem(f"f_{k}") for k in "silu mul high low".split())
        hg_ev, hg_d, hg_ln, hg_t, hg_h, hg_l, hg_gg, hg_z = (sem(f"hg_{k}") for k in "ev d ln t h l gg z".split())
        hd, hd_cp, sp_d, sp_e, sp_m, sp_k, sp_s, sp_c0, sp_c1 = (sem(k) for k in "hd hd_cp sp_d sp_e sp_m sp_k sp_s sp_c0 sp_c1".split())
        o_o, o_sq, o_ms, o_ln, o_rs, o_n, o_g, o_h, o_l = (sem(f"o_{k}") for k in "o sq ms ln rs n g h l".split())
        r_high, r_low, r_lt, r_lc, r_lg, r_d, r_e, r_rank, r_flag = (sem(f"r_{k}") for k in "high low lt lc lg d e rank flag".split())
        x_gain, x_part = sem("x_gain"), sem("x_part")
        m_sel, m_gat, m_pt, m_scat, m_hh, m_hl = (sem(f"m_{k}") for k in "sel gat pt scat hh hl".split())
        m_si, m_mul, m_t, m_ah, m_al, m_yh, m_yl, m_sc, m_add = (sem(f"m_{k}") for k in "si mul t ah al yh yl sc add".split())
        stored = sem("stored")
        n_const = {}

        def in_cols(w):
            return w.rearrange("(c p) f -> p c f", p=P)

        def out_rows(w):
            return w.rearrange("(s c p) d -> s p c d", p=P, c=OC)

        ab_in, ab_out = in_cols(A["ab_w_in"][0]), out_rows(A["ab_w_out"][0])
        ffn_in, ffn_out = in_cols(A["ffn_w_in"][0]), out_rows(A["ffn_w_out"][0])
        hg_in, hg_out = in_cols(A["hgrn_w_in"][0]), out_rows(A["hgrn_w_out"][0])
        FFN_UP = FFN_STEPS * UC
        MOE_UP = MOE_STEPS * UC

        def as_in(t, slot):
            return t[:, slot, :].rearrange("p (c f) -> p c f", c=KC)

        def as_out(t, slot):
            return t[:, slot, :].rearrange("p (c d) -> p c d", c=OC)

        def second(g):
            return g + 1 - len([n for n in range(g + 1) if n >= GROUPS - 8 and n % 2 == 0])

        def wait_split(eng, u0, rounds=0):
            if POOL_FROM <= u0 < POOL_TO:
                eng.wait_ge(w_low_pool, u0 - POOL_FROM + 1)
            elif u0 < POOL_FROM:
                eng.wait_ge(w_low, u0 + 1)
            else:
                eng.wait_ge(w_low, u0 + 1 - (POOL_TO - POOL_FROM) + R * rounds)

        def level_of(t, g, li):
            return t[:, g % 2, :].rearrange("p (a l t) -> p a l t", a=2, l=2)[:, :, li, :]

        def half_of(v, h, half):
            return v.rearrange("p a (b s r) -> p a b s r", s=2, r=h)[:, :, :, half, :]

        def last_scores(g):
            return g if g // 8 == 3 and g % 2 == 0 and g >= 26 else g - 1

        def load(sp, u0, view, src, rounds=0):
            if u0 >= R:
                wait_split(sp, u0 - R, rounds)
            sp.dma_start(view(raw, u0 % R), src).then_inc(w_in[u0 % R], 16)

        def split_high(act, u0, rounds=0):
            act.wait_ge(w_in[u0 % R], 16 * (u0 // R + 1) + 16 * rounds)
            if u0 >= S:
                act.wait_ge(w_used, u0 - S + 1 + R * rounds)
            act.activation(w_h[:, u0 % S, :], raw[:, u0 % R, :], ACT.Copy).then_inc(w_high, 1)

        def split_low(eng, u0, rounds=0):
            eng.wait_ge(w_high, u0 + 1 + R * rounds)
            eng.tensor_tensor(w_l[:, u0 % S, :], raw[:, u0 % R, :], w_h[:, u0 % S, :],
                              ALU.subtract).then_inc(w_low_pool if POOL_FROM <= u0 < POOL_TO else w_low, 1)

        block = ctx.enter_context(nc.Block())

        def param_rows(eng, done, *rows):
            for src, at in rows:
                v = src.rearrange("l (c p) -> (l c) p", p=P)
                eng.dma_start(par_rows[at:at + v.shape[0], :], v).then_inc(done, 16)

        @block.gpsimd
        def _(pool):
            made = [0]

            def step(ins):
                made[0] += 1
                ins.then_inc(const, 1)
                pool.wait_ge(const, made[0])

            def select(view, pattern, base, cm, op=ALU.is_ge, fill=0.0):
                step(pool.affine_select(out=view, in_=view, compare_op=op, fill=fill, base=base, pattern=pattern,
                                        channel_multiplier=cm))

            step(pool.memset(ident[:], 0.0))
            select(ident[:], [[-1, P]], 0, 1, ALU.not_equal, 1.0)
            step(pool.memset(par_rows[:], 0.0))
            step(pool.memset(dw_rows[:], 0.0))
            n_const["rows"] = made[0]
            with nc.allow_non_contiguous_dma(reason="small parameters, loaded once"):
                param_rows(pool, par_in_pool, (A["conv_dw_bias"], C_DWB), (A["conv_gn_gain"], C_GG), (A["conv_gn_bias"], C_GB))
                pool.dma_start(lam_rows[:], A["da_lambda"].rearrange("o a b -> o (a b)").to_broadcast([P, 4 * HD])).then_inc(lam_in, 16)
                pool.dma_start(router[:], A["moe_router"][0].rearrange("(c p) e -> p c e", p=P)).then_inc(rout_in, 16)
            step(pool.memset(ones[:], 1.0))
            step(pool.memset(mean_all[:], 1.0 / P))
            step(pool.memset(mean_64[:], 1.0 / HD))
            select(mean_64[:, 0:HD], [[0, HD]], HD - 1, -1)
            select(mean_64[:, HD:P], [[0, HD]], -HD, 1)
            step(pool.memset(ident_b[:], 0.0))
            select(ident_b[:], [[-1, P]], 0, 1, ALU.not_equal, 1.0)
            step(pool.memset(mask_b[:], 0.0))
            select(mask_b[:], [[-1, P]], 0, 1, ALU.is_ge, NEG)
            step(pool.memset(ident_h[:], 0.0))
            select(ident_h[:], [[-1, P]], 0, 1, ALU.not_equal, 1.0)
            step(pool.memset(conv_in[:, :, 0:TAPS - 1], 0.0))
            step(pool.memset(before[:], 1.0))
            select(before[:], [[1, P]], -1, -1)
            for r in range(2):
                step(pool.iota(slot_no[:, r, :], pattern=[[1, P]], base=CAP * r, channel_multiplier=0,
                               allow_small_or_imprecise_dtypes=True))
                if CAP < P:
                    step(pool.memset(slot_no[:, r, CAP:P], -5.0))
            step(pool.iota(expert_no[:], pattern=[[-1, NE]], base=NE, channel_multiplier=0,
                           allow_small_or_imprecise_dtypes=True))
            n_const["early"] = made[0]
            for u in range(POOL_FROM, POOL_TO):
                if u == POOL_TO - 1:
                    pool.wait_ge(par_cp, 2)
                    for c in range(2):
                        for k in range(PE_TAPS):
                            col = (TAPS - PE_TAPS + k) * 4 + 2 + c
                            pool.tensor_scalar(diag[:, c * PE_TAPS + k, :], ident[:], dw[:, col:col + 1], None, ALU.mult).then_inc(c_diag, 1)
                split_low(pool, u)
            step(pool.memset(span[:].bitcast(F32), 1.0))
            step(pool.memset(lmask[:], 0))
            for n, h in enumerate(LEVELS):
                nb = P // (2 * h)
                for view in ([span[:, n // 2, n % 2, :]] if n < 6 else [span[:, 3, 0, :], span[:, 4, 0, :]]):
                    v = view.rearrange("p (b s r) -> p b s r", s=2, r=h)
                    select(v[:, :, 1, :], [[-2 * h, nb], [0, h]], -h, 1)
                    select(v[:, :, 1, :], [[2 * h, nb], [1, h]], h, -1)
                    select(v[:, :, 0, :], [[-2 * h, nb], [-1, h]], -1, 1)
                    select(v[:, :, 0, :], [[2 * h, nb], [0, h]], h - 1, -1)
                v = lmask[:, n, :].rearrange("p (b s r) -> p b s r", s=2, r=h)
                step(pool.memset(v[:, :, 1, :], 1))
                select(v[:, :, 1, :], [[-2 * h, nb], [0, h]], 0, 1)
                select(v[:, :, 1, :], [[2 * h, nb], [0, h]], h - 1, -1)
            select(span[:, 3, 1, :], [[-1, P]], -1, 1)
            select(span[:, 4, 1, :], [[1, P]], 0, -1)
            n_const["all"] = made[0]

            def gate_gain(heads):
                for h in heads:
                    pool.tensor_scalar(gate_t[:, h, :], gate_t[:, h, :], par[:, C_HN + h:C_HN + h + 1], None,
                                       ALU.mult).then_inc(hg_gg, 1)

            pool.wait_ge(hg_ev, 15)
            gate_gain(range(HH - 2))
            pool.wait_ge(hg_z, 2)
            pool.wait_ge(hg_d, 12)
            for g in range(GROUPS):
                p, hp, tt = g // 8, (g // 2) % 4, g % 2
                pool.wait_ge(sp_e, g + 1)
                if g >= 2:
                    pool.wait_ge(sp_s, last_scores(g))
                k = key_t[:, 2 * hp:2 * hp + 2, tt * P:(tt + 1) * P]
                for li in range(2):
                    if 2 * p + li < 7:
                        h = LEVELS[2 * p + li]
                        ins = pool.tensor_tensor(half_of(level_of(dk, g, li), h, 0), half_of(k, h, 0),
                                                 half_of(level_of(decay, g, li), h, 0), ALU.mult)
                    elif tt == 0:
                        ins = pool.tensor_tensor(level_of(dk, g, li), k, level_of(decay, g, li), ALU.mult)
                ins.then_inc(sp_k, 1)
            pool.wait_ge(hg_ev, 20)
            gate_gain((HH - 2, HH - 1))
            pool.wait_ge(o_ms, 4)
            pool.dma_start(gain_row[:], A["ffn_norm"][1:2, :].to_broadcast([P, D])).then_inc(gain_in, 16)
            pool.wait_ge(gain_in, 16)
            for tt in range(TT):
                pool.wait_ge(n_xn, 2 * 3 + tt + 1)
                pool.tensor_tensor(x_g[:, tt, :], xn[:, tt, :], gain_row[:], ALU.mult).then_inc(x_gain, 1)
            for part in range(2):
                for tt in range(TT):
                    pool.wait_ge(x_part, 2 * part + tt + 1)
                    dst = x_g[:, tt, :] if part == 0 else x_b[:, 2, tt, :]
                    pool.tensor_tensor(dst, x_g[:, tt, :], x_b[:, part, tt, :], ALU.subtract).then_inc(x_gain, 1)

        @block.sync
        def _(sp):
            for tt in range(TT):
                sp.dma_start(x[:, tt, :], A["x"][0, tt * P:(tt + 1) * P, :]).then_inc(x_in, 16)
            sp.wait_ge(const, n_const["rows"])
            with nc.allow_non_contiguous_dma(reason="small parameters, loaded once"):
                sp.dma_start(dw_rows[0:TAPS * 4, :], A["conv_dw"].rearrange("o k (c p) -> (o k c) p", p=P)).then_inc(par_in, 16)
                param_rows(sp, par_in, (A["ffn_norm"], C_FFN), (A["hgrn_norm"], C_HN), (A["hgrn_lb_logits"], C_LB))
            for i in range(N_AB_IN):
                load(sp, U_AB_IN + i, as_in, ab_in[:, :, AB_ORDER[i]:AB_ORDER[i] + UC])
            for i in range(N_OUT):
                load(sp, U_AB_OUT + i, as_out, ab_out[i])

            def ffn_ab(u0, step, rounds=0):
                load(sp, u0, as_in, ffn_in[:, :, bass.ds(step * UC, UC)], rounds)
                load(sp, u0 + 1, as_in, ffn_in[:, :, bass.ds(step * UC + FFN_UP, UC)], rounds)

            ffn_ab(U_FFN, 0)
            ffn_ab(U_FFN + 2, 1)
            load(sp, U_FFN + 4, as_out, ffn_out[0])
            with sp.Fori(0, 4) as j:
                for k in (0, 1):
                    u0 = U_FFN + 5 + 3 * k
                    ffn_ab(u0, j * 2 + (2 + k), j)
                    load(sp, u0 + 2, as_out, ffn_out[j * 2 + (1 + k)], j)
            ffn_ab(U_FFN + 29, 10)
            load(sp, U_FFN + 31, as_out, ffn_out[9])
            load(sp, U_FFN + 32, as_out, ffn_out[10])
            for i in range(N_HG_IN):
                load(sp, U_HG_IN + i, as_in, hg_in[:, :, HG_ORDER[i]:HG_ORDER[i] + UC])
            for i in range(N_OUT):
                load(sp, U_HG_OUT + i, as_out, hg_out[i])

            w1, w2 = A["moe_w_in"][0], A["moe_w_out"][0]

            def moe_a(u0, e, step, rounds):
                load(sp, u0, as_in, in_cols(w1[e])[:, :, bass.ds(step * UC, UC)], rounds)

            def moe_b(u0, e, step, rounds):
                load(sp, u0, as_in, in_cols(w1[e])[:, :, bass.ds(step * UC + MOE_UP, UC)], rounds)

            def moe_c(u0, e, step, rounds):
                load(sp, u0, as_out, out_rows(w2[e])[step], rounds)

            def expert(u, e, nxt, rounds):
                moe_b(u + 3, e, 1, rounds)
                moe_c(u + 4, e, 0, rounds)
                with sp.Fori(0, 6) as j:
                    for k in (0, 1):
                        moe_a(u + 5 + 3 * k, e, j * 2 + (2 + k), rounds + j)
                        moe_b(u + 6 + 3 * k, e, j * 2 + (2 + k), rounds + j)
                        moe_c(u + 7 + 3 * k, e, j * 2 + (1 + k), rounds + j)
                moe_c(u + 41, e, 13, rounds)
                moe_a(u + 42, nxt, 0, rounds)
                moe_b(u + 43, nxt, 0, rounds)
                moe_a(u + 44, nxt, 1, rounds)

            def moe_round(r):
                u = U_MOE + r * NE * MOE_UNITS
                with sp.Fori(0, NE - 1) as e:
                    expert(u, e, e + 1, e * 7)
                expert(u, NE - 1, 0, 7 * (NE - 1))

            moe_a(U_MOE, 0, 0, 0)
            moe_b(U_MOE + 1, 0, 0, 0)
            moe_a(U_MOE + 2, 0, 1, 0)
            moe_round(0)
            sp.wait_ge(r_flag, 1)
            over = sp.value_load(flag[0:1, 0:1], min_val=0, max_val=1)
            with sp.If(over > 0):
                moe_round(1)
            for tt in range(TT):
                sp.wait_ge(m_add, over * (4 * (NE + 1)) + (4 * NE + 3 + 2 * tt))
                sp.dma_start(out[0, tt * P:(tt + 1) * P, :], x[:, tt, :]).then_inc(stored, 16)
            sp.wait_ge(stored, 16 * TT)

        @block.vector
        def _(dve):
            dve.memset(eps[:], EPS).then_inc(dve_const, 1)
            def norm_scale(n):
                dve.wait_ge(n_rs, n + 1)
                for tt in range(TT):
                    dve.tensor_scalar(xn[:, tt, :], x[:, tt, :], n_stat[:, n, 2, tt:tt + 1], None, ALU.mult).then_inc(n_xn, 1)

            def norm_low(n, col):
                for j in range(4):
                    dve.wait_ge(n_high, 8 * n + 2 * j + 2)
                    b = j if n == 3 else 4 + j
                    for c in range(2):
                        dve.scalar_tensor_tensor(out=h_l[:, 2 * j + c, :], in0=bank[:, b, c * T:(c + 1) * T],
                                                 scalar=par[:, col + 2 * j + c:col + 2 * j + c + 1], in1=h_h[:, 2 * j + c, :],
                                                 op0=ALU.mult, op1=ALU.subtract).then_inc(n_low, 1)

            def residual(units):
                for tt in range(TT):
                    if tt == 0:
                        dve.wait_ge(o_part, {U_FFN: 1, U_HG_IN: 2, U_MOE: 3}[units])
                    else:
                        dve.wait_ge(w_used, units)
                    for half in range(2):
                        v = x[:, tt, half * 512:(half + 1) * 512]
                        dve.tensor_tensor(v, bank[:, 4 + 2 * tt + half, :], v, ALU.add).then_inc(x_add, 1)

            norm_scale(0)
            split_low(dve, 0)
            dve.wait_ge(par_t, 1)
            dve.tensor_copy(par[:], bank[:, 0, 0:P]).then_inc(par_cp, 1)
            dve.wait_ge(par_t, 2)
            dve.tensor_copy(dw[:], bank[:, 1, 0:P]).then_inc(par_cp, 1)
            dve.wait_ge(par_cp, 2)
            dve.tensor_scalar(par[:, C_SUB:C_SUB + 1], par[:, C_SUB:C_SUB + 1], 1.0 - LAM_INIT, None, ALU.mult).then_inc(sub_g, 1)
            norm_low(0, C_MIX)
            split_low(dve, 1)
            split_low(dve, 2)
            dve.wait_ge(lam_in, 16)
            for i in range(2):
                dve.tensor_tensor(lam_prod[:, i, :], lam_rows[:, 2 * i, :], lam_rows[:, 2 * i + 1, :], ALU.mult).then_inc(lam_d, 1)
            dve.wait_ge(lam_d, 2)
            dve.tensor_reduce(lam[:, 0:2], lam_prod[:], AX.X, ALU.add).then_inc(lam_d, 1)

            def conv_value(i):
                dve.wait_ge(c_s, i + 1)
                dve.tensor_tensor(conv_in[:, 2 * i:2 * i + 2, TAPS - 1:], bank[:, 0, :].rearrange("p (a t) -> p a t", a=2),
                                  sig[:].rearrange("p (a t) -> p a t", a=2), ALU.mult).then_inc(c_g, 1)

            def conv_taps(i, first, end):
                if first == 0:
                    dve.wait_ge(c_g, i + 1)
                    for c in (2 * i, 2 * i + 1):
                        dve.tensor_scalar(conv_y[:, c, :], conv_in[:, c, 0:T], dw[:, c:c + 1], par[:, C_DWB + c:C_DWB + c + 1],
                                          ALU.mult, ALU.add).then_inc(c_y, 1)
                    first = 1
                with dve.Fori(first, end) as k:
                    for c in (0, 1):
                        ch = 2 * i + c
                        dve.wait_ge(c_y, k * 2 + (2 * TAPS * i + c - 1))
                        dve.scalar_tensor_tensor(out=conv_y[:, ch, :], in0=conv_in[:, ch, bass.ds(k, T)],
                                                 scalar=dw[:, bass.ds(k * 4 + ch, 1)], in1=conv_y[:, ch, :],
                                                 op0=ALU.mult, op1=ALU.add).then_inc(c_y, 1)

            def qk_norm(i):
                dst, col = (q_t, C_QG) if i < 2 else (k_t, C_KG)
                dve.wait_ge(qk_rs, i + 1)
                dve.scalar_tensor_tensor(out=dst[:, 2 * (i % 2):2 * (i % 2) + 2, :],
                                         in0=q_raw[:, i, :].rearrange("p (a t) -> p a t", a=2), scalar=par[:, col:col + 1],
                                         in1=rs[:, i % 2, :].rearrange("p (a t) -> p a t", a=2),
                                         op0=ALU.mult, op1=ALU.mult).then_inc(q_n, 1)

            dve.wait_ge(const, n_const["early"])
            conv_value(0)
            conv_taps(0, 0, 10)
            conv_value(1)
            conv_taps(0, 10, TAPS)
            conv_taps(1, 0, 4)
            qk_norm(0)
            qk_norm(1)
            conv_taps(1, 4, 11)
            qk_norm(2)
            qk_norm(3)
            dve.wait_ge(lam_e, 1)
            dve.tensor_tensor(lam[:, 4:5], lam[:, 3:4], lam[:, 2:3], ALU.subtract).then_inc(lam_d, 1)
            dve.wait_ge(lam_d, 4)
            dve.tensor_scalar(lam[:, 5:6], lam[:, 4:5], -LAM_INIT, None, ALU.add).then_inc(lam_d, 1)

            def row_max(b):
                n, w, idx = (4, P, 4 * b) if b < 2 else (2, T, 8 + 2 * (b - 2))
                dve.wait_ge(s_sc, b + 1)
                dve.tensor_reduce(smx[:, idx:idx + n], bank[:, 2 + b, 0:n * w].rearrange("p (n w) -> p n w", n=n),
                                  AX.X, ALU.max).then_inc(s_mx, 1)
                dve.wait_ge(s_mx, b + 1)
                dve.tensor_scalar(nmx[:, idx:idx + n], smx[:, idx:idx + n], -HD ** -0.5, None, ALU.mult).then_inc(s_nm, 1)

            def weights(qt, pr):
                dve.wait_ge(s_ex, 8 * qt + 8)
                dve.reciprocal(rsum[:, 8 * qt:8 * qt + 8], ssum[:, 8 * qt:8 * qt + 8]).then_inc(s_rc, 1)
                dve.wait_ge(s_rc, 2 * qt + 1)
                dve.wait_ge(lam_d, 5)
                dve.tensor_scalar(rsum[:, 8 * qt + 4:8 * qt + 8], rsum[:, 8 * qt + 4:8 * qt + 8], lam[:, 5:6], None, ALU.mult).then_inc(s_rc, 1)
                dve.wait_ge(s_rc, 2 * qt + 2)
                for h in range(HEADS):
                    dve.wait_ge(s_p0, 4 * qt + h + 1)
                    dve.scalar_tensor_tensor(out=pr[:, 0, h, :], in0=pr[:, 1, h, :], scalar=rsum[:, 8 * qt + 4 + h:8 * qt + 5 + h],
                                             in1=pr[:, 0, h, :], op0=ALU.mult, op1=ALU.add).then_inc(s_w, 1)

            row_max(0)
            row_max(1)
            conv_taps(1, 11, 13)
            row_max(2)
            conv_taps(1, 13, 15)
            row_max(3)
            weights(0, p_0)
            row_max(4)
            row_max(5)
            conv_taps(1, 15, 17)
            weights(1, p_1)
            dve.wait_ge(c_pe, 1)
            dve.wait_ge(c_y, 2 * TAPS + 2 * 17)
            dve.tensor_tensor(conv_y[:, 2:4, :], bank[:, 0, :].rearrange("p (a t) -> p a t", a=2), conv_y[:, 2:4, :],
                              ALU.add).then_inc(c_sum, 1)
            dve.wait_ge(c_sum, 1)
            conv_taps(1, 17, TAPS - PE_TAPS)
            dve.wait_ge(sub_g, 1)
            for b in range(2):
                dve.wait_ge(a_rs, b + 1)
                dve.scalar_tensor_tensor(out=q_raw[:, b, :], in0=bank[:, 6 + b, :], scalar=par[:, C_SUB:C_SUB + 1], in1=rs[:, b, :],
                                         op0=ALU.mult, op1=ALU.mult).then_inc(a_of, 1)
            for b in range(2):
                dve.wait_ge(a_h, b + 1)
                dve.tensor_tensor(h_l[:, 2 * b:2 * b + 2, :], q_raw[:, b, :].rearrange("p (a t) -> p a t", a=2),
                                  h_h[:, 2 * b:2 * b + 2, :], ALU.subtract).then_inc(a_l, 1)
            for b in range(2):
                dve.wait_ge(g_m, b + 1)
                v = conv_y[:, 2 * b:2 * b + 2, :]
                dve.tensor_tensor(v, v, bank[:, 2 + b, :].rearrange("p (a t) -> p a t", a=2), ALU.subtract).then_inc(g_c, 1)
            for b in range(2):
                dve.wait_ge(g_rs, b + 1)
                v = conv_y[:, 2 * b:2 * b + 2, :]
                dve.tensor_tensor(v, v, rs[:, b, :].rearrange("p (a t) -> p a t", a=2), ALU.mult).then_inc(g_n, 1)
            for b in range(2):
                dve.wait_ge(g_h, b + 1)
                dve.tensor_tensor(h_l[:, 4 + 2 * b:6 + 2 * b, :], conv_y[:, 2 * b:2 * b + 2, :], h_h[:, 4 + 2 * b:6 + 2 * b, :],
                                  ALU.subtract).then_inc(g_l, 1)
            dve.wait_ge(r_high, 1)
            dve.tensor_tensor(router_l[:], router[:], router_h[:], ALU.subtract).then_inc(r_low, 1)
            for u in range(U_AB_OUT, U_FFN - 1):
                split_low(dve, u + 3)
            residual(U_FFN)

            norm_scale(1)
            split_low(dve, U_FFN + 2)
            norm_low(1, C_FFN)

            def ffn_mul(s0, j2, par_s, used):
                dve.wait_ge(w_used, used)
                dve.wait_ge(f_silu, j2 + (s0 + 1))
                if s0:
                    dve.wait_ge(f_low, j2 + s0)
                dve.tensor_tensor(act_f[:], silu_g[:], bank[:, 2 + par_s, :], ALU.mult).then_inc(f_mul, 1)

            def ffn_low(s0, j2, par_s):
                dve.wait_ge(f_high, j2 + (s0 + 1))
                dve.tensor_tensor(act_l[:, par_s, :], act_f[:], act_h[:, par_s, :], ALU.subtract).then_inc(f_low, 1)

            def ffn_step(s0, j, par_s, last=False):
                ffn_mul(s0, j * 2, par_s, j * 6 + (U_FFN + (3 * s0 + 1 if s0 else 2)))
                split_low(dve, U_FFN + 3 * s0 + 3, j)
                ffn_low(s0, j * 2, par_s)
                split_low(dve, U_FFN + 3 * s0 + 4, j)
                if not last:
                    split_low(dve, U_FFN + 3 * s0 + 5, j)

            ffn_step(0, 0, 0)
            ffn_step(1, 0, 1)
            with dve.Fori(0, 4) as j:
                ffn_step(2, j, 0)
                ffn_step(3, j, 1)
            ffn_step(10, 0, 0, True)
            residual(U_HG_IN)

            norm_scale(2)
            split_low(dve, U_HG_IN + 2)
            norm_low(2, C_MIX + 8)
            dve.tensor_tensor(lb[:, 0, :], par[:, C_LB:C_LB + HH], par[:, C_LB:C_LB + HH], ALU.subtract).then_inc(lb_d, 1)
            dve.wait_ge(lb_d, 2)
            dve.reciprocal(lb[:, 2, :], lb[:, 1, :]).then_inc(lb_d, 1)
            dve.wait_ge(lb_d, 3)
            dve.tensor_tensor(lb[:, 3, :], lb[:, 1, :], lb[:, 2, :], ALU.mult).then_inc(lb_d, 1)
            dve.wait_ge(lb_d, 4)
            dve.tensor_tensor(lb[:, 0, :], lb[:, 3, :], lb[:, 3, :], ALU.subtract).then_inc(lb_d, 1)
            dve.wait_ge(lb_d, 5)
            dve.tensor_scalar(lb[:, 4, :], lb[:, 0, :], -1.0, 1.0, ALU.mult, ALU.add).then_inc(lb_d, 1)
            dve.memset(dq[:], 0.0).then_inc(hg_z, 1)
            dve.memset(dk[:], 0.0).then_inc(hg_z, 1)
            dve.wait_ge(lb_d, 6)
            for i in range(N_HG_IN - 1):
                if i < 4:
                    dve.wait_ge(hg_ev, 2 * i + 2)
                    for h in (2 * i, 2 * i + 1):
                        dve.tensor_scalar(log_f[:, h, :], log_f[:, h, :], lb[:, 4, h:h + 1], lb[:, 0, h:h + 1],
                                          ALU.mult, ALU.add).then_inc(hg_z, 1)
                        dve.tensor_scalar(key_t[:, h, :], key_t[:, h, :], lb[:, 4, h:h + 1], None, ALU.mult).then_inc(hg_d, 1)
                    dve.wait_ge(hg_z, 2 * i + 4)
                    dve.tensor_scalar(log_f[:, 2 * i:2 * i + 2, :], log_f[:, 2 * i:2 * i + 2, :], 1.2e-38, None, ALU.max).then_inc(hg_d, 1)
                split_low(dve, U_HG_IN + i + 3)
                if i == 13:
                    for q in range(4):
                        tt, hq = q // 2, q % 2
                        dve.wait_ge(hg_h, q + 1)
                        v = slice(hq * 512, (hq + 1) * 512)
                        dve.tensor_tensor(lf_l[:, tt, v], bank[:, 2 + q, :], lf_h[:, tt, v], ALU.subtract).then_inc(hg_l, 1)
            for q in range(4):
                tt, hq = q // 2, q % 2
                dve.wait_ge(hd, q + 1)
                dve.tensor_tensor(att[:, 4 * hq:4 * hq + 4, 2 * tt, :], bank[:, 2 + q, :].rearrange("p (h t) -> p h t", h=4),
                                  ident[:].unsqueeze(1).to_broadcast([P, 4, P]), ALU.mult).then_inc(hd_cp, 1)

            def decayed(g):
                p, hp, tt = g // 8, (g // 2) % 4, g % 2
                dve.wait_ge(sp_e, g + 1)
                if g >= 2:
                    dve.wait_ge(sp_s, last_scores(g))
                q = qry_t[:, 2 * hp:2 * hp + 2, tt * P:(tt + 1) * P]
                for li in range(2):
                    if 2 * p + li < 7:
                        h = LEVELS[2 * p + li]
                        ins = dve.tensor_tensor(level_of(dq, g, li)[:, :, 0:P // 2].rearrange("p a (b r) -> p a b r", r=h),
                                                half_of(q, h, 1), half_of(level_of(decay, g, li), h, 1), ALU.mult)
                    elif tt == 1:
                        ins = dve.tensor_tensor(level_of(dq, g, li), q, level_of(decay, g, li), ALU.mult)
                ins.then_inc(sp_m, 1)

            def keep(g, li):
                p, hp, tt = g // 8, (g // 2) % 4, g % 2
                b = bank[:, 2 + g % 4, :].rearrange("p (a l t) -> p a l t", a=2, l=2)[:, :, li, :]
                h = LEVELS[min(2 * p + li, 6)]
                if li == 0:
                    dve.wait_ge(sp_s, g + 1)
                    if g >= 8:
                        dve.wait_ge(sp_c1, second(g - 8))
                else:
                    dve.wait_ge(sp_c0, g + 1)
                if 2 * p + li < 7:
                    mask = lmask[:, 2 * p + li, :].rearrange("p (b s r) -> p b s r", s=2, r=h)[:, :, 1, :]
                    dve.copy_predicated(half_of(att[:, 2 * hp:2 * hp + 2, 2 * tt, :], h, 1),
                                        mask.unsqueeze(1).to_broadcast([P, 2, P // (2 * h), h]),
                                        b[:, :, 0:P // 2].rearrange("p a (b r) -> p a b r", r=h)).then_inc((sp_c0, sp_c1)[li], 1)
                elif tt == 1:
                    dve.tensor_copy(att[:, 2 * hp:2 * hp + 2, 1, :], b).then_inc(sp_c1, 1)

            dve.wait_ge(const, n_const["all"])
            dve.wait_ge(hd_cp, 4)
            decayed(0)
            for g in range(GROUPS):
                if g + 1 < GROUPS:
                    decayed(g + 1)
                keep(g, 0)
                if g:
                    keep(g - 1, 1)
            keep(GROUPS - 1, 1)
            dve.wait_ge(hg_gg, HH - 2)

            def hg_low(j):
                dve.wait_ge(o_h, j + 1)
                dve.tensor_tensor(h_l[:, 2 * j:2 * j + 2, :], o_nrm(j).rearrange("p (a t) -> p a t", a=2),
                                  h_h[:, 2 * j:2 * j + 2, :], ALU.subtract).then_inc(o_l, 1)

            for j in range(4):
                dve.wait_ge(o_rs, j + 1)
                dve.tensor_tensor(o_nrm(j), bank[:, O_BANK[j], :], o_inv(j), ALU.mult).then_inc(o_n, 1)
                if j >= 1:
                    hg_low(j - 1)
                if j == 3:
                    split_low(dve, U_HG_OUT + 2)
                    dve.wait_ge(hg_gg, HH)
                dve.wait_ge(o_n, j + 1)
                v = o_nrm(j).rearrange("p (a t) -> p a t", a=2)
                dve.tensor_tensor(v, v, gate_t[:, 2 * j:2 * j + 2, :], ALU.mult).then_inc(o_g, 1)
            hg_low(3)
            for u in range(U_HG_OUT, U_MOE - 1):
                split_low(dve, u + 3)
            residual(U_MOE)

            norm_scale(3)
            split_low(dve, U_MOE + 2)
            norm_low(3, C_FFN + 8)
            done = [0]

            def step(ins):
                done[0] += 1
                ins.then_inc(r_d, 1)
                dve.wait_ge(r_d, done[0])

            def wide(v):
                return v.unsqueeze(2).to_broadcast([P, TT, NE])

            ordr = expert_no[:].unsqueeze(1).to_broadcast([P, TT, NE])
            dve.wait_ge(r_lt, 1)
            dve.tensor_copy(logit_t[:], bank[0:NE, 4, 0:T]).then_inc(r_lc, 1)
            dve.wait_ge(r_lg, 1)
            step(dve.tensor_copy(logit[:, 0, :, :], bank[:, 5, 0:TT * NE].rearrange("p (a e) -> p a e", a=TT)))
            for k in range(2):
                src, sl = logit[:, 2 * k + 0, :, :] if k == 0 else logit[:, 3, :, :], logit[:, 4 + k, :, :]
                step(dve.tensor_reduce(pick[:, k, :], src, AX.X, ALU.max))
                step(dve.tensor_tensor(logit[:, 1, :, :], src, wide(pick[:, k, :]), ALU.is_ge))
                step(dve.tensor_tensor(logit[:, 2, :, :], logit[:, 1, :, :], ordr, ALU.mult))
                step(dve.tensor_reduce(pick[:, 2 + k, :], logit[:, 2, :, :], AX.X, ALU.max))
                step(dve.tensor_tensor(sl, ordr, wide(pick[:, 2 + k, :]), ALU.is_equal))
                if k == 0:
                    step(dve.scalar_tensor_tensor(out=logit[:, 3, :, :], in0=sl, scalar=-3.0e38, in1=src, op0=ALU.mult, op1=ALU.add))
            step(dve.tensor_tensor(pick[:, 4, :], pick[:, 1, :], pick[:, 0, :], ALU.subtract))
            n_const["exp"] = done[0]
            step(dve.tensor_tensor(logit[:, 6, :, :], logit[:, 4, :, :], logit[:, 5, :, :], ALU.add))
            n_const["sel"] = done[0]
            dve.wait_ge(r_e, 1)
            step(dve.tensor_scalar(pick[:, 6, :], pick[:, 5, :], 1.0, None, ALU.add))
            step(dve.reciprocal(pick[:, 7, :], pick[:, 6, :]))
            step(dve.tensor_tensor(pick[:, 8, :], pick[:, 5, :], pick[:, 7, :], ALU.mult))
            step(dve.tensor_tensor(logit[:, 7, :, :], logit[:, 4, :, :], wide(pick[:, 7, :]), ALU.mult))
            step(dve.tensor_tensor(logit[:, 8, :, :], logit[:, 5, :, :], wide(pick[:, 8, :]), ALU.mult))
            step(dve.memset(comb[:], 0.0))
            step(dve.memset(rank[:], -1.0))
            step(dve.tensor_tensor(comb[:].rearrange("p (a e) -> p a e", a=TT)[:, :, 1:], logit[:, 7, :, :], logit[:, 8, :, :], ALU.add))
            dve.wait_ge(r_rank, 1)
            step(dve.scalar_tensor_tensor(out=logit[:, 9, :, :], in0=bank[:, 4, 0:TT * NE].rearrange("p (a e) -> p a e", a=TT), scalar=1.0,
                                          in1=logit[:, 6, :, :], op0=ALU.add, op1=ALU.mult))
            step(dve.tensor_scalar(rank[:].rearrange("p (a e) -> p a e", a=TT)[:, :, 0:NE], logit[:, 9, :, :], -1.0, None, ALU.add))
            dve.memset(pick[:, 11, :], 0.0).then_inc(m_add, 1)

            def choose(e, r, n):
                for tt in range(TT):
                    dve.tensor_scalar(sel[:, tt, :], slot_no[:, r, :], rank[:, bass.ds(e + tt * (NE + 1), 1)], None,
                                      ALU.is_equal).then_inc(m_sel, 1)

            def residual_part(e, tt, n):
                for half in range(2):
                    dve.wait_ge(m_sc, n * 4 + (2 * tt + half + 1))
                    v = x[:, tt, half * 512:(half + 1) * 512]
                    dve.scalar_tensor_tensor(out=v, in0=bank[:, 5 + half, :], scalar=comb[:, bass.ds(e + tt * (NE + 1), 1)], in1=v,
                                             op0=ALU.mult, op1=ALU.add).then_inc(m_add, 1)

            def gather_low(n):
                for j in range(2):
                    dve.wait_ge(m_hh, n * 2 + (j + 1))
                    dve.tensor_tensor(hs_l[:, 4 * j:4 * j + 4, :], bank[:, 5 + j, :].rearrange("p (c t) -> p c t", c=4),
                                      hs_h[:, 4 * j:4 * j + 4, :], ALU.subtract).then_inc(m_hl, 1)

            def moe_mul(g, b):
                dve.wait_ge(m_si, g + 1)
                dve.tensor_tensor(m_act[:], m_silu[:], bank[:, b, UC:2 * UC], ALU.mult).then_inc(m_mul, 1)

            def moe_low(g, b):
                dve.wait_ge(m_ah, g + 1)
                dve.tensor_tensor(ma_l[:, b, :], bank[:, 2, 0:UC], ma_h[:, b, :], ALU.subtract).then_inc(m_al, 1)

            def moe_step(u, k, gs, rounds, last=False):
                moe_mul(gs, (1 + k) % 2)
                split_low(dve, u + 6 + 3 * k, rounds)
                split_low(dve, u + 7 + 3 * k, rounds)
                moe_low(gs, (1 + k) % 2)
                if last:
                    moe_mul(gs + 1, k % 2)
                split_low(dve, u + 8 + 3 * k, rounds)

            def moe_round(r):
                u = U_MOE + r * NE * MOE_UNITS
                g0 = r * NE * MOE_STEPS
                n0 = r * (NE + 1)
                if r:
                    dve.wait_ge(m_pt, n0)
                choose(0, r, n0)
                if r == 0:
                    step(dve.tensor_reduce(pick[:, 9, 0:1], bank[:, 4, TT * NE:(TT + 1) * NE], AX.X, ALU.max))
                    step(dve.tensor_scalar(pick[:, 10, 0:1], pick[:, 9, 0:1], CAP + 0.5, None, ALU.is_gt))
                    dve.tensor_copy(flag[:], pick[:, 10, 0:1]).then_inc(r_flag, 1)
                dve.memset(scat[:].bitcast(F32), 0.0).then_inc(m_scat, 1)
                dve.memset(y_h[:].bitcast(F32), 0.0).then_inc(m_yl, 1)
                dve.memset(y_l[:].bitcast(F32), 0.0).then_inc(m_yl, 1)
                gather_low(n0)
                with dve.Fori(0, NE) as e:
                    q = e * 7
                    g = e * MOE_STEPS + g0
                    n = e + n0
                    split_low(dve, u + 3, q)
                    moe_mul(g, 0)
                    residual_part(e, 0, n)
                    split_low(dve, u + 4, q)
                    moe_low(g, 0)
                    split_low(dve, u + 5, q)
                    residual_part(e, 1, n)
                    dve.wait_ge(m_pt, e + (n0 + 1))
                    choose(e + 1, r, n + 1)
                    with dve.Fori(0, 5) as j:
                        for k in (0, 1):
                            moe_step(u, k, g + j * 2 + (1 + k), q + j)
                    for k in (0, 1):
                        moe_step(u + 5 * 6, k, g + (11 + k), q, k == 1)
                    gather_low(n + 1)
                    moe_low(g + 13, 1)
                    split_low(dve, u + 42, q)
                    split_low(dve, u + 43, q)
                    for j in range(2):
                        dve.wait_ge(m_yh, e * 2 + (r * NE * 2 + j + 1))
                        dve.tensor_tensor(y_l[:, j * 512:(j + 1) * 512], bank[:, 3 + j, :],
                                          y_h[:, j * 512:(j + 1) * 512], ALU.subtract).then_inc(m_yl, 1)
                    split_low(dve, u + 44, q)
                for tt in range(TT):
                    residual_part(NE, tt, NE + n0)

            moe_round(0)
            over = dve.value_load(flag[0:1, 0:1], min_val=0, max_val=1)
            with dve.If(over > 0):
                moe_round(1)

        @block.scalar
        def _(act):
            act.wait_ge(const, n_const["rows"])
            with nc.allow_non_contiguous_dma(reason="small parameters, loaded once"):
                param_rows(act, par_in, (A["mix_norm"], C_MIX), (A["da_subln"], C_SUB))
                for c in (0, 1):
                    act.dma_start(par_rows[C_QG:C_QG + 1, c * HD:(c + 1) * HD], A["da_q_gain"]).then_inc(par_in, 16)
                    act.dma_start(par_rows[C_KG:C_KG + 1, c * HD:(c + 1) * HD], A["da_k_gain"]).then_inc(par_in, 16)

            tables = [0]

            def table(func):
                act.activation(warm[:, tables[0]:tables[0] + 1], eps[:], func)
                tables[0] += 1

            def norm_sums(n):
                act.wait_ge(dve_const, 1)
                table(ACT.Ln)
                for tt in range(TT):
                    if n == 0:
                        act.wait_ge(x_in, 16 * TT)
                    else:
                        act.wait_ge(x_add, 4 * (n - 1) + 2 * (tt + 1))
                        act.wait_ge(n_t, 4 * n)
                    act.activation(xn[:, tt, :], x[:, tt, :], ACT.Square, accum_out=n_stat[:, n, 0, tt:tt + 1]).then_inc(n_sq, 1)
                act.wait_ge(n_sq, TT * (n + 1))
                act.activation(n_stat[:, n, 1, :], n_stat[:, n, 0, :], ACT.Ln, scale=1.0 / D, bias=eps[:]).then_inc(n_ln, 1)
                act.wait_ge(n_ln, n + 1)
                act.activation(n_stat[:, n, 2, :], n_stat[:, n, 1, :], ACT.Exp, scale=-0.5).then_inc(n_rs, 1)

            def norm_high(n, col):
                if n == 0:
                    act.wait_ge(par_cp, 1)
                for j in range(4):
                    act.wait_ge(n_t, 4 * n + j + 1)
                    b = j if n == 3 else 4 + j
                    for c in range(2):
                        act.activation(h_h[:, 2 * j + c, :], bank[:, b, c * T:(c + 1) * T], ACT.Copy,
                                       scale=par[:, col + 2 * j + c:col + 2 * j + c + 1]).then_inc(n_high, 1)

            def inv_rms(n, count, src, dst, ready, ln, rs_sem, before=None):
                for i in range(n, n + count):
                    act.wait_ge(ready, i + 1)
                    if before is not None and before(i):
                        act.wait_ge(*before(i))
                    act.activation(dst(i), src(i), ACT.Ln, bias=eps[:]).then_inc(ln, 1)
                for i in range(n, n + count):
                    act.wait_ge(ln, i + 1)
                    act.activation(dst(i), dst(i), ACT.Exp, scale=-0.5).then_inc(rs_sem, 1)

            norm_sums(0)
            table(ACT.Sigmoid)
            split_high(act, 0)
            norm_high(0, C_MIX)
            split_high(act, 1)
            split_high(act, 2)

            def qk_inv(i):
                inv_rms(i, 2, lambda i: bank[:, 6 + i % 2, :], lambda i: rs[:, i % 2, :], qk_ms, qk_ln, qk_rs,
                        lambda i: (q_n, i - 1) if i >= 2 else None)

            def values(u):
                act.activation(v_n[:, :, (u - 8) * UC:(u - 7) * UC], bank[:, u % 2, :].rearrange("p (a f) -> p a f", a=TT),
                               ACT.Copy).then_inc(v_cp, 1)

            for u in range(N_AB_IN - 1):
                act.wait_ge(w_used, u + 1)
                if u in (1, 3):
                    if u == 3:
                        act.wait_ge(c_g, 1)
                    act.activation(sig[:], bank[:, 1, :], ACT.Sigmoid).then_inc(c_s, 1)
                if 4 <= u < 8:
                    i = u - 4
                    if i >= 2:
                        act.wait_ge(qk_ms, i - 1)
                    act.activation(q_raw[:, i, :], bank[:, u % 2, :], ACT.Copy).then_inc(qk_raw, 1)
                    act.activation(sq[:, i % 2, :], bank[:, u % 2, :], ACT.Square).then_inc(qk_sq, 1)
                if u == 8:
                    values(u)
                split_high(act, u + 3)
                if u in (6, 7):
                    qk_inv(2 * (u - 6))
            act.wait_ge(lam_d, 3)
            act.activation(lam[:, 2:4], lam[:, 0:2], ACT.Exp).then_inc(lam_e, 1)
            def numerators(b):
                act.wait_ge(s_nm, b + 1)
                n = 4 if b < 2 else 2
                for g in range(n):
                    idx = 4 * b + g if b < 2 else 8 + 2 * (b - 2) + g
                    c, h = (b, g) if b < 2 else ((b - 2) // 2, 2 * ((b - 2) % 2) + g)
                    w = P if b < 2 else T
                    dst = p_0[:, c, h, :] if b < 2 else p_1[:, c, h, :]
                    act.activation(dst, bank[:, 2 + b, g * w:(g + 1) * w], ACT.Exp, scale=HD ** -0.5,
                                   bias=nmx[:, idx:idx + 1], accum_out=ssum[:, idx:idx + 1]).then_inc(s_ex, 1)

            def scaled(qt, pr):
                act.wait_ge(s_rc, 2 * qt + 1)
                for h in range(HEADS):
                    act.activation(pr[:, 0, h, :], pr[:, 0, h, :], ACT.Copy,
                                   scale=rsum[:, 8 * qt + h:8 * qt + h + 1]).then_inc(s_p0, 1)

            for b in range(4):
                numerators(b)
            scaled(0, p_0)
            numerators(4)
            numerators(5)
            scaled(1, p_1)
            act.wait_ge(w_used, N_AB_IN)
            values(N_AB_IN - 1)
            split_high(act, N_AB_IN + 2)
            table(ACT.Ln)
            for h in range(HEADS):
                act.wait_ge(a_t, h + 1)
                act.activation(w_t[:, h, :], bank[:, 2 + h, 0:384], ACT.Copy).then_inc(a_wt, 1)
            act.wait_ge(qk_ms, 4)
            for b in range(2):
                act.wait_ge(a_o, b + 1)
                act.activation(sq[:, b, :], bank[:, 6 + b, :], ACT.Square).then_inc(a_sq, 1)
            inv_rms(0, 2, lambda b: bank[:, b, :], lambda b: rs[:, b, :], a_ms, a_ln, a_rs, lambda b: (q_n, 4))
            for b in range(2):
                act.wait_ge(a_of, b + 1)
                act.activation(h_h[:, 2 * b:2 * b + 2, :], q_raw[:, b, :].rearrange("p (a t) -> p a t", a=2), ACT.Copy).then_inc(a_h, 1)
            table(ACT.Ln)
            for b in range(2):
                act.wait_ge(g_c, b + 1)
                act.wait_ge(a_ms, b + 1)
                act.activation(sq[:, b, :].rearrange("p (a t) -> p a t", a=2), conv_y[:, 2 * b:2 * b + 2, :], ACT.Square).then_inc(g_sq, 1)
            inv_rms(0, 2, lambda b: bank[:, 2 + b, :], lambda b: rs[:, b, :], g_v, g_ln, g_rs, lambda b: (a_of, b + 1))
            table(ACT.Silu)
            for b in range(2):
                act.wait_ge(g_n, b + 1)
                for c in (2 * b, 2 * b + 1):
                    act.activation(conv_y[:, c, :], conv_y[:, c, :], ACT.Silu, scale=par[:, C_GG + c:C_GG + c + 1],
                                   bias=par[:, C_GB + c:C_GB + c + 1]).then_inc(g_s, 1)
                act.wait_ge(g_s, 2 * b + 2)
                act.activation(h_h[:, 4 + 2 * b:6 + 2 * b, :], conv_y[:, 2 * b:2 * b + 2, :], ACT.Copy).then_inc(g_h, 1)
            act.wait_ge(rout_in, 16)
            act.activation(router_h[:], router[:], ACT.Copy).then_inc(r_high, 1)
            for u in range(U_AB_OUT, U_FFN - 1):
                split_high(act, u + 3)

            norm_sums(1)
            table(ACT.Silu)
            split_high(act, U_FFN + 2)
            norm_high(1, C_FFN)

            def ffn_gate(s0, j2, s_par, a_used):
                act.wait_ge(w_used, a_used)
                if not (isinstance(j2, int) and s0 + j2 == 0):
                    act.wait_ge(f_mul, s0 + j2)
                act.activation(silu_g[:], bank[:, s_par, :], ACT.Silu).then_inc(f_silu, 1)

            def ffn_high(s0, j2, s_par):
                act.wait_ge(f_mul, s0 + j2 + 1)
                if s0 >= 2:
                    act.wait_ge(w_used, U_FFN + 3 * s0 - 1 + (j2 * 3))
                act.activation(act_h[:, s_par, :], act_f[:], ACT.Copy).then_inc(f_high, 1)

            ffn_gate(0, 0, 0, U_FFN + 1)
            split_high(act, U_FFN + 3)
            ffn_high(0, 0, 0)
            split_high(act, U_FFN + 4)
            split_high(act, U_FFN + 5)
            ffn_gate(1, 0, 1, U_FFN + 3)
            split_high(act, U_FFN + 6)
            ffn_high(1, 0, 1)
            split_high(act, U_FFN + 7)
            split_high(act, U_FFN + 8)
            with act.Fori(0, 4) as j:
                for k in (0, 1):
                    ffn_gate(2 + k, j * 2, k, U_FFN + 6 + 3 * k + j * 6)
                    split_high(act, U_FFN + 9 + 3 * k, j)
                    ffn_high(2 + k, j * 2, k)
                    split_high(act, U_FFN + 10 + 3 * k, j)
                    split_high(act, U_FFN + 11 + 3 * k, j)
            ffn_gate(10, 0, 0, U_FFN + 30)
            split_high(act, U_FFN + 33)
            ffn_high(10, 0, 0)
            split_high(act, U_FFN + 34)

            norm_sums(2)
            table(ACT.Sigmoid)
            split_high(act, U_HG_IN + 2)
            norm_high(2, C_MIX + 8)
            act.wait_ge(lb_d, 1)
            act.activation(lb[:, 1, :], lb[:, 0, :], ACT.Exp).then_inc(lb_d, 1)
            for i in range(N_HG_IN - 1):
                act.wait_ge(w_used, U_HG_IN + i + 1)
                src = bank[:, (U_HG_IN + i) % 2, :].rearrange("p (a t) -> p a t", a=2)
                c = 2 * (i % 4)
                if i < 4:
                    act.activation(log_f[:, c:c + 2, :], src, ACT.Sigmoid).then_inc(hg_ev, 1)
                    act.activation(key_t[:, c:c + 2, :], src, ACT.Sigmoid, scale=-1.0).then_inc(hg_ev, 1)
                elif i < 8:
                    act.activation(qry_t[:, c:c + 2, :], src, ACT.Silu).then_inc(hg_ev, 1)
                elif i < 11:
                    if i == 8:
                        act.wait_ge(n_t, 12)
                    act.activation(gate_t[:, c:c + 2, :], src, ACT.Silu).then_inc(hg_ev, 1)
                else:
                    act.activation(val_n[:, :, (i - 11) * UC:(i - 10) * UC], src, ACT.Copy).then_inc(hg_ev, 1)
                split_high(act, U_HG_IN + i + 3)
                if i == 11:
                    for q in range(4):
                        act.wait_ge(hg_d, 3 * 4)
                        act.activation(log_f[:, 2 * q:2 * q + 2, :], log_f[:, 2 * q:2 * q + 2, :], ACT.Ln).then_inc(hg_ln, 1)
                if i == 13:
                    for q in range(4):
                        act.wait_ge(hg_t, q + 1)
                        tt, hq = q // 2, q % 2
                        act.activation(lf_h[:, tt, hq * 512:(hq + 1) * 512], bank[:, 2 + q, :], ACT.Copy).then_inc(hg_h, 1)
            for g in range(GROUPS):
                act.wait_ge(sp_d, g + 1)
                if g >= 2:
                    act.wait_ge(sp_m, g - 1)
                    act.wait_ge(sp_k, g - 1)
                act.activation(decay[:, g % 2, :], bank[:, (0, 1, 6)[g % 3], :], ACT.Exp).then_inc(sp_e, 1)

            table(ACT.Ln)
            for j in range(4):
                act.wait_ge(o_o, j + 1)
                act.activation(o_sqs(j), bank[:, O_BANK[j], :], ACT.Square).then_inc(o_sq, 1)
            inv_rms(0, 4, lambda j: bank[:, 2 + j, :], o_inv, o_ms, o_ln, o_rs)
            table(ACT.Silu)
            act.wait_ge(w_used, U_HG_OUT)
            for j in range(4):
                if j == 3:
                    act.activation(gate_t[:, HH - 2:HH, :], bank[:, 2, :].rearrange("p (a t) -> p a t", a=2), ACT.Silu).then_inc(hg_ev, 1)
                    split_high(act, U_HG_OUT + 2)
                act.wait_ge(o_g, j + 1)
                act.activation(h_h[:, 2 * j:2 * j + 2, :], o_nrm(j).rearrange("p (a t) -> p a t", a=2), ACT.Copy).then_inc(o_h, 1)
            for u in range(U_HG_OUT, U_MOE - 1):
                split_high(act, u + 3)

            norm_sums(3)
            split_high(act, U_MOE + 2)
            norm_high(3, C_FFN + 8)
            for part in range(2):
                for tt in range(TT):
                    act.wait_ge(x_gain, 2 * part + tt + 1)
                    act.activation(x_b[:, part, tt, :], x_g[:, tt, :], ACT.Copy).then_inc(x_part, 1)
            act.wait_ge(r_d, n_const["exp"])
            act.activation(pick[:, 5, :], pick[:, 4, :], ACT.Exp).then_inc(r_e, 1)

            def gather_high(n):
                for j in range(2):
                    act.wait_ge(m_gat, n * 2 + (j + 1))
                    act.activation(hs_h[:, 4 * j:4 * j + 4, :], bank[:, 5 + j, :].rearrange("p (c t) -> p c t", c=4), ACT.Copy).then_inc(m_hh, 1)

            def moe_gate(g, first, b_par, b_used):
                act.wait_ge(w_used, b_used)
                if not first:
                    act.wait_ge(m_mul, g)
                act.activation(m_silu[:], bank[:, b_par, 0:UC], ACT.Silu).then_inc(m_si, 1)

            def moe_high(g, b):
                act.wait_ge(m_t, g + 1)
                act.activation(ma_h[:, b, :], bank[:, 2, 0:UC], ACT.Copy).then_inc(m_ah, 1)

            def moe_step(u, k, gs, used, rounds):
                moe_gate(gs, False, (1 + k) % 2, used)
                split_high(act, u + 6 + 3 * k, rounds)
                split_high(act, u + 7 + 3 * k, rounds)
                moe_high(gs, (1 + k) % 2)
                split_high(act, u + 8 + 3 * k, rounds)

            def moe_round(r):
                u = U_MOE + r * NE * MOE_UNITS
                g0 = r * NE * MOE_STEPS
                n0 = r * (NE + 1)
                act.activation(m_silu[:, 0:1], eps[:], ACT.Silu)
                gather_high(n0)
                with act.Fori(0, NE) as e:
                    q = e * 7
                    g = e * MOE_STEPS + g0
                    split_high(act, u + 3, q)
                    act.wait_ge(w_used, e * MOE_UNITS + (u + 2))
                    act.activation(m_silu[:], bank[:, 0, 0:UC], ACT.Silu).then_inc(m_si, 1)
                    split_high(act, u + 4, q)
                    moe_high(g, 0)
                    split_high(act, u + 5, q)
                    with act.Fori(0, 5) as j:
                        for k in (0, 1):
                            moe_step(u, k, g + j * 2 + (1 + k), e * MOE_UNITS + j * 6 + (u + 4 + 3 * k), q + j)
                    act.wait_ge(m_pt, e + (n0 + 1))
                    act.wait_ge(m_sc, e * 4 + (4 * n0 + 4))
                    act.activation(scat[:], bank[:, 7, 0:T], ACT.Copy).then_inc(m_scat, 1)
                    for k in (0, 1):
                        moe_step(u + 5 * 6, k, g + (11 + k), e * MOE_UNITS + (u + 34 + 3 * k), q)
                    moe_gate(g + 13, False, 1, e * MOE_UNITS + (u + 40))
                    gather_high(e + (n0 + 1))
                    moe_high(g + 13, 1)
                    split_high(act, u + 42, q)
                    split_high(act, u + 43, q)
                    act.wait_ge(w_used, e * MOE_UNITS + (u + 42))
                    for j in range(2):
                        act.activation(y_h[:, j * 512:(j + 1) * 512], bank[:, 3 + j, :], ACT.Copy).then_inc(m_yh, 1)
                    split_high(act, u + 44, q)

            moe_round(0)
            act.wait_ge(r_flag, 1)
            over = act.value_load(flag[0:1, 0:1], min_val=0, max_val=1)
            with act.If(over > 0):
                moe_round(1)

        @block.tensor
        def _(pe):
            def three(o, a_high, a_low, b_high, b_low, start, stop):
                pe.matmul(o, a_high, b_high, start=start, stop=False, skip_group_check=True)
                pe.matmul(o, a_high, b_low, start=False, stop=False, skip_group_check=True)
                return pe.matmul(o, a_low, b_high, start=False, stop=stop, skip_group_check=True)

            def keep_warm(n, b):
                for _ in range(n):
                    pe.matmul(bank[:, b, :].rearrange("p (a t) -> p a t", a=4), ident_h[:],
                              ident_h[:].unsqueeze(1).to_broadcast([P, 4, P]), start=True, stop=True)

            def unit_to_features(u0, b, rounds=0, norm=None):
                wait_split(pe, u0, rounds)
                wh, wl = as_in(w_h, u0 % S), as_in(w_l, u0 % S)
                for mch in range(2):
                    f = slice(mch * P, (mch + 1) * P)
                    for c in range(KC):
                        if norm is not None and mch == 0:
                            pe.wait_ge(n_low, KC * norm + c + 1)
                        last = three(bank[:, b, mch * T:(mch + 1) * T], wh[:, c, f], wl[:, c, f], h_h[:, c, :], h_l[:, c, :],
                                     c == 0, c == KC - 1)
                last.then_inc(w_used, 1)

            def unit_to_tokens(u0, b, midway=None):
                wait_split(pe, u0)
                wh, wl = as_in(w_h, u0 % S), as_in(w_l, u0 % S)
                for tt in range(TT):
                    if tt == 1 and midway is not None:
                        midway()
                    t = slice(tt * P, (tt + 1) * P)
                    for c in range(KC):
                        last = three(bank[:, b, tt * UC:(tt + 1) * UC], h_h[:, c, t], h_l[:, c, t], wh[:, c, :], wl[:, c, :],
                                     c == 0, c == KC - 1)
                last.then_inc(w_used, 1)

            def unit_out(u0, ah, al, first, last_unit, rounds=0, midway=None):
                wait_split(pe, u0, rounds)
                wh, wl = as_out(w_h, u0 % S), as_out(w_l, u0 % S)
                for c in range(OC):
                    if c == 1 and midway is not None:
                        midway()
                    for tt in range(TT):
                        for half in range(2):
                            v = slice(half * 512, (half + 1) * 512)
                            last = three(bank[:, 4 + 2 * tt + half, :], ah(c, tt), al(c, tt), wh[:, c, v], wl[:, c, v],
                                         first and c == 0, last_unit and c == OC - 1)
                        if last_unit and c == OC - 1 and tt == 0:
                            last.then_inc(o_part, 1)
                last.then_inc(w_used, 1)

            def norm_turn(n):
                for tt in range(TT):
                    pe.wait_ge(n_xn, TT * n + tt + 1)
                    for j in range(4):
                        b = j if n == 3 else 4 + j
                        for c in range(2):
                            last = pe.transpose(bank[:, b, c * T + tt * P:c * T + (tt + 1) * P],
                                                xn[:, tt, (2 * j + c) * P:(2 * j + c + 1) * P], ident[:])
                        if tt == TT - 1:
                            last.then_inc(n_t, 1)

            pe.wait_ge(const, n_const["rows"])
            norm_turn(0)
            pe.wait_ge(par_in, 16 * 10)
            pe.wait_ge(par_in_pool, 16 * 3)
            pe.transpose(bank[:, 0, 0:P], par_rows[:], ident[:]).then_inc(par_t, 1)
            pe.transpose(bank[:, 1, 0:P], dw_rows[:], ident[:]).then_inc(par_t, 1)
            pe.wait_ge(par_cp, 2)
            free = {2: (c_g, 1), 3: (c_s, 1), 4: (c_g, 2), 5: (c_s, 2), 6: (qk_sq, 1), 7: (qk_sq, 2), 8: (qk_sq, 3), 9: (qk_sq, 4)}

            def qk_mean(i):
                pe.wait_ge(qk_sq, i + 1)
                if i >= 2:
                    pe.wait_ge(qk_ln, i - 1)
                pe.matmul(bank[:, 6 + i % 2, :], mean_64[:], sq[:, i % 2, :], start=True, stop=True).then_inc(qk_ms, 1)

            for u in range(N_AB_IN - 1):
                if u in free:
                    pe.wait_ge(*free[u])
                if u < 8:
                    unit_to_features(u, u % 2, norm=0 if u == 0 else None)
                else:
                    unit_to_tokens(u, u % 2, lambda: qk_mean(3))
                if 5 <= u <= 7:
                    qk_mean(u - 5)
            keep_warm(20, 1)
            pe.wait_ge(q_n, 4)
            pe.wait_ge(qk_ln, 4)
            for b in range(6):
                qt = 0 if b < 2 else 1
                c = b if b < 2 else (b - 2) // 2
                n, w = (4, P) if qt == 0 else (2, T)
                rows = slice(HD * c, HD * (c + 1))
                for g in range(n):
                    h = g if qt == 0 else 2 * ((b - 2) % 2) + g
                    pe.matmul(bank[:, 2 + b, g * w:(g + 1) * w], q_t[rows, h, qt * P:(qt + 1) * P], k_t[rows, h, 0:w],
                              start=True, stop=False, skip_group_check=True)
                    last = pe.matmul(bank[:, 2 + b, g * w + qt * P:g * w + (qt + 1) * P], ident_b[:], mask_b[:], start=False, stop=True,
                                     skip_group_check=True)
                last.then_inc(s_sc, 1)
            pe.wait_ge(*free[N_AB_IN - 1])
            unit_to_tokens(N_AB_IN - 1, (N_AB_IN - 1) % 2)
            pe.wait_ge(c_diag, 2 * PE_TAPS)
            pe.wait_ge(v_cp, 1)
            for c in range(2):
                for k in range(PE_TAPS):
                    first = TAPS - PE_TAPS + k
                    last = pe.matmul(bank[:, 0, c * T:(c + 1) * T], diag[:, c * PE_TAPS + k, :], conv_in[:, 2 + c, first:first + T],
                                     start=k == 0, stop=k == PE_TAPS - 1)
            last.then_inc(c_pe, 1)
            for h in range(HEADS):
                pe.wait_ge(s_w, 4 + h + 1)
                pe.transpose(bank[:, 2 + h, 0:P], p_0[:, 0, h, :], ident[:])
                pe.transpose(bank[:, 2 + h, P:2 * P], p_1[:, 0, h, 0:P], ident[:])
                pe.transpose(bank[:, 2 + h, 2 * P:3 * P], p_1[:, 0, h, P:2 * P], ident[:]).then_inc(a_t, 1)
            pe.wait_ge(v_cp, 2)
            for b in range(2):
                for h in (2 * b, 2 * b + 1):
                    pe.wait_ge(a_wt, h + 1)
                    o = (h % 2) * T
                    pe.matmul(bank[:, 6 + b, o:o + T], v_n[:, 0, h * P:(h + 1) * P], w_t[:, h, 0:T], start=True, stop=False,
                              skip_group_check=True)
                    last = pe.matmul(bank[:, 6 + b, o + P:o + T], v_n[:, 1, h * P:(h + 1) * P], w_t[:, h, T:T + P], start=False,
                                     stop=True, skip_group_check=True)
                last.then_inc(a_o, 1)
            def from_h(i):
                return (lambda c, tt: h_h[:, 2 * i + c, tt * P:(tt + 1) * P]), (lambda c, tt: h_l[:, 2 * i + c, tt * P:(tt + 1) * P])

            def ab_out_unit(i, midway=None):
                pe.wait_ge(*((a_l, i + 1) if i < 2 else (g_l, i - 1)))
                unit_out(U_AB_OUT + i, *from_h(i), i == 0, i == N_OUT - 1, midway=midway)

            pe.wait_ge(c_sum, 1)
            for b in range(2):
                pe.wait_ge(a_sq, b + 1)
                pe.matmul(bank[:, b, :], mean_all[:], sq[:, b, :], start=True, stop=True).then_inc(a_ms, 1)
            pe.wait_ge(c_y, 4 * TAPS - 2 * PE_TAPS)
            for b in range(2):
                pe.matmul(bank[:, 2 + b, :], mean_64[:], conv_y[:, 2 * b:2 * b + 2, :], start=True, stop=True).then_inc(g_m, 1)

            def variances():
                for b in range(2):
                    pe.wait_ge(g_sq, b + 1)
                    pe.matmul(bank[:, 2 + b, :], mean_64[:], sq[:, b, :], start=True, stop=True).then_inc(g_v, 1)

            ab_out_unit(0, variances)
            ab_out_unit(1)
            ab_out_unit(2)
            ab_out_unit(3)
            norm_turn(1)

            def ffn_out_unit(s0, j, b, first, last_unit, u0=None):
                pe.wait_ge(f_low, j * 2 + (s0 + 1))
                unit_out(U_FFN + 3 * s0 + 4 if u0 is None else u0, lambda c, tt: act_h[:, b, c * T + tt * P:c * T + (tt + 1) * P],
                         lambda c, tt: act_l[:, b, c * T + tt * P:c * T + (tt + 1) * P], first, last_unit, j)

            def ffn_body(s0, j, b):
                nb = 1 - b
                if s0:
                    pe.wait_ge(f_silu, j * 2 + s0)
                unit_to_features(U_FFN + 3 * s0 + 2, nb, j)
                if s0:
                    pe.wait_ge(f_mul, j * 2 + s0)
                unit_to_features(U_FFN + 3 * s0 + 3, 2 + nb, j)
                ffn_out_unit(s0, j, b, s0 == 0, False)

            unit_to_features(U_FFN, 0, norm=1)
            unit_to_features(U_FFN + 1, 2)
            ffn_body(0, 0, 0)
            with pe.Fori(0, 4) as j:
                ffn_body(1, j, 1)
                ffn_body(2, j, 0)
            ffn_body(9, 0, 1)
            ffn_out_unit(10, 0, 0, False, True, U_FFN + 32)
            norm_turn(2)

            for i in range(N_HG_IN - 1):
                if i >= 2:
                    pe.wait_ge(hg_ev, 2 * (i - 1) if i < 6 else i + 3)
                if i < 11:
                    unit_to_features(U_HG_IN + i, (U_HG_IN + i) % 2, norm=2 if i == 0 else None)
                else:
                    unit_to_tokens(U_HG_IN + i, (U_HG_IN + i) % 2)
                if i == 13:
                    for q in range(4):
                        tt, hq = q // 2, q % 2
                        pe.wait_ge(hg_ln, 2 * hq + 2)
                        for h in range(4):
                            last = pe.transpose(bank[:, 2 + q, h * P:(h + 1) * P], log_f[:, 4 * hq + h, tt * P:(tt + 1) * P], ident[:])
                        last.then_inc(hg_t, 1)
            pe.wait_ge(hg_l, 4)
            for q in range(4):
                tt, hq = q // 2, q % 2
                for h in range(4):
                    t = slice(tt * P, (tt + 1) * P)
                    last = pe.matmul(bank[:, 2 + q, h * P:(h + 1) * P], key_t[:, 4 * hq + h, t], qry_t[:, 4 * hq + h, t], start=True, stop=True)
                last.then_inc(hd, 1)

            def spans(g):
                p, hp, tt = g // 8, (g // 2) % 4, g % 2
                if g >= 3:
                    pe.wait_ge(sp_e, g - 2)
                b = (0, 1, 6)[g % 3]
                mm = span[:, p if p < 3 else 3 + tt, :, :]
                for a in range(2):
                    f = slice((2 * hp + a) * P, (2 * hp + a + 1) * P)
                    pe.matmul(bank[:, b, a * T:(a + 1) * T], lf_h[:, tt, f], mm, start=True, stop=False)
                    last = pe.matmul(bank[:, b, a * T:(a + 1) * T], lf_l[:, tt, f], mm, start=False, stop=True)
                last.then_inc(sp_d, 1)

            def scores(g):
                p, hp, tt = g // 8, (g // 2) % 4, g % 2
                pe.wait_ge(sp_m, g + 1)
                pe.wait_ge(sp_k, g + 1)
                if g >= 4:
                    pe.wait_ge(sp_c0, g - 3)
                    pe.wait_ge(sp_c1, second(g - 4))
                else:
                    pe.wait_ge(hd_cp, g % 4 + 1)
                b = 2 + g % 4
                for a in range(2):
                    for li in range(2):
                        v = slice((2 * a + li) * P, (2 * a + li + 1) * P)
                        if 2 * p + li < 7:
                            last = pe.matmul(bank[:, b, v], dk[:, g % 2, v], dq[:, g % 2, v], start=True, stop=True)
                        elif tt == 1:
                            last = pe.matmul(bank[:, b, v], dk[:, 1 - g % 2, v], dq[:, g % 2, v], start=True, stop=True)
                last.then_inc(sp_s, 1)

            def head_outputs(j):
                pe.wait_ge(sp_c0, GROUPS - 8 + 2 * j + 2)
                pe.wait_ge(sp_c1, second(GROUPS - 8 + 2 * j + 1))
                if j:
                    pe.wait_ge(sp_e, GROUPS - 3 + j)
                for h in (2 * j, 2 * j + 1):
                    o = (h % 2) * T
                    pe.matmul(bank[:, O_BANK[j], o:o + T], val_n[:, 0, h * P:(h + 1) * P], att[:, h, 0:2, :], start=True, stop=False,
                              skip_group_check=True)
                    last = pe.matmul(bank[:, O_BANK[j], o + P:o + T], val_n[:, 1, h * P:(h + 1) * P], att[:, h, 2, :], start=False,
                                     stop=True, skip_group_check=True)
                last.then_inc(o_o, 1)

            def head_means(j):
                pe.wait_ge(o_sq, j + 1)
                pe.wait_ge(sp_c0, GROUPS - 3 + j)
                pe.wait_ge(sp_c1, second(GROUPS - 4 + j))
                pe.matmul(bank[:, 2 + j, :], mean_all[:], o_sqs(j), start=True, stop=True).then_inc(o_ms, 1)

            pe.wait_ge(const, n_const["all"])
            pe.wait_ge(hg_ev, 19)
            spans(0)
            spans(1)
            for g in range(GROUPS):
                if g + 2 < GROUPS:
                    spans(g + 2)
                scores(g)
                if g >= GROUPS - 5 and g % 2 == 1 and g < GROUPS - 1:
                    head_outputs((g - (GROUPS - 5)) // 2)
            head_outputs(2)
            for j in range(3):
                head_means(j)
            head_outputs(3)
            head_means(3)
            pe.wait_ge(o_ln, 1)
            unit_to_features(U_HG_OUT - 1, 2)
            for i in range(N_OUT):
                pe.wait_ge(o_l, i + 1)
                if i == 0:
                    pe.wait_ge(o_n, 2)
                unit_out(U_HG_OUT + i, *from_h(i), i == 0, i == N_OUT - 1)
            norm_turn(3)

            pe.wait_ge(r_low, 1)
            for c in range(KC):
                pe.wait_ge(n_low, KC * 3 + c + 1)
                three(bank[0:NE, 4, 0:T], router_h[:, c, :], router_l[:, c, :], h_h[:, c, :], h_l[:, c, :], c == 0, False)
                last = pe.matmul(bank[0:NE, 4, 0:T], router_l[:, c, :], h_l[:, c, :], start=False, stop=c == KC - 1,
                                 skip_group_check=True)
            last.then_inc(r_lt, 1)
            pe.wait_ge(r_lc, 1)
            for tt in range(TT):
                last = pe.transpose(bank[:, 5, tt * NE:(tt + 1) * NE], logit_t[:, tt * P:(tt + 1) * P], ident[0:NE, 0:NE])
            last.then_inc(r_lg, 1)
            pe.wait_ge(r_d, n_const["sel"])
            s0, s1 = logit[:, 6, 0, :], logit[:, 6, 1, :]
            pe.matmul(bank[:, 4, 0:NE], before[:], s0, start=True, stop=True)
            pe.matmul(bank[:, 4, NE:2 * NE], ones[:], s0, start=True, stop=False)
            pe.matmul(bank[:, 4, NE:2 * NE], before[:], s1, start=False, stop=True)
            pe.matmul(bank[:, 4, 2 * NE:3 * NE], ones[:], s0, start=True, stop=False)
            pe.matmul(bank[:, 4, 2 * NE:3 * NE], ones[:], s1, start=False, stop=True).then_inc(r_rank, 1)

            def gather(n):
                pe.wait_ge(m_sel, n * 2 + 2)
                pe.wait_ge(m_add, n * 4 + 1)
                for j in range(2):
                    for c in range(4):
                        f = slice((4 * j + c) * P, (4 * j + c + 1) * P)
                        for tt in range(TT):
                            for part in range(3):
                                last = pe.matmul(bank[:, 5 + j, c * P:(c + 1) * P], x_b[:, part, tt, f], sel[:, tt, :],
                                                 start=tt == 0 and part == 0, stop=tt == 1 and part == 2, skip_group_check=True)
                    last.then_inc(m_gat, 1)
                pe.wait_ge(m_scat, n + 1)
                for tt in range(TT):
                    last = pe.matmul(bank[:, 7, tt * P:(tt + 1) * P], sel[:, tt, :], ident_h[:], start=True, stop=True)
                last.then_inc(m_pt, 1)

            def scatter(tt, n):
                if tt == 0:
                    pe.wait_ge(m_yl, n * 2 + 2)
                    pe.wait_ge(m_scat, n + 1)
                else:
                    pe.wait_ge(m_add, n * 4 + 3)
                for half in range(2):
                    v = slice(half * 512, (half + 1) * 512)
                    pe.matmul(bank[:, 5 + half, :], scat[:, tt * P:(tt + 1) * P], y_h[:, v], start=True, stop=False, skip_group_check=True)
                    pe.matmul(bank[:, 5 + half, :], scat[:, tt * P:(tt + 1) * P], y_l[:, v], start=False, stop=True,
                              skip_group_check=True).then_inc(m_sc, 1)

            def moe_in(u0, b, half, rounds):
                wait_split(pe, u0, rounds)
                wh, wl = as_in(w_h, u0 % S), as_in(w_l, u0 % S)
                for c in range(KC):
                    last = three(bank[:, b, half * UC:(half + 1) * UC], hs_h[:, c, :], hs_l[:, c, :], wh[:, c, :], wl[:, c, :],
                                 c == 0, c == KC - 1)
                last.then_inc(w_used, 1)

            def moe_turn(g):
                pe.wait_ge(m_mul, g + 1)
                for c in range(2):
                    last = pe.transpose(bank[:, 2, c * P:(c + 1) * P], m_act[:, c * P:(c + 1) * P], ident[:])
                last.then_inc(m_t, 1)

            def moe_out(u0, g, b, first, last_unit, rounds, turn=None):
                pe.wait_ge(m_al, g + 1)
                wait_split(pe, u0, rounds)
                wh, wl = as_out(w_h, u0 % S), as_out(w_l, u0 % S)
                for c in range(OC):
                    if c == 1 and turn is not None:
                        moe_turn(turn)
                    t = slice(c * P, (c + 1) * P)
                    for half in range(2):
                        v = slice(half * 512, (half + 1) * 512)
                        last = three(bank[:, 3 + half, :], ma_h[:, b, t], ma_l[:, b, t], wh[:, c, v], wl[:, c, v],
                                     first and c == 0, last_unit and c == OC - 1)
                last.then_inc(w_used, 1)

            def moe_step(u, k, gs, rounds, last=False):
                pe.wait_ge(m_mul, gs)
                moe_in(u + 5 + 3 * k, k, 0, rounds)
                moe_turn(gs)
                moe_in(u + 6 + 3 * k, k, 1, rounds)
                moe_out(u + 7 + 3 * k, gs, (1 + k) % 2, False, False, rounds, gs + 1 if last else None)

            def moe_round(r):
                u = U_MOE + r * NE * MOE_UNITS
                g0 = r * NE * MOE_STEPS
                n0 = r * (NE + 1)
                gather(n0)
                with pe.Fori(0, NE) as e:
                    q = e * 7
                    g = e * MOE_STEPS + g0
                    n = e + n0
                    pe.wait_ge(m_hl, e * 2 + (2 * n0 + 2))
                    moe_in(u, 0, 0, q)
                    moe_in(u + 1, 0, 1, q)
                    scatter(0, n)
                    moe_in(u + 2, 1, 0, q)
                    moe_turn(g)
                    moe_in(u + 3, 1, 1, q)
                    scatter(1, n)
                    moe_out(u + 4, g, 0, True, False, q)
                    with pe.Fori(0, 5) as j:
                        for k in (0, 1):
                            moe_step(u, k, g + j * 2 + (1 + k), q + j)
                    gather(n + 1)
                    for k in (0, 1):
                        moe_step(u + 5 * 6, k, g + (11 + k), q, k == 1)
                    moe_out(u + 41, g + 13, 1, False, True, q)
                for tt in range(TT):
                    scatter(tt, NE + n0)

            pe.wait_ge(x_gain, 6)
            moe_round(0)
            pe.wait_ge(r_flag, 1)
            over = pe.value_load(flag[0:1, 0:1], min_val=0, max_val=1)
            with pe.If(over > 0):
                moe_round(1)


_INS = ['x', 'mix_norm', 'ffn_norm', 'ab_w_in', 'ab_w_out', 'da_q_gain', 'da_k_gain', 'da_lambda', 'da_subln',
        'conv_dw', 'conv_dw_bias', 'conv_gn_gain', 'conv_gn_bias', 'hgrn_w_in', 'hgrn_lb_logits', 'hgrn_norm',
        'hgrn_w_out', 'ffn_w_in', 'ffn_w_out', 'moe_router', 'moe_w_in', 'moe_w_out']


def kernel(**inputs):
    import numpy as np
    import concourse.bacc as bacc
    from concourse.bass_utils import run_bass_kernel_spmd

    nc = bacc.Bacc("TRN2", target_bir_lowering=False, num_devices=1)
    arrays, args = {}, {}
    for name in _INS:
        a = np.ascontiguousarray(inputs[name])
        arrays[f"in_{name}"] = a
        args[name] = nc.dram_tensor(f"in_{name}", a.shape, mybir.dt.from_np(a.dtype), kind="ExternalInput").ap()
    out = nc.dram_tensor("out", (1, T, D), F32, kind="ExternalOutput").ap()
    build(nc, args, out)
    return run_bass_kernel_spmd(nc, [arrays], core_ids=[0]).results[0]["out"]
```
